# Optimizing a Trainium2 kernel written in Bass

```python
import math
import jax, jax.numpy as jnp
from jax import lax
import numpy as np

D_MODEL = 1024
BATCH = 1
SEQ = 2048
DEPTH = 1

SSM_HEADS = 16
SSM_HEAD_DIM = 64
SSM_INNER = SSM_HEADS * SSM_HEAD_DIM
SSM_GROUPS = 4
SSM_HEADS_PER_GROUP = SSM_HEADS // SSM_GROUPS
SSM_STATE = 128
SSM_CONV = 4
SSM_CHUNK = 128
SSM_CONV_DIM = SSM_INNER + 2 * SSM_GROUPS * SSM_STATE

ATTN_HEAD_DIM = 64
ATTN_SLOTS = 8
ATTN_PATTERNS = ((128, 1), (512, 4), (2048, 16))
ATTN_GROUPS = len(ATTN_PATTERNS)
ATTN_Q_WIDTH = ATTN_GROUPS * ATTN_SLOTS * ATTN_HEAD_DIM
ATTN_KV_WIDTH = ATTN_SLOTS * ATTN_HEAD_DIM
ATTN_BLOCK = 128

SC_WIDTH = 512
SC_CONV = 3

N_BRANCH = 3
NORM_EPS = 1e-6

SPLITS = (
    SSM_INNER,
    SSM_CONV_DIM,
    SSM_HEADS,
    ATTN_Q_WIDTH,
    ATTN_KV_WIDTH,
    ATTN_KV_WIDTH,
    ATTN_KV_WIDTH,
    SC_WIDTH,
    SC_WIDTH,
    SC_WIDTH,
    SC_WIDTH,
    N_BRANCH * D_MODEL,
)
IN_WIDTH = sum(SPLITS)
SPLIT_OFFSETS = tuple(int(o) for o in np.cumsum(SPLITS)[:-1])

kernel_name = "hybrid_ssd_dilated_attn_shortconv"

def rms_norm(x, w):
    xf = x.astype(jnp.float32)
    y = xf * lax.rsqrt(jnp.mean(xf * xf, axis=-1, keepdims=True) + NORM_EPS)
    return (y * w.astype(jnp.float32)).astype(x.dtype)

def causal_depthwise_conv(x, w):
    k_width = w.shape[0]
    return lax.conv_general_dilated(
        x, w[:, None, :].astype(x.dtype), window_strides=(1,),
        padding=((k_width - 1, 0),), dimension_numbers=("NWC", "WIO", "NWC"),
        feature_group_count=x.shape[-1])

def ssd_scan(xdt, a, b_in, c_in):
    bsz, s = xdt.shape[:2]
    n_chunks = s // SSM_CHUNK

    def chunks(t):
        return jnp.moveaxis(t.reshape(bsz, n_chunks, SSM_CHUNK, *t.shape[2:]), 1, 0)

    causal = jnp.tril(jnp.ones((SSM_CHUNK, SSM_CHUNK), dtype=bool))[None, :, :, None, None]

    def step(state, inp):
        xc, ac, bc, cc = inp
        cs = jnp.cumsum(ac, axis=1)
        seg = cs[:, :, None] - cs[:, None, :]
        lmat = jnp.exp(jnp.where(causal, seg, -jnp.inf))
        cb = jnp.einsum("blgn,bsgn->blsg", cc, bc)
        y_diag = jnp.einsum("blsg,blsgj,bsgjp->blgjp", cb, lmat, xc)
        y_off = jnp.einsum("blgn,bgjpn,blgj->blgjp", cc, state, jnp.exp(cs))
        decay = jnp.exp(cs[:, -1:] - cs)
        new_state = (state * jnp.exp(cs[:, -1])[..., None, None]
                     + jnp.einsum("blgn,blgj,blgjp->bgjpn", bc, decay, xc))
        return new_state, y_diag + y_off

    state0 = jnp.zeros((bsz, SSM_GROUPS, SSM_HEADS_PER_GROUP, SSM_HEAD_DIM, SSM_STATE), jnp.float32)
    _, ys = lax.scan(step, state0, (chunks(xdt), chunks(a), chunks(b_in), chunks(c_in)))
    return jnp.moveaxis(ys, 0, 1).reshape(xdt.shape)

def ssd_branch(z, xbc, dt_raw, conv_w, conv_b, dt_bias, a_log, d_skip, norm_w):
    bsz, s, _ = xbc.shape
    xbc = jax.nn.silu(causal_depthwise_conv(xbc, conv_w) + conv_b.astype(xbc.dtype))
    gn = SSM_GROUPS * SSM_STATE
    xs = xbc[..., :SSM_INNER].astype(jnp.float32).reshape(
        bsz, s, SSM_GROUPS, SSM_HEADS_PER_GROUP, SSM_HEAD_DIM)
    b_in = xbc[..., SSM_INNER:SSM_INNER + gn].astype(jnp.float32).reshape(bsz, s, SSM_GROUPS, SSM_STATE)
    c_in = xbc[..., SSM_INNER + gn:].astype(jnp.float32).reshape(bsz, s, SSM_GROUPS, SSM_STATE)
    dt = jax.nn.softplus(dt_raw.astype(jnp.float32) + dt_bias.astype(jnp.float32))
    dt = dt.reshape(bsz, s, SSM_GROUPS, SSM_HEADS_PER_GROUP)
    a_neg = -jnp.exp(a_log.astype(jnp.float32)).reshape(SSM_GROUPS, SSM_HEADS_PER_GROUP)
    y = ssd_scan(xs * dt[..., None], dt * a_neg, b_in, c_in)
    y = y + xs * d_skip.astype(jnp.float32).reshape(SSM_GROUPS, SSM_HEADS_PER_GROUP, 1)
    yg = y.reshape(bsz, s, SSM_INNER) * jax.nn.silu(z.astype(jnp.float32))
    yg = yg.reshape(bsz, s, SSM_GROUPS, SSM_INNER // SSM_GROUPS)
    yg = yg * lax.rsqrt(jnp.mean(yg * yg, axis=-1, keepdims=True) + NORM_EPS)
    yg = yg.reshape(bsz, s, SSM_INNER) * norm_w.astype(jnp.float32)
    return yg.astype(z.dtype)

def dilated_window_attention(q, k, v, window, dilation):
    bsz, s, h, dh = q.shape
    n_back = window // dilation
    length = s // dilation
    n_blocks = -(-length // ATTN_BLOCK)
    padded = n_blocks * ATTN_BLOCK

    def residues(t):
        return t.reshape(bsz, length, dilation, h, dh).transpose(0, 2, 1, 3, 4)

    qr = jnp.pad(residues(q), ((0, 0), (0, 0), (0, padded - length), (0, 0), (0, 0)))
    qb = qr.reshape(bsz, dilation, n_blocks, ATTN_BLOCK, h, dh)

    def key_blocks(t):
        tr = jnp.pad(residues(t), ((0, 0), (0, 0), (ATTN_BLOCK, padded - length), (0, 0), (0, 0)))
        tr = tr.reshape(bsz, dilation, n_blocks + 1, ATTN_BLOCK, h, dh)
        return jnp.concatenate([tr[:, :, :-1], tr[:, :, 1:]], axis=3)

    kb = key_blocks(k)
    vb = key_blocks(v)
    q_idx = jnp.arange(ATTN_BLOCK)[:, None] + ATTN_BLOCK
    k_idx = jnp.arange(2 * ATTN_BLOCK)[None, :]
    diff = q_idx - k_idx
    band = (diff >= 0) & (diff <= n_back)
    key_pos = jnp.arange(n_blocks)[:, None] * ATTN_BLOCK - ATTN_BLOCK + k_idx
    valid = band[None] & (key_pos >= 0)[:, None, :]

    scores = jnp.einsum("brnqhd,brnkhd->brnhqk", qb, kb) * (ATTN_HEAD_DIM ** -0.5)
    scores = jnp.where(valid[None, None, :, None], scores, -jnp.inf)
    m = jnp.max(scores, axis=-1, keepdims=True)
    p = jnp.exp(scores - m)
    den = jnp.sum(p, axis=-1)
    o = jnp.einsum("brnhqk,brnkhd->brnqhd", p, vb) / jnp.moveaxis(den, -1, -2)[..., None]
    lse = jnp.moveaxis(m[..., 0] + jnp.log(den), -1, -2)

    o = o.reshape(bsz, dilation, padded, h, dh)[:, :, :length]
    o = o.transpose(0, 2, 1, 3, 4).reshape(bsz, s, h, dh)
    lse = lse.reshape(bsz, dilation, padded, h)[:, :, :length]
    lse = lse.transpose(0, 2, 1, 3).reshape(bsz, s, h)
    return o, lse

def attention_branch(q, k, v):
    bsz, s, _ = q.shape
    qf = q.astype(jnp.float32).reshape(bsz, s, ATTN_GROUPS, ATTN_SLOTS, ATTN_HEAD_DIM)
    kf = k.astype(jnp.float32).reshape(bsz, s, ATTN_SLOTS, ATTN_HEAD_DIM)
    vf = v.astype(jnp.float32).reshape(bsz, s, ATTN_SLOTS, ATTN_HEAD_DIM)
    outs, lses = [], []
    for g, (window, dilation) in enumerate(ATTN_PATTERNS):
        o, lse = dilated_window_attention(qf[:, :, g], kf, vf, window, dilation)
        outs.append(o)
        lses.append(lse)
    weights = jax.nn.softmax(jnp.stack(lses, axis=0), axis=0)
    out = jnp.sum(weights[..., None] * jnp.stack(outs, axis=0), axis=0)
    return out.reshape(bsz, s, ATTN_KV_WIDTH).astype(q.dtype)

def hybrid_layer(x, norm_pre, norm_post, w_in, ssm_conv_w, ssm_conv_b, dt_bias, a_log,
                 d_skip, ssm_norm, sc_conv_w, p_ssm, p_attn, p_sc, w_out):
    bsz, s, _ = x.shape
    h = rms_norm(x, norm_pre)
    proj = h @ w_in.astype(h.dtype)
    (z, xbc, dt_raw, q, k, v, g_attn, u, b_sc, c_sc, g_sc, merge) = jnp.split(
        proj, SPLIT_OFFSETS, axis=-1)

    y_ssm = ssd_branch(z, xbc, dt_raw, ssm_conv_w, ssm_conv_b, dt_bias, a_log, d_skip, ssm_norm)
    y_attn = attention_branch(q, k, v) * jax.nn.silu(g_attn)
    y_sc = b_sc * causal_depthwise_conv(c_sc * u, sc_conv_w) * jax.nn.silu(g_sc)

    gates = jax.nn.sigmoid(merge.astype(jnp.float32)).reshape(bsz, s, N_BRANCH, D_MODEL)
    merged = (gates[:, :, 0] * (y_ssm @ p_ssm.astype(y_ssm.dtype)).astype(jnp.float32)
              + gates[:, :, 1] * (y_attn @ p_attn.astype(y_attn.dtype)).astype(jnp.float32)
              + gates[:, :, 2] * (y_sc @ p_sc.astype(y_sc.dtype)).astype(jnp.float32))
    out = merged.astype(x.dtype) @ w_out.astype(x.dtype)
    return x + rms_norm(out, norm_post)

def setup_inputs(seed: int = 0) -> dict:
    key = jax.random.key(seed)
    ks = jax.random.split(key, 16)

    def nrm(k, shape, scale):
        return jax.random.normal(k, shape, jnp.float32) * scale

    x = nrm(ks[0], (BATCH, SEQ, D_MODEL), 1.0)
    norm_pre = 1.0 + nrm(ks[1], (DEPTH, D_MODEL), 0.05)
    norm_post = 1.0 + nrm(ks[2], (DEPTH, D_MODEL), 0.05)
    w_in = nrm(ks[3], (DEPTH, D_MODEL, IN_WIDTH), D_MODEL ** -0.5)
    ssm_conv_w = nrm(ks[4], (DEPTH, SSM_CONV, SSM_CONV_DIM), SSM_CONV ** -0.5)
    ssm_conv_b = nrm(ks[5], (DEPTH, SSM_CONV_DIM), 0.01)
    dt0 = jnp.exp(jax.random.uniform(ks[6], (DEPTH, SSM_HEADS), jnp.float32,
                                     math.log(1e-3), math.log(1e-1)))
    dt_bias = dt0 + jnp.log(-jnp.expm1(-dt0))
    a_log = jnp.log(jax.random.uniform(ks[7], (DEPTH, SSM_HEADS), jnp.float32, 1.0, 16.0))
    d_skip = 1.0 + nrm(ks[8], (DEPTH, SSM_HEADS), 0.05)
    ssm_norm = 1.0 + nrm(ks[9], (DEPTH, SSM_INNER), 0.05)
    sc_conv_w = nrm(ks[10], (DEPTH, SC_CONV, SC_WIDTH), SC_CONV ** -0.5)
    p_ssm = nrm(ks[11], (DEPTH, SSM_INNER, D_MODEL), SSM_INNER ** -0.5)
    p_attn = nrm(ks[12], (DEPTH, ATTN_KV_WIDTH, D_MODEL), ATTN_KV_WIDTH ** -0.5)
    p_sc = nrm(ks[13], (DEPTH, SC_WIDTH, D_MODEL), SC_WIDTH ** -0.5)
    w_out = nrm(ks[14], (DEPTH, D_MODEL, D_MODEL), D_MODEL ** -0.5)
    return {"x": x, "norm_pre": norm_pre, "norm_post": norm_post, "w_in": w_in,
            "ssm_conv_w": ssm_conv_w, "ssm_conv_b": ssm_conv_b, "dt_bias": dt_bias,
            "a_log": a_log, "d_skip": d_skip, "ssm_norm": ssm_norm, "sc_conv_w": sc_conv_w,
            "p_ssm": p_ssm, "p_attn": p_attn, "p_sc": p_sc, "w_out": w_out}

def reference(x, norm_pre, norm_post, w_in, ssm_conv_w, ssm_conv_b, dt_bias, a_log,
              d_skip, ssm_norm, sc_conv_w, p_ssm, p_attn, p_sc, w_out):
    for i in range(DEPTH):
        x = hybrid_layer(x, norm_pre[i], norm_post[i], w_in[i], ssm_conv_w[i], ssm_conv_b[i],
                         dt_bias[i], a_log[i], d_skip[i], ssm_norm[i], sc_conv_w[i],
                         p_ssm[i], p_attn[i], p_sc[i], w_out[i])
    return x


_drawn_inputs = setup_inputs


def setup_inputs(seed=0):
    import zlib

    import numpy as np

    out = dict(_drawn_inputs(seed))
    spreads = {}
    factors = {'ssm_conv_b': 6.037, 'd_skip': 9.164}
    for name, (base, spread) in spreads.items():
        noise = np.random.default_rng([zlib.crc32(name.encode()), seed]).standard_normal(out[name].shape)
        drawn = base * np.exp(spread * noise) if base else spread * noise
        out[name] = __import__('jax').numpy.asarray(drawn.astype(out[name].dtype))
    for name, factor in factors.items():
        out[name] = (out[name] * factor).astype(out[name].dtype)
    return out
```

```python
from contextlib import ExitStack

import concourse.bass as bass
from concourse import mybir

F32 = mybir.dt.float32
F32R = mybir.dt.float32r
ALU = mybir.AluOpType
ACT = mybir.ActivationFunctionType

P = 128
SEQ, DM = 2048, 1024
KC = DM // P
TILES = SEQ // P
BANK = 512
SPANS = SEQ // BANK
HEADS, HDIM, GROUPS, STATE = 16, 64, 4, 128
SSM = HEADS * HDIM
GW = SSM // GROUPS
SLOTS, PATTERNS = 8, ((128, 1), (512, 4), (2048, 16))
KV = SLOTS * HDIM
SC = 512
EPS = 1e-6
NEG = -1e30

C_Z = 0
C_XBC = C_Z + SSM
C_DT = C_XBC + SSM + 2 * GROUPS * STATE
C_Q = C_DT + HEADS
C_G = C_Q + 3 * KV + 2 * KV
C_U = C_G + KV
C_B, C_C, C_GSC = C_U + SC, C_U + 2 * SC, C_U + 3 * SC
C_MERGE = C_U + 4 * SC
IN_W = C_MERGE + 3 * DM


class Scope:

    def __init__(self, nc, stack):
        self.nc, self.stack = nc, stack

    def sb(self, name, shape, dt=F32):
        return self.stack.enter_context(self.nc.sbuf_tensor(name, shape, dt))

    def ps(self, name, shape, dt=F32):
        return self.stack.enter_context(self.nc.psum_tensor(name, shape, dt))

    def sem(self, name):
        return self.stack.enter_context(self.nc.semaphore(name))

    def sems(self, name, n):
        return [self.sem(f"{name}{i}") for i in range(n)]


def wait_alone(eng, sem, value, carrier):
    eng.wait_ge(sem, value)
    eng.sem_inc(carrier, 1)


def norm_stage(nc, w, h_hi, h_lo, ident, eps):
    with ExitStack() as stack:
        s = Scope(nc, stack)
        x_sb = s.sb("nx", [P, 2, DM])
        sq = s.sb("nsq", [P, DM])
        h_tok = s.sb("nh", [P, 2, DM])
        w_pre = s.sb("nw", [P, DM])
        ssum = s.sb("nss", [P, TILES])
        std = s.sb("nstd", [P, TILES])
        rstd = s.sb("nrstd", [P, TILES])
        tr = s.ps("ntr", [P, 2, DM])
        x_loaded = s.sems("n_x_loaded", 2)
        w_loaded = s.sem("n_w_loaded")
        squared = s.sem("n_squared")
        std_ready = s.sem("n_std_ready")
        eps_ready = s.sem("n_eps_ready")
        rstd_ready = s.sem("n_rstd_ready")
        h_made = s.sems("n_h_made", 2)
        tr_made = s.sems("n_tr_made", 2)
        tr_free = s.sems("n_tr_free", 2)
        hi_ready = s.sem("n_hi_ready")
        id_zero = s.sem("n_id_zero")
        id_ready = s.sem("n_id_ready")
        with nc.Block() as block:

            @block.sync
            def _(sp):
                sp.dma_start(w_pre[:], w["norm_pre"][0:1, :].to_broadcast([P, DM])).then_inc(w_loaded, 16)
                with sp.Fori(0, TILES // 2) as i:
                    for k in range(2):
                        sp.wait_ge(h_made[k], i + 1)
                        sp.dma_start(x_sb[:, k, :], w["x"][0, bass.ds((2 * i + k) * P, P), :]
                                     ).then_inc(x_loaded[k], 16)

            @block.gpsimd
            def _(pool):
                pool.memset(eps[:], EPS).then_inc(eps_ready, 1)
                pool.memset(ident[:], 0.0).then_inc(id_zero, 1)
                pool.wait_ge(id_zero, 1)
                pool.affine_select(out=ident[:], in_=ident[:], compare_op=ALU.not_equal, fill=1.0, base=0,
                                   pattern=[[-1, P]], channel_multiplier=1).then_inc(id_ready, 1)

            @block.scalar
            def _(act):
                act.wait_ge(eps_ready, 1)
                with act.Fori(0, TILES // 2) as i:
                    for k in range(2):
                        act.wait_ge(x_loaded[k], 16 * i + 16)
                        act.activation(sq[:], x_sb[:, k, :], ACT.Square,
                                       accum_out=ssum[:, bass.ds(2 * i + k, 1)]).then_inc(squared, 1)
                        act.wait_ge(squared, 2 * i + k + 1)
                        act.activation(std[:, bass.ds(2 * i + k, 1)], ssum[:, bass.ds(2 * i + k, 1)], ACT.Sqrt,
                                       bias=eps[:], scale=1.0 / DM).then_inc(std_ready, 1)
                        act.wait_ge(tr_made[k], i + 2)
                        act.activation(h_hi[:, :, bass.ds((2 * i + k) * P, P)],
                                       tr[:, k, :].rearrange("p (c t) -> p c t", c=KC), ACT.Copy
                                       ).then_inc(hi_ready, 1)

            @block.vector
            def _(dve):
                for k in range(2):
                    dve.sem_inc(h_made[k], 1)
                    dve.sem_inc(tr_free[k], 1)
                dve.wait_ge(w_loaded, 16)
                with dve.Fori(0, TILES // 2) as i:
                    for k in range(2):
                        n = 2 * i + k
                        at = bass.ds(n, 1)
                        dve.wait_ge(std_ready, n + 1)
                        dve.reciprocal(rstd[:, at], std[:, at]).then_inc(rstd_ready, 1)
                        dve.wait_ge(rstd_ready, n + 1)
                        dve.wait_ge(tr_made[k], i + 1)
                        dve.scalar_tensor_tensor(h_tok[:, k, :], x_sb[:, k, :], rstd[:, at], w_pre[:], ALU.mult,
                                                 ALU.mult).then_inc(h_made[k], 1)
                        dve.wait_ge(hi_ready, n + 1)
                        dve.tensor_tensor(h_lo[:, :, bass.ds(n * P, P)],
                                          tr[:, k, :].rearrange("p (c t) -> p c t", c=KC),
                                          h_hi[:, :, bass.ds(n * P, P)], ALU.subtract).then_inc(tr_free[k], 1)

            @block.tensor
            def _(pe):
                for k in range(2):
                    pe.sem_inc(tr_made[k], 1)
                pe.wait_ge(id_ready, 1)
                with pe.Fori(0, TILES // 2) as i:
                    for k in range(2):
                        pe.wait_ge(h_made[k], i + 2)
                        pe.wait_ge(tr_free[k], i + 1)
                        for c in range(KC):
                            last = pe.transpose(tr[:, k, c * P:(c + 1) * P], h_tok[:, k, c * P:(c + 1) * P], ident[:])
                        last.then_inc(tr_made[k], 1)


def projection_stage(nc, w, d, h_hi, h_lo):
    pairs = {"z": SSM // P // 2, "xbc": (C_DT - C_XBC) // P // 2, "qkv": 5 * KV // P // 2, "g": KV // P // 2,
             "sc": 4 * SC // P // 2, "merge": 3 * DM // P // 2}
    base, n_pairs = {}, 0
    for kind, n in pairs.items():
        base[kind] = n_pairs
        n_pairs += n
    with ExitStack() as stack:
        s = Scope(nc, stack)
        raw = s.sb("p_raw", [P, 2, KC, P])
        w_hi = s.sb("p_whi", [P, 2, KC, P], F32R)
        w_lo = s.sb("p_wlo", [P, 2, KC, P], F32R)
        stage = s.sb("p_stage", [P, 2, SEQ])
        work = s.sb("p_work", [P, 2, SEQ])
        cw = s.sb("p_cw", [P, 16, 4])
        cb = s.sb("p_cb", [P, 16])
        scw = s.sb("p_scw", [P, 4, 3])
        acc = s.ps("p_acc", [P, 2, SEQ])
        raw_loaded = s.sems("p_raw_loaded", 2)
        consts_loaded = s.sem("p_consts_loaded")
        hi_ready = s.sem("p_hi_ready")
        carried = s.sem("p_carried")
        w_made = s.sems("p_w_made", 2)
        acc_made = s.sems("p_acc_made", 2)
        acc_taken = s.sems("p_acc_taken", 2)
        stored = s.sems("p_stored", 2)
        conv_step = s.sem("p_conv_step")
        conv_taken = s.sem("p_conv_taken")
        sc_step = s.sem("p_sc_step")
        sc_done = s.sem("p_sc_done")
        with nc.Block() as block:

            @block.sync
            def _(sp):
                def load(slot, use, col):
                    sp.wait_ge(w_made[slot], use + 1)
                    sp.dma_start(raw[:, slot], w["w_in"][0, :, bass.ds(col, P)].rearrange("(c p) n -> p c n", p=P)
                                 ).then_inc(raw_loaded[slot], 16)

                load(0, 0, C_DT)
                with nc.allow_non_contiguous_dma(reason="per-channel taps, once"):
                    for t in range(4):
                        sp.dma_start(cw[:, :, t:t + 1], w["ssm_conv_w"][0, t, :].rearrange("(b p o) -> p b o", p=P, o=1)
                                     ).then_inc(consts_loaded, 16)
                    sp.dma_start(cb[:], w["ssm_conv_b"][0, :].rearrange("(b p) -> p b", p=P)
                                 ).then_inc(consts_loaded, 16)
                    for t in range(3):
                        sp.dma_start(scw[:, :, t:t + 1], w["sc_conv_w"][0, t, :].rearrange("(b p o) -> p b o", p=P, o=1)
                                     ).then_inc(consts_loaded, 16)

                def run(kind, col, step=P):
                    with sp.Fori(0, pairs[kind]) as i:
                        load(1, base[kind] + i, col + 2 * P * i)
                        load(0, base[kind] + i + 1, col + 2 * P * i + P)

                run("z", C_Z)
                run("xbc", C_XBC)
                run("qkv", C_Q)
                run("g", C_G)
                with sp.Fori(0, SC // P) as f:
                    load(1, base["sc"] + 2 * f, C_U + P * f)
                    load(0, base["sc"] + 2 * f + 1, C_C + P * f)
                    load(1, base["sc"] + 2 * f + 1, C_B + P * f)
                    load(0, base["sc"] + 2 * f + 2, C_GSC + P * f)
                run("merge", C_MERGE)

            @block.gpsimd
            def _(pool):
                for k in range(2):
                    pool.sem_inc(w_made[k], 1)

                def split(slot, use, n):
                    pool.wait_ge(raw_loaded[slot], 16 * use + 16)
                    wait_alone(pool, acc_made[slot], use + 1, carried)
                    pool.tensor_copy(w_hi[:, slot], raw[:, slot]).then_inc(hi_ready, 1)
                    pool.wait_ge(hi_ready, n + 1)
                    pool.tensor_tensor(w_lo[:, slot], raw[:, slot], w_hi[:, slot], ALU.subtract
                                       ).then_inc(w_made[slot], 1)

                split(0, 0, 0)
                with pool.Fori(0, n_pairs) as i:
                    split(1, i, 2 * i + 1)
                    split(0, i + 1, 2 * i + 2)

            @block.tensor
            def _(pe):
                for k in range(2):
                    pe.sem_inc(acc_made[k], 1)

                def product(slot, use):
                    pe.wait_ge(w_made[slot], use + 2)
                    pe.wait_ge(acc_taken[slot], use + 1)
                    for t in range(SPANS):
                        span = slice(t * BANK, (t + 1) * BANK)
                        for c in range(KC):
                            pe.matmul(acc[:, slot, span], w_hi[:, slot, c], h_hi[:, c, span], start=c == 0, stop=False)
                            pe.matmul(acc[:, slot, span], w_hi[:, slot, c], h_lo[:, c, span], start=False, stop=False)
                            last = pe.matmul(acc[:, slot, span], w_lo[:, slot, c], h_hi[:, c, span], start=False,
                                             stop=c == KC - 1)
                    last.then_inc(acc_made[slot], 1)

                product(0, 0)
                with pe.Fori(0, n_pairs) as i:
                    product(1, i)
                    product(0, i + 1)

            @block.scalar
            def _(act):
                act.sem_inc(stored[0], 16)
                act.sem_inc(stored[1], 16)
                act.sem_inc(acc_taken[0], 1)
                act.sem_inc(acc_taken[1], 1)
                act.sem_inc(conv_taken, 2)

                def put(slot, use, func, out):
                    act.wait_ge(acc_made[slot], use + 2)
                    act.wait_ge(stored[slot], 16 * use + 16)
                    act.activation(stage[:, slot], acc[:, slot], func).then_inc(acc_taken[slot], 1)
                    act.wait_ge(acc_taken[slot], use + 2)
                    act.dma_start(out, stage[:, slot]).then_inc(stored[slot], 16)

                def run(kind, func, dest):
                    with act.Fori(0, pairs[kind]) as i:
                        put(1, base[kind] + i, func, dest[bass.ds(2 * i, 1)].rearrange("o p t -> p (o t)"))
                        put(0, base[kind] + i + 1, func, dest[bass.ds(2 * i + 1, 1)].rearrange("o p t -> p (o t)"))

                put(0, 0, ACT.Copy, d["dt"])
                run("z", ACT.Silu, d["z"])
                with act.Fori(0, pairs["xbc"]) as i:
                    for k in range(2):
                        slot, use = 1 - k, base["xbc"] + i + k
                        act.wait_ge(acc_taken[slot], use + 2)
                        act.wait_ge(stored[slot], 16 * use + 16)
                        act.activation(stage[:, slot], work[:, k], ACT.Silu).then_inc(conv_taken, 1)
                        act.wait_ge(conv_taken, 2 * i + k + 3)
                        act.dma_start(d["xbc"][bass.ds(2 * i + k, 1)].rearrange("o p t -> p (o t)"), stage[:, slot]
                                      ).then_inc(stored[slot], 16)
                run("qkv", ACT.Copy, d["qkv"])
                run("g", ACT.Silu, d["g"])
                with act.Fori(0, SC // P) as f:
                    use = base["sc"] + 2 * f
                    act.wait_ge(acc_made[1], use + 2)
                    act.wait_ge(sc_done, f + 1)
                    act.activation(work[:, 0], acc[:, 1], ACT.Copy).then_inc(acc_taken[1], 1)
                    act.wait_ge(acc_made[0], use + 4)
                    act.wait_ge(stored[1], 16 * use + 16)
                    act.activation(stage[:, 1], acc[:, 0], ACT.Silu).then_inc(acc_taken[0], 1)
                    act.wait_ge(sc_done, f + 2)
                    act.sem_inc(stored[0], 32)
                    act.sem_inc(stored[1], 16)
                    act.dma_start(d["y_sc"][bass.ds(f, 1)].rearrange("o p t -> p (o t)"), stage[:, 1]
                                  ).then_inc(stored[1], 16)
                run("merge", ACT.Sigmoid, d["gates"])
                act.wait_ge(stored[0], 16 * (n_pairs + 2))
                act.wait_ge(stored[1], 16 * (n_pairs + 1))

            @block.vector
            def _(dve):
                dve.sem_inc(sc_done, 1)
                dve.wait_ge(consts_loaded, 16 * 8)
                with dve.Fori(0, pairs["xbc"]) as i:
                    for k in range(2):
                        slot, use, b = 1 - k, base["xbc"] + i + k, 2 * i + k
                        n = 4 * b
                        dve.wait_ge(acc_made[slot], use + 2)
                        dve.wait_ge(conv_taken, b + 1)
                        dve.tensor_scalar(work[:, k], acc[:, slot], cw[:, bass.ds(b, 1), 3].rearrange("p o -> p o"),
                                          cb[:, bass.ds(b, 1)], ALU.mult, ALU.add).then_inc(conv_step, 1)
                        for tap in range(3):
                            back = 3 - tap
                            dve.wait_ge(conv_step, 3 * b + tap + 1)
                            ins = dve.scalar_tensor_tensor(work[:, k, back:], acc[:, slot, :SEQ - back],
                                                           cw[:, bass.ds(b, 1), tap], work[:, k, back:], ALU.mult,
                                                           ALU.add)
                            ins.then_inc(conv_step if tap < 2 else acc_taken[slot], 1)
                with dve.Fori(0, SC // P) as f:
                    use = base["sc"] + 2 * f
                    tap = lambda t: scw[:, bass.ds(f, 1), t]
                    dve.wait_ge(acc_made[0], use + 3)
                    dve.wait_ge(acc_taken[1], use + 2)
                    dve.tensor_tensor(work[:, 1], acc[:, 0], work[:, 0], ALU.mult).then_inc(acc_taken[0], 1)
                    dve.wait_ge(acc_taken[0], use + 3)
                    dve.tensor_scalar(work[:, 0], work[:, 1], tap(2), None, ALU.mult).then_inc(sc_step, 1)
                    for back in (1, 2):
                        dve.wait_ge(sc_step, 3 * f + back)
                        dve.scalar_tensor_tensor(work[:, 0, back:], work[:, 1, :SEQ - back], tap(2 - back),
                                                 work[:, 0, back:], ALU.mult, ALU.add).then_inc(sc_step, 1)
                    dve.wait_ge(sc_step, 3 * f + 3)
                    dve.wait_ge(acc_made[1], use + 3)
                    dve.tensor_tensor(work[:, 0], acc[:, 1], work[:, 0], ALU.mult).then_inc(acc_taken[1], 1)
                    dve.wait_ge(acc_taken[1], use + 3)
                    dve.wait_ge(acc_taken[0], use + 4)
                    dve.tensor_tensor(stage[:, 1], stage[:, 1], work[:, 0], ALU.mult).then_inc(sc_done, 1)


def ssd_stage(nc, w, d, ident, eps):
    N = TILES * HEADS
    with ExitStack() as stack:
        s = Scope(nc, stack)
        dt_raw = s.sb("s_dtraw", [HEADS, SEQ])
        bias_b, alog_b, dskip_b = (s.sb(n, [P, HEADS]) for n in ("s_bias", "s_alog", "s_dskip"))
        norm_b = s.sb("s_norm", [P, SSM])
        tri = s.sb("s_tri", [P, P])
        ones = s.sb("s_ones", [P, P])
        t0, t1, t2, t3 = (s.sb(f"s_t{i}", [P, N]) for i in range(4))
        dt, a, cs, ecs, elast, wdec = (s.sb(n, [P, N]) for n in ("s_dtt", "s_a", "s_cs", "s_ecs", "s_elast", "s_wdec"))
        xbc_t = s.sb("s_xbct", [P, 2, 16, P])
        z_t = s.sb("s_zt", [P, 2, KC, P])
        x_tok = s.sb("s_xtok", [P, 2, SSM])
        b_tok = s.sb("s_btok", [P, 2, GROUPS * STATE])
        a_now = s.sb("s_anow", [P, 2, HEADS])
        xdt = s.sb("s_xdt", [P, 2, SSM])
        xdec = s.sb("s_xdec", [P, 2, SSM])
        xd = s.sb("s_xd", [P, 2, SSM])
        cbm = s.sb("s_cbm", [P, GROUPS, P])
        fall = s.sb("s_fall", [P, 2, 4, P])
        decay = s.sb("s_decay", [P, 2, 4, P])
        mix = s.sb("s_mix", [P, 2, 4, P])
        state = s.sb("s_state", [P, SSM])
        sdec = s.sb("s_sdec", [P, SSM])
        y = s.sb("s_y", [P, SSM])
        yg = s.sb("s_yg", [P, TILES, SSM])
        sq = s.sb("s_sq", [P, 2, SSM])
        ss = s.sb("s_ss", [P, TILES * GROUPS])
        rstd = s.sb("s_rstd", [P, TILES * GROUPS])
        yn = s.sb("s_yn", [P, 2, SSM])
        y_out = s.sb("s_yout", [P, 2, KC, P])
        ps_x = s.ps("s_psx", [P, SSM])
        ps_m = s.ps("s_psm", [P, SSM])
        ps_bc = s.ps("s_psbc", [P, 2, BANK])
        ps_y = s.ps("s_psy", [P, 2, 2, GW])
        consts_loaded, turn = s.sem("s_consts_loaded"), s.sem("s_turn")
        loaded = s.sems("s_loaded", 2)
        x_transposed, b_transposed, cb_ready, z_transposed = (
            s.sem(n) for n in ("s_xT", "s_bT", "s_cb", "s_zT"))
        x_tok_ready, b_tok_ready, cbm_ready, yo_ready, skip_added, sdec_ready = (
            s.sem(n) for n in ("s_xtok_r", "s_btok_r", "s_cbm_r", "s_yo_r", "s_skip_r", "s_sdec_r"))
        a_ready, xdt_ready, xdec_ready, squared, bc_ready = (
            s.sem(n) for n in ("s_a_r", "s_xdt_r", "s_xdec_r", "s_sq_r", "s_bc_r"))
        y_made = s.sem("s_y_made")
        decay_made = s.sem("s_decay_made")
        fall_made = s.sem("s_fall_made")
        mix_made = s.sem("s_mix_made")
        y_taken = s.sem("s_y_taken")
        update_made = s.sem("s_update_made")
        gated = s.sem("s_gated")
        xd_made = s.sem("s_xd_made")
        state_made = s.sem("s_state_made")
        turn2, carried = s.sem("s_turn2"), s.sem("s_carried")
        yn_made = s.sem("s_yn_made")
        out_taken = s.sem("s_out_taken")
        out_made = s.sem("s_out_made")
        stored = s.sems("s_stored", 2)

        def heads(ap):
            return ap.rearrange("p (h q) -> p h q", q=HDIM)

        def spread(ap, n, width=HDIM):
            return ap.unsqueeze(2).to_broadcast([P, n, width])

        with nc.Block() as block:

            @block.sync
            def _(sp):
                sp.dma_start(dt_raw[:], d["dt"][0:HEADS, :]).then_inc(consts_loaded, 16)
                for to, of in ((bias_b, "dt_bias"), (alog_b, "a_log"), (dskip_b, "d_skip")):
                    sp.dma_start(to[:], w[of][0:1, :].to_broadcast([P, HEADS])).then_inc(consts_loaded, 16)
                sp.dma_start(norm_b[:], w["ssm_norm"][0:1, :].to_broadcast([P, SSM])).then_inc(consts_loaded, 16)
                with sp.Fori(0, TILES // 2) as i:
                    for k in range(2):
                        c = 2 * i + k
                        sp.wait_ge(y_made, 4 * c + 4)
                        at = bass.ds(c * P, P)
                        sp.dma_start(xbc_t[:, k], d["xbc"][:, :, at].rearrange("b p t -> p b t")).then_inc(loaded[k], 16)
                        sp.dma_start(z_t[:, k], d["z"][:, :, at].rearrange("b p t -> p b t")).then_inc(loaded[k], 16)

            @block.gpsimd
            def _(pool):
                pool.sem_inc(xd_made, 2)
                pool.memset(ones[:], 1.0).then_inc(turn, 1)
                pool.wait_ge(turn, 1)
                pool.affine_select(out=tri[:], in_=ones[:], compare_op=ALU.is_ge, fill=0.0, base=0,
                                   pattern=[[1, P]], channel_multiplier=-1).then_inc(turn, 1)
                pool.memset(state[:], 0.0).then_inc(state_made, 1)
                pool.wait_ge(turn, 21)
                with pool.Fori(0, TILES // 2) as i:
                    for k in range(2):
                        c = 2 * i + k
                        at = bass.ds(c * HEADS, HEADS)
                        wait_alone(pool, y_made, 4 * c + 4, carried)
                        pool.tensor_copy(a_now[:, k], a[:, at]).then_inc(a_ready, 1)
                        pool.wait_ge(x_tok_ready, c + 1)
                        pool.tensor_tensor(heads(xdt[:, k]), heads(x_tok[:, k]), spread(dt[:, at], HEADS), ALU.mult
                                           ).then_inc(xdt_ready, 1)
                        pool.wait_ge(update_made, c + 1)
                        pool.tensor_tensor(heads(xdec[:, k]), heads(x_tok[:, k]), spread(wdec[:, at], HEADS), ALU.mult
                                           ).then_inc(xdec_ready, 1)
                        pool.wait_ge(gated, c + 1)
                        pool.tensor_tensor(heads(xd[:, k]), heads(x_tok[:, k]), spread(dskip_b[:], HEADS), ALU.mult
                                           ).then_inc(xd_made, 1)
                        pool.wait_ge(state_made, c + 1)
                        pool.tensor_tensor(heads(sdec[:]), heads(state[:]), spread(elast[:, at], HEADS), ALU.mult
                                           ).then_inc(sdec_ready, 1)

            @block.tensor
            def _(pe):
                pe.sem_inc(y_made, 8)
                pe.sem_inc(update_made, 2)
                pe.wait_ge(consts_loaded, 80)
                pe.wait_ge(turn, 2)
                for c in range(TILES):
                    last = pe.transpose(ps_x[:, c * HEADS:(c + 1) * HEADS], dt_raw[:, c * P:(c + 1) * P],
                                        ident[:HEADS, :HEADS])
                last.then_inc(turn, 1)
                pe.wait_ge(turn, 16)
                pe.matmul(ps_y[:, 0, 0], tri[:], a[:], start=True, stop=True)
                pe.matmul(ps_y[:, 1, 0], ones[:], a[:], start=True, stop=True).then_inc(turn, 1)
                pe.wait_ge(turn, 21)
                with pe.Fori(0, TILES // 2) as i:
                    for k in range(2):
                        c = 2 * i + k
                        b_t, c_t = xbc_t[:, k, 8:12], xbc_t[:, k, 12:16]
                        pe.wait_ge(loaded[k], 32 * i + 32)
                        pe.wait_ge(gated, c + 2)
                        for b in range(KC):
                            last = pe.transpose(ps_x[:, b * P:(b + 1) * P], xbc_t[:, k, b], ident[:])
                        last.then_inc(x_transposed, 1)
                        pe.wait_ge(state_made, c + 1)
                        for g in range(GROUPS):
                            last = pe.transpose(ps_m[:, g * P:(g + 1) * P], b_t[:, g], ident[:])
                        last.then_inc(b_transposed, 1)
                        for g in range(GROUPS):
                            last = pe.matmul(ps_m[:, BANK + g * P:BANK + (g + 1) * P], b_t[:, g], c_t[:, g],
                                             start=True, stop=True)
                        last.then_inc(cb_ready, 1)

                        def running_sums(g):
                            pe.wait_ge(fall_made, 4 * c + g + 1)
                            for j in range(4):
                                h = 4 * g + j
                                last = pe.matmul(ps_bc[:, g % 2, j * P:(j + 1) * P],
                                                 a_now[:, k, h:h + 1].to_broadcast([P, P]), tri[:], start=True, stop=True)
                            last.then_inc(bc_ready, 1)

                        def group(g):
                            pe.wait_ge(mix_made, 4 * c + g + 3)
                            pe.wait_ge(y_taken, 4 * c + g + 1)
                            for j in range(4):
                                at = slice(j * HDIM, (j + 1) * HDIM)
                                pe.matmul(ps_y[:, g % 2, 0, at], mix[:, g % 2, j], xdt[:, k, g * GW + j * HDIM:
                                          g * GW + (j + 1) * HDIM], start=True, stop=True)
                            pe.matmul(ps_y[:, g % 2, 1], c_t[:, g], state[:, g * GW:(g + 1) * GW], start=True,
                                      stop=True).then_inc(y_made, 1)

                        pe.wait_ge(a_ready, c + 1)
                        running_sums(0)
                        pe.wait_ge(x_tok_ready, c + 1)
                        for b in range(KC):
                            last = pe.transpose(ps_x[:, b * P:(b + 1) * P], z_t[:, k, b], ident[:])
                        last.then_inc(z_transposed, 1)
                        running_sums(1)
                        pe.wait_ge(xdt_ready, c + 1)
                        group(0)
                        running_sums(2)
                        group(1)
                        running_sums(3)
                        group(2)
                        group(3)
                        pe.wait_ge(b_tok_ready, c + 1)
                        pe.wait_ge(xdec_ready, c + 1)
                        pe.wait_ge(cbm_ready, c + 1)
                        for g in range(GROUPS):
                            last = pe.matmul(ps_m[:, g * GW:(g + 1) * GW], b_tok[:, k, g * P:(g + 1) * P],
                                             xdec[:, k, g * GW:(g + 1) * GW], start=True, stop=True)
                        last.then_inc(update_made, 1)
                with pe.Fori(0, TILES // 2) as i:
                    for k in range(2):
                        bank = (ps_x, ps_m)[k]
                        pe.wait_ge(yn_made, 2 * i + k + 3)
                        pe.wait_ge(out_taken, 2 * i + k + 1)
                        for b in range(KC):
                            last = pe.transpose(bank[:, b * P:(b + 1) * P], yn[:, k, b * P:(b + 1) * P], ident[:])
                        last.then_inc(out_made, 1)

            @block.scalar
            def _(act):
                act.sem_inc(decay_made, 2)
                act.sem_inc(squared, 1)
                act.sem_inc(fall_made, 2)
                act.sem_inc(out_taken, 2)
                act.wait_ge(turn, 5)
                act.activation(t1[:], t1[:], ACT.Exp, scale=-1.0).then_inc(turn, 1)
                act.wait_ge(turn, 7)
                act.activation(t3[:], t2[:], ACT.Ln).then_inc(turn, 1)
                act.activation(alog_b[:], alog_b[:], ACT.Exp).then_inc(turn, 1)
                act.wait_ge(turn, 17)
                act.activation(ecs[:], ps_y[:, 0, 0], ACT.Exp).then_inc(turn, 1)
                act.activation(elast[:], ps_y[:, 1, 0], ACT.Exp).then_inc(turn, 1)
                act.wait_ge(turn, 20)
                act.activation(t1[:], t0[:], ACT.Exp).then_inc(turn2, 1)
                with act.Fori(0, TILES // 2) as i:
                    for k in range(2):
                        c = 2 * i + k
                        act.wait_ge(x_transposed, c + 1)
                        act.wait_ge(xd_made, c + 1)
                        act.activation(x_tok[:, k], ps_x[:], ACT.Copy).then_inc(x_tok_ready, 1)
                        act.wait_ge(b_transposed, c + 1)
                        act.wait_ge(update_made, c + 1)
                        act.activation(b_tok[:, k], ps_m[:, :BANK], ACT.Copy).then_inc(b_tok_ready, 1)
                        for g in range(GROUPS):
                            act.wait_ge(bc_ready, 4 * c + g + 1)
                            act.wait_ge(mix_made, 4 * c + g + 1)
                            for j in range(4):
                                last = act.activation(fall[:, g % 2, j], ps_bc[:, g % 2, j * P:(j + 1) * P], ACT.Relu,
                                                      bias=cs[:, bass.ds(c * HEADS + 4 * g + j, 1)], scale=-1.0)
                            last.then_inc(fall_made, 1)
                            act.wait_ge(fall_made, 4 * c + g + 3)
                            act.activation(decay[:, g % 2], fall[:, g % 2], ACT.Exp, scale=-1.0).then_inc(decay_made, 1)
                        if k:
                            act.wait_ge(squared, i + 1)
                            for q in range(2):
                                act.wait_ge(gated, 2 * i + q + 3)
                                for g in range(GROUPS):
                                    last = act.activation(sq[:, q, g * GW:(g + 1) * GW], yg[:, bass.ds(2 * i + q, 1), g * GW:(g + 1) * GW
                                                                    ].rearrange("p o q -> p (o q)"), ACT.Square,
                                                          accum_out=ss[:, bass.ds((2 * i + q) * GROUPS + g, 1)])
                            last.then_inc(squared, 1)
                act.wait_ge(squared, TILES // 2 + 1)
                act.activation(rstd[:], ss[:], ACT.Sqrt, bias=eps[:], scale=1.0 / GW).then_inc(turn2, 1)
                with act.Fori(0, TILES // 2) as i:
                    for k in range(2):
                        c = 2 * i + k
                        act.wait_ge(out_made, c + 1)
                        act.wait_ge(stored[k], 16 * i + 16)
                        act.activation(y_out[:, k], (ps_x, ps_m)[k][:], ACT.Copy).then_inc(out_taken, 1)
                        act.wait_ge(out_taken, c + 3)
                        act.dma_start(d["y_ssm"][:, :, bass.ds(c * P, P)].rearrange("b p t -> p b t"), y_out[:, k]
                                      ).then_inc(stored[k], 16)
                for k in range(2):
                    act.wait_ge(stored[k], 16 * (TILES // 2) + 16)

            @block.vector
            def _(dve):
                dve.sem_inc(mix_made, 2)
                dve.sem_inc(y_taken, 2)
                dve.sem_inc(gated, 2)
                dve.sem_inc(yn_made, 2)
                for k in range(2):
                    dve.sem_inc(stored[k], 16)
                tt, ts, stt = dve.tensor_tensor, dve.tensor_scalar, dve.scalar_tensor_tensor
                chunked = lambda ap: ap.rearrange("p (c h) -> p c h", h=HEADS)
                every = lambda ap: ap.unsqueeze(1).to_broadcast([P, TILES, HEADS])
                dve.wait_ge(turn, 3)
                tt(chunked(t0[:]), chunked(ps_x[:, :N]), every(bias_b[:]), ALU.add).then_inc(turn, 1)
                dve.wait_ge(turn, 4)
                stt(t1[:], t0[:], -1.0, t0[:], ALU.mult, ALU.max).then_inc(turn, 1)
                dve.wait_ge(turn, 6)
                ts(t2[:], t1[:], 1.0, None, ALU.add).then_inc(turn, 1)
                dve.wait_ge(turn, 9)
                ts(t2[:], t2[:], -1.0, None, ALU.add).then_inc(turn, 1)
                dve.wait_ge(turn, 10)
                ts(dt[:], t2[:], 0.0, None, ALU.is_equal).then_inc(turn, 1)
                dve.wait_ge(turn, 11)
                tt(t3[:], t3[:], dt[:], ALU.add)
                tt(t2[:], t2[:], dt[:], ALU.add).then_inc(turn, 1)
                dve.wait_ge(turn, 12)
                dve.reciprocal(t2[:], t2[:])
                tt(t3[:], t3[:], t1[:], ALU.mult).then_inc(turn, 1)
                dve.wait_ge(turn, 13)
                tt(t3[:], t3[:], t2[:], ALU.mult).then_inc(turn, 1)
                dve.wait_ge(turn, 14)
                stt(dt[:], t0[:], 0.0, t3[:], ALU.max, ALU.add).then_inc(turn, 1)
                dve.wait_ge(turn, 15)
                stt(chunked(a[:]), chunked(dt[:]), -1.0, every(alog_b[:]), ALU.mult, ALU.mult).then_inc(turn, 1)
                dve.wait_ge(turn, 19)
                dve.tensor_copy(cs[:], ps_y[:, 0, 0]).then_inc(turn2, 1)
                dve.wait_ge(turn2, 1)
                tt(t0[:], ps_y[:, 1, 0], cs[:], ALU.subtract).then_inc(turn, 1)
                dve.wait_ge(turn2, 2)
                tt(wdec[:], dt[:], t1[:], ALU.mult).then_inc(turn, 1)
                with dve.Fori(0, TILES // 2) as i:
                    for k in range(2):
                        c = 2 * i + k
                        dve.wait_ge(cb_ready, c + 1)
                        tt(cbm[:], ps_m[:, BANK:].rearrange("p (g l) -> p g l", l=P),
                           tri[:].unsqueeze(1).to_broadcast([P, GROUPS, P]), ALU.mult).then_inc(cbm_ready, 1)
                        dve.wait_ge(cbm_ready, c + 1)

                        def combine(g):
                            dve.wait_ge(decay_made, 4 * c + g + 3)
                            dve.wait_ge(y_made, 4 * c + g + 7)
                            tt(mix[:, g % 2], decay[:, g % 2], cbm[:, g].unsqueeze(1).to_broadcast([P, 4, P]),
                               ALU.mult).then_inc(mix_made, 1)

                        def take(g):
                            at = slice(g * GW, (g + 1) * GW)
                            dve.wait_ge(y_made, 4 * c + g + 9)
                            tt(heads(y[:, at]), heads(ps_y[:, g % 2, 1]), spread(ecs[:, bass.ds(c * HEADS + 4 * g, 4)], 4),
                               ALU.mult).then_inc(yo_ready, 1)
                            dve.wait_ge(yo_ready, 4 * c + g + 1)
                            tt(y[:, at], ps_y[:, g % 2, 0], y[:, at], ALU.add).then_inc(y_taken, 1)

                        combine(0)
                        combine(1)
                        take(0)
                        combine(2)
                        take(1)
                        combine(3)
                        take(2)
                        take(3)
                        dve.wait_ge(y_taken, 4 * c + 6)
                        dve.wait_ge(xd_made, c + 3)
                        tt(y[:], y[:], xd[:, k], ALU.add).then_inc(skip_added, 1)
                        dve.wait_ge(skip_added, c + 1)
                        dve.wait_ge(z_transposed, c + 1)
                        tt(yg[:, bass.ds(c, 1)].rearrange("p o q -> p (o q)"), ps_x[:], y[:], ALU.mult).then_inc(gated, 1)
                        dve.wait_ge(sdec_ready, c + 1)
                        dve.wait_ge(update_made, c + 3)
                        tt(state[:], ps_m[:], sdec[:], ALU.add).then_inc(state_made, 1)
                dve.wait_ge(turn2, 3)
                dve.reciprocal(rstd[:], rstd[:]).then_inc(turn2, 1)
                dve.wait_ge(turn2, 4)
                with dve.Fori(0, TILES // 2) as i:
                    for k in range(2):
                        c = 2 * i + k
                        dve.wait_ge(out_taken, c + 1)
                        for g in range(GROUPS):
                            at = slice(g * GW, (g + 1) * GW)
                            last = stt(yn[:, k, at], yg[:, bass.ds(c, 1), at].rearrange("p o q -> p (o q)"),
                                       rstd[:, bass.ds(c * GROUPS + g, 1)], norm_b[:, at], ALU.mult, ALU.mult)
                        last.then_inc(yn_made, 1)


def attention_stage(nc, w, d, ident):
    NB, W, PAIRS = TILES, HDIM + 2, SLOTS // 2
    dil = [x[1] for x in PATTERNS]
    blocks = [[(r, n) for r in range(x) for n in range(SEQ // x // P)] for x in dil]
    steps = [(g, sl, b) for g in range(3) for sl in range(2) for b in range(0, NB, 2)]
    NS, NV = len(steps), 12
    HALF = (NS + NV) // 2
    stores = [1, dil[1], 1]
    with ExitStack() as stack:
        s = Scope(nc, stack)
        q_t, k_t, v_t = s.sb("a_q", [P, 3, SEQ]), s.sb("a_k", [P, 3, SEQ]), s.sb("a_v", [P, SEQ])
        qr = s.sb("a_qr", [P, 2, SEQ])
        v_tok = s.sb("a_vt", [P, 3, NB, P])
        band = s.sb("a_band", [P, 2, P])
        zero = s.sb("a_zero", [P, 2, P])
        scores = s.sb("a_scores", [P, 4, 2, 2 * P])
        probs = s.sb("a_probs", [P, 4, 2, 2 * P])
        probs_t = s.sb("a_probst", [P, 4, 4, P])
        neg = s.sb("a_neg", [P, 4, 2])
        att = s.sb("a_att", [P, 3, NB, 2, W])
        ps_s = s.ps("a_pss", [P, 2, 2, 2 * P])
        ps_t = s.ps("a_pst", [P, 4, 4, P])
        ps_o = s.ps("a_pso", [P, 2, 8, HDIM])
        q_loaded, v_loaded, band_turn = s.sem("a_q_loaded"), s.sem("a_v_loaded"), s.sem("a_band_turn")
        permuted, v_turned, max_made, negated = (s.sem(n) for n in ("a_permuted", "a_vT", "a_max", "a_neg_r"))
        s_made = s.sem("a_s_made")
        masked = s.sem("a_masked")
        exped = s.sem("a_exped")
        p_turned = s.sem("a_pT")
        t_taken = s.sems("a_t_taken", 2)
        o_made = s.sem("a_o_made")
        o_taken = s.sem("a_o_taken")
        stored = s.sems("a_stored", 3)
        carried = s.sems("a_carried", 2)

        def width(g, b):
            return (1 if blocks[g][b][1] == 0 else 2) * P

        def strided(ap, g):
            return ap.rearrange("p (m r) -> p r m", r=dil[g])

        def row(block):
            return block.rearrange("o p t -> p (o t)")

        def evacuate(eng, parity, copy, i, j):
            eng.wait_ge(p_turned, NS * i + j + 5)
            eng.wait_ge(o_made, NS * i + j + 1)
            n = NV + j
            g, sl, b = steps[j]
            if width(g, b) == width(g, b + 1) == 2 * P:
                copy(probs_t[:, j % 4], ps_t[:, n % 4]).then_inc(t_taken[parity], 1)
            elif width(g, b + 1) == P:
                copy(probs_t[:, j % 4, 1::2], ps_t[:, n % 4, 1::2]).then_inc(t_taken[parity], 1)
            else:
                copy(probs_t[:, j % 4, 1:], ps_t[:, n % 4, 1:]).then_inc(t_taken[parity], 1)

        def evacuate_v(eng, parity, copy, i):
            eng.wait_ge(o_made, NS * i + 4)
            for n in range(parity, NV, 2):
                eng.wait_ge(v_turned, NV * i + n + 1)
                copy(v_tok[:, n // 4, n % 4 * 4:n % 4 * 4 + 4], ps_t[:, n % 4]).then_inc(t_taken[parity], 1)

        with nc.Block() as block:

            @block.sync
            def _(sp):
                with sp.Fori(0, PAIRS) as i:
                    sp.wait_ge(s_made, NS * i + 1)
                    sp.dma_start(v_t[:], row(d["qkv"][bass.ds(16 + i, 1)])).then_inc(v_loaded, 16)
                    sp.dma_start(k_t[:, 0], row(d["qkv"][bass.ds(12 + i, 1)])).then_inc(q_loaded, 16)
                    for g in range(3):
                        sp.dma_start(q_t[:, g], row(d["qkv"][bass.ds(4 * g + i, 1)])).then_inc(q_loaded, 16)
                    for g in range(3):
                        sp.wait_ge(o_taken, 12 * i + 4 * g + 6)
                        to = d["att"][g, :, bass.ds(i, 1)]
                        for r in range(stores[g]):
                            if g == 1:
                                n = NB // dil[1]
                                sp.dma_start(to.rearrange("(n p r) o q -> r p n (o q)", p=P, r=dil[1])[r],
                                             att[:, g, r * n:(r + 1) * n].rearrange("p n a b -> p n (a b)")
                                             ).then_inc(stored[g], 16)
                            else:
                                order = "(n p) o q -> p n (o q)" if g == 0 else "(p n) o q -> p n (o q)"
                                sp.dma_start(to.rearrange(order, p=P), att[:, g].rearrange("p n a b -> p n (a b)")
                                             ).then_inc(stored[g], 16)
                for g in range(3):
                    sp.wait_ge(stored[g], 16 * stores[g] * (PAIRS + 1))

            @block.gpsimd
            def _(pool):
                pool.memset(zero[:], 0.0).then_inc(band_turn, 1)
                pool.wait_ge(band_turn, 1)
                pool.affine_select(out=band[:, 0], in_=zero[:, 0], compare_op=ALU.is_ge, fill=NEG, base=0,
                                   pattern=[[1, P]], channel_multiplier=-1).then_inc(band_turn, 1)
                pool.affine_select(out=band[:, 1], in_=zero[:, 1], compare_op=ALU.is_ge, fill=NEG, base=0,
                                   pattern=[[-1, P]], channel_multiplier=1).then_inc(band_turn, 1)
                with pool.Fori(0, PAIRS) as i:
                    wait_alone(pool, q_loaded, 64 * i + 64, carried[0])
                    for g in (1, 2):
                        pool.tensor_copy(k_t[:, g].rearrange("p (r m) -> p r m", r=dil[g]), strided(k_t[:, 0], g))
                        pool.tensor_copy(qr[:, g - 1].rearrange("p (r m) -> p r m", r=dil[g]), strided(q_t[:, g], g)
                                         ).then_inc(permuted, 1)

            @block.tensor
            def _(pe):
                pe.sem_inc(s_made, 1)
                pe.sem_inc(p_turned, 4)
                pe.sem_inc(o_made, 4)
                with pe.Fori(0, PAIRS) as i:
                    pe.wait_ge(v_loaded, 16 * i + 16)
                    for n in range(NV):
                        g = n // 4
                        pe.wait_ge(t_taken[n % 2], HALF * i + n // 2 + 1)
                        for b in range(4):
                            r, m = blocks[g][n % 4 * 4 + b]
                            last = pe.transpose(ps_t[:, n % 4, b], strided(v_t[:], g)[:, r, m * P:(m + 1) * P], ident[:])
                        last.then_inc(v_turned, 1)
                    pe.wait_ge(q_loaded, 64 * i + 64)

                    def score(j):
                        g, sl, b = steps[j]
                        if b == 0 and sl == 0 and g:
                            pe.wait_ge(permuted, 2 * i + g)
                        rows = slice(HDIM * sl, HDIM * sl + HDIM)
                        pe.wait_ge(masked, NS * i + j + 1)
                        q = q_t[rows, 0] if g == 0 else qr[rows, g - 1]
                        for e in range(2):
                            n, at = width(g, b + e), (b + e) * P
                            last = pe.matmul(ps_s[:, j % 2, e, 2 * P - n:], q[:, at:at + P],
                                             k_t[rows, g, at + P - n:at + P], start=True, stop=True)
                        last.then_inc(s_made, 1)

                    def turn(j):
                        g, sl, b = steps[j]
                        pe.wait_ge(exped, NS * i + j + 5)
                        pe.wait_ge(t_taken[j % 2], HALF * i + (NV + j) // 2 + 1)
                        for e in range(2):
                            for h in range(2 - width(g, b + e) // P, 2):
                                last = pe.transpose(ps_t[:, (NV + j) % 4, 2 * e + h], probs[:, j % 4, e, h * P:(h + 1) * P],
                                                    ident[:])
                        last.then_inc(p_turned, 1)

                    def output(j):
                        g, sl, b = steps[j]
                        if j == 0:
                            pe.wait_ge(t_taken[1], HALF * i + NV // 2 + 2)
                        pe.wait_ge(t_taken[j % 2], HALF * i + (NV + j) // 2 + 3)
                        if j % 4 == 0:
                            pe.wait_ge(o_taken, 12 * i + j // 4 + 1)
                        for e in range(2):
                            first = 2 - width(g, b + e) // P
                            for h in range(first, 2):
                                last = pe.matmul(ps_o[:, j // 4 % 2, (b + e) % 8], probs_t[:, j % 4, 2 * e + h],
                                                 v_tok[:, g, b + e - 1 + h, HDIM * sl:HDIM * sl + HDIM],
                                                 start=h == first, stop=h == 1)
                        last.then_inc(o_made, 1)

                    for j in range(NS + 4):
                        if j < NS:
                            score(j)
                        if 2 <= j < NS + 2:
                            turn(j - 2)
                        if j >= 4:
                            output(j - 4)

            @block.scalar
            def _(act):
                act.sem_inc(exped, 4)
                act.sem_inc(t_taken[1], 2)
                copy = lambda to, of: act.activation(to, of, ACT.Copy)
                with act.Fori(0, PAIRS) as i:
                    evacuate_v(act, 1, copy, i)
                    for j in range(NS + 2):
                        if j < NS:
                            g, sl, b = steps[j]
                            act.wait_ge(negated, NS * i + j + 1)
                            act.wait_ge(p_turned, NS * i + j + 1)
                            if j % 16 == 0:
                                act.wait_ge(stored[g], 16 * stores[g] * (i + 1))
                            for e in range(2):
                                n = width(g, b + e)
                                last = act.activation(probs[:, j % 4, e, 2 * P - n:], scores[:, j % 4, e, 2 * P - n:],
                                                      ACT.Exp, bias=neg[:, j % 4, e:e + 1], scale=HDIM ** -0.5,
                                                      accum_out=att[:, g, b + e, sl, HDIM + 1:])
                            last.then_inc(exped, 1)
                        if j >= 2 and j % 2:
                            evacuate(act, 1, copy, i, j - 2)

            @block.vector
            def _(dve):
                dve.sem_inc(masked, 2)
                dve.sem_inc(t_taken[0], 2)
                dve.sem_inc(o_taken, 2)
                for g in range(3):
                    dve.sem_inc(stored[g], 16 * stores[g])
                dve.wait_ge(band_turn, 3)
                keys = band[:].rearrange("p a k -> p (a k)")
                with dve.Fori(0, PAIRS) as i:
                    evacuate_v(dve, 0, dve.tensor_copy, i)
                    for j in range(NS + 5):
                        if j < NS:
                            g, sl, b = steps[j]
                            if j % 16 == 0:
                                dve.wait_ge(stored[g], 16 * stores[g] * (i + 1))
                            dve.wait_ge(exped, NS * i + j + 1)
                            wait_alone(dve, s_made, NS * i + j + 2, carried[1])
                            for e in range(2):
                                n = width(g, b + e)
                                last = dve.tensor_tensor_reduce(
                                    out=scores[:, j % 4, e, 2 * P - n:], in0=ps_s[:, j % 2, e, 2 * P - n:],
                                    in1=keys[:, 2 * P - n:], scale=1.0, scalar=NEG, op0=ALU.add, op1=ALU.max,
                                    accum_out=att[:, g, b + e, sl, HDIM:HDIM + 1])
                            last.then_inc(masked, 1)
                            dve.wait_ge(masked, NS * i + j + 3)
                            dve.tensor_scalar(neg[:, j % 4], att[:, g, b:b + 2, sl, HDIM], -HDIM ** -0.5, None, ALU.mult
                                              ).then_inc(negated, 1)
                        if 2 <= j < NS + 2 and j % 2 == 0:
                            evacuate(dve, 0, dve.tensor_copy, i, j - 2)
                        if j >= 8 and j % 4 == 0:
                            grp = j // 4 - 2
                            g, sl, b = steps[4 * grp]
                            dve.wait_ge(o_made, NS * i + 4 * grp + 8)
                            dve.tensor_copy(att[:, g, b:b + 8, sl, :HDIM], ps_o[:, grp % 2]).then_inc(o_taken, 1)


def attention_merge_stage(nc, d, ident):
    W = HDIM + 2
    with ExitStack() as stack:
        s = Scope(nc, stack)
        att = s.sb("m_att", [P, 2, 3, SLOTS, W])
        g_t = s.sb("m_gt", [P, 2, KV // P, P])
        top = s.sb("m_top", [P, 2, SLOTS])
        low = s.sb("m_low", [P, 2, 3, SLOTS])
        ex = s.sb("m_ex", [P, 2, 3, SLOTS])
        den = s.sb("m_den", [P, 2, SLOTS])
        part = s.sb("m_part", [P, 2, 3, SLOTS, HDIM])
        o = s.sb("m_o", [P, 2, KV])
        y = s.sb("m_y", [P, 2, KV // P, P])
        ps = s.ps("m_ps", [P, 2, KV])
        loaded, stored = s.sems("m_loaded", 2), s.sems("m_stored", 2)
        low_made, ex_made, step, part_made, o_half = (s.sem("m_" + n) for n in ("low", "exr", "step", "partr", "ohalf"))
        den_made, ex_scaled = s.sem("m_denr"), s.sem("m_exs")
        o_made = s.sem("m_o_made")
        turned = s.sem("m_turned")
        y_made = s.sem("m_y_made")
        with nc.Block() as block:

            @block.sync
            def _(sp):
                with sp.Fori(0, TILES // 2) as i:
                    for k in range(2):
                        c = 2 * i + k
                        at = bass.ds(c * P, P)
                        sp.wait_ge(y_made, c + 1)
                        for g in range(3):
                            sp.dma_start(att[:, k, g].rearrange("p s q -> p (s q)"),
                                         d["att"][g, at].rearrange("t a q -> t (a q)")).then_inc(loaded[k], 16)
                        sp.dma_start(g_t[:, k], d["g"][:, :, at].rearrange("b p t -> p b t")).then_inc(loaded[k], 16)

            @block.vector
            def _(dve):
                tt = dve.tensor_tensor
                dve.sem_inc(y_made, 2)
                with dve.Fori(0, TILES // 2) as i:
                    for k in range(2):
                        c = 2 * i + k
                        m = lambda g: att[:, k, g, :, HDIM]
                        dve.wait_ge(loaded[k], 64 * i + 64)
                        tt(top[:, k], m(0), m(1), ALU.max).then_inc(step, 1)
                        dve.wait_ge(step, 4 * c + 1)
                        tt(top[:, k], top[:, k], m(2), ALU.max).then_inc(step, 1)
                        dve.wait_ge(step, 4 * c + 2)
                        tt(low[:, k], att[:, k, :, :, HDIM], top[:, k].unsqueeze(1).to_broadcast([P, 3, SLOTS]),
                           ALU.subtract).then_inc(low_made, 1)
                        dve.wait_ge(ex_made, c + 1)
                        tt(low[:, k], ex[:, k], att[:, k, :, :, HDIM + 1], ALU.mult).then_inc(step, 1)
                        dve.wait_ge(step, 4 * c + 3)
                        dve.tensor_reduce(den[:, k], low[:, k].rearrange("p g s -> p s g"), mybir.AxisListType.X, ALU.add
                                          ).then_inc(step, 1)
                        dve.wait_ge(step, 4 * c + 4)
                        dve.reciprocal(den[:, k], den[:, k]).then_inc(den_made, 1)
                        dve.wait_ge(den_made, c + 1)
                        tt(ex[:, k], ex[:, k], den[:, k].unsqueeze(1).to_broadcast([P, 3, SLOTS]), ALU.mult
                           ).then_inc(ex_scaled, 1)
                        dve.wait_ge(ex_scaled, c + 1)
                        dve.wait_ge(o_made, c + 1)
                        for g in range(3):
                            last = tt(part[:, k, g], att[:, k, g, :, :HDIM], ex[:, k, g].unsqueeze(2).to_broadcast(
                                [P, SLOTS, HDIM]), ALU.mult)
                        last.then_inc(part_made, 1)
                        dve.wait_ge(turned, c + 3)
                        dve.wait_ge(stored[k], 16 * i + 16)
                        tt(y[:, k], ps[:, k].rearrange("p (b t) -> p b t", t=P), g_t[:, k], ALU.mult).then_inc(y_made, 1)

            @block.gpsimd
            def _(pool):
                pool.sem_inc(o_made, 2)
                flat = lambda ap: ap.rearrange("p s q -> p (s q)")
                with pool.Fori(0, TILES // 2) as i:
                    for k in range(2):
                        c = 2 * i + k
                        pool.wait_ge(part_made, c + 1)
                        pool.wait_ge(turned, c + 1)
                        pool.tensor_tensor(o[:, k], flat(part[:, k, 0]), flat(part[:, k, 1]), ALU.add).then_inc(o_half, 1)
                        pool.wait_ge(o_half, c + 1)
                        pool.tensor_tensor(o[:, k], o[:, k], flat(part[:, k, 2]), ALU.add).then_inc(o_made, 1)

            @block.tensor
            def _(pe):
                pe.sem_inc(turned, 2)
                with pe.Fori(0, TILES // 2) as i:
                    for k in range(2):
                        c = 2 * i + k
                        pe.wait_ge(o_made, c + 3)
                        pe.wait_ge(y_made, c + 1)
                        for b in range(KV // P):
                            last = pe.transpose(ps[:, k, b * P:(b + 1) * P], o[:, k, b * P:(b + 1) * P], ident[:])
                        last.then_inc(turned, 1)

            @block.scalar
            def _(act):
                act.sem_inc(stored[0], 16)
                act.sem_inc(stored[1], 16)
                with act.Fori(0, TILES // 2) as i:
                    for k in range(2):
                        c = 2 * i + k
                        act.wait_ge(low_made, c + 1)
                        act.activation(ex[:, k], low[:, k], ACT.Exp, scale=HDIM ** -0.5).then_inc(ex_made, 1)
                        act.wait_ge(y_made, c + 3)
                        act.dma_start(d["y_attn"][:, :, bass.ds(c * P, P)].rearrange("b p t -> p b t"), y[:, k]
                                      ).then_inc(stored[k], 16)
                for k in range(2):
                    act.wait_ge(stored[k], 16 * (TILES // 2) + 16)


def branch_stage(nc, w, d):
    HALF, NM = SEQ // 2, DM // P
    branches = [("y_ssm", "p_ssm", 8), ("y_attn", "p_attn", 4), ("y_sc", "p_sc", 4)]
    starts = [0, 8, 12]
    with ExitStack() as stack:
        s = Scope(nc, stack)
        y_raw = s.sb("b_yraw", [P, 2, HALF])
        y_hi, y_lo = s.sb("b_yhi", [P, 16, HALF], F32R), s.sb("b_ylo", [P, 16, HALF], F32R)
        raw = s.sb("b_raw", [P, 16, P])
        w_hi, w_lo = s.sb("b_whi", [P, 2, 16, P], F32R), s.sb("b_wlo", [P, 2, 16, P], F32R)
        gate = s.sb("b_gate", [P, 3, HALF])
        total = s.sb("b_total", [P, 2, HALF])
        part = s.sb("b_part", [P, 2, HALF])
        acc = s.ps("b_acc", [P, 3, HALF])
        y_loaded, gate_loaded, raw_loaded = s.sems("b_y_loaded", 2), s.sems("b_gate_loaded", 3), s.sem("b_raw_loaded")
        y_hi_made, w_hi_made, part_made = s.sem("b_yhi_r"), s.sem("b_whi_r"), s.sem("b_part_r")
        y_made = s.sem("b_y_made")
        w_made = s.sem("b_w_made")
        acc_made = s.sems("b_acc_made", 3)
        acc_taken = s.sems("b_acc_taken", 3)
        total_step, carried = s.sem("b_total_step"), s.sem("b_carried")
        stored = s.sems("b_stored", 2)
        with nc.Block() as block:

            @block.sync
            def _(sp):
                with sp.Fori(0, 2) as h:
                    tokens = bass.ds(h * HALF, HALF)
                    for b, (y, _, n) in enumerate(branches):
                        for c in range(n):
                            j = starts[b] + c
                            sp.wait_ge(y_made, 16 * h + j + 1)
                            sp.dma_start(y_raw[:, j % 2], d[y][c, :, tokens]).then_inc(y_loaded[j % 2], 16)
                    with sp.Fori(0, NM // 2) as i:
                        for k in range(2):
                            m = 2 * i + k
                            for b in range(3):
                                sp.wait_ge(acc_taken[b], NM * h + m + 1)
                                sp.dma_start(gate[:, b], d["gates"][bass.ds(NM * b + m, 1), :, tokens].rearrange(
                                    "o p t -> p (o t)")).then_inc(gate_loaded[b], 16)
                            sp.wait_ge(total_step, 2 * (NM * h + m) + 2)
                            sp.dma_start(d["merged"][bass.ds(m, 1), :, tokens].rearrange("o p t -> p (o t)"),
                                         total[:, k]).then_inc(stored[k], 16)
                for k in range(2):
                    sp.wait_ge(stored[k], 16 * NM + 16)

            @block.gpsimd
            def _(pool):
                pool.sem_inc(w_made, 1)
                with pool.Fori(0, 2) as h:
                    with pool.Fori(0, NM // 2) as i:
                        for k in range(2):
                            m = 2 * i + k
                            u = NM * h + m
                            pool.wait_ge(raw_loaded, 48 * u + 48)
                            wait_alone(pool, acc_made[2], u + 1, carried)
                            pool.tensor_copy(w_hi[:, k], raw[:]).then_inc(w_hi_made, 1)
                            pool.wait_ge(w_hi_made, u + 1)
                            pool.tensor_tensor(w_lo[:, k], raw[:], w_hi[:, k], ALU.subtract).then_inc(w_made, 1)

            @block.scalar
            def _(act):
                act.sem_inc(stored[0], 16)
                act.sem_inc(stored[1], 16)

                def load_weights(m, u):
                    act.wait_ge(w_made, u + 1)
                    for b, (_, p, n) in enumerate(branches):
                        act.dma_start(raw[:, starts[b]:starts[b] + n], w[p][0, :, bass.ds(m * P, P)].rearrange(
                            "(c p) n -> p c n", p=P)).then_inc(raw_loaded, 16)

                with act.Fori(0, 2) as h:
                    for j in range(16):
                        act.wait_ge(y_loaded[j % 2], 128 * h + 16 * (j // 2) + 16)
                        if j in (0, 8, 12):
                            act.wait_ge(acc_made[starts.index(j)], NM * h + 2)
                        act.activation(y_hi[:, j], y_raw[:, j % 2], ACT.Copy).then_inc(y_hi_made, 1)
                    with act.Fori(0, NM // 2) as i:
                        for k in range(2):
                            m = 2 * i + k
                            load_weights(m, NM * h + m)

            @block.tensor
            def _(pe):
                for b in range(3):
                    pe.sem_inc(acc_made[b], 2)
                with pe.Fori(0, 2) as h:
                    with pe.Fori(0, NM // 2) as i:
                        for k in range(2):
                            u = NM * h + 2 * i + k
                            pe.wait_ge(w_made, u + 2)
                            for b, (_, _, n) in enumerate(branches):
                                pe.wait_ge(y_made, 16 * h + starts[b] + n + 2)
                                pe.wait_ge(acc_taken[b], u + 1)
                                for t in range(2):
                                    span = slice(t * BANK, (t + 1) * BANK)
                                    for c in range(starts[b], starts[b] + n):
                                        to = acc[:, b, span]
                                        pe.matmul(to, w_hi[:, k, c], y_hi[:, c, span], start=c == starts[b], stop=False)
                                        pe.matmul(to, w_hi[:, k, c], y_lo[:, c, span], start=False, stop=False)
                                        last = pe.matmul(to, w_lo[:, k, c], y_hi[:, c, span], start=False,
                                                         stop=c == starts[b] + n - 1)
                                last.then_inc(acc_made[b], 1)

            @block.vector
            def _(dve):
                dve.sem_inc(y_made, 2)
                for b in range(3):
                    dve.sem_inc(acc_taken[b], 1)
                with dve.Fori(0, 2) as h:
                    for j in range(16):
                        dve.wait_ge(y_hi_made, 16 * h + j + 1)
                        dve.tensor_tensor(y_lo[:, j], y_raw[:, j % 2], y_hi[:, j], ALU.subtract).then_inc(y_made, 1)
                    with dve.Fori(0, NM // 2) as i:
                        for k in range(2):
                            u = NM * h + 2 * i + k
                            dve.wait_ge(stored[k], 64 * h + 16 * i + 16)
                            for b in range(3):
                                dve.wait_ge(acc_made[b], u + 3)
                                dve.wait_ge(gate_loaded[b], 16 * u + 16)
                                to = total[:, k] if b == 0 else part[:, b - 1]
                                if b == 2:
                                    dve.wait_ge(total_step, 2 * u + 1)
                                dve.tensor_tensor(to, acc[:, b], gate[:, b], ALU.mult).then_inc(acc_taken[b], 1)
                                dve.wait_ge(acc_taken[b], u + 2)
                                if b:
                                    dve.tensor_tensor(total[:, k], total[:, k], part[:, b - 1], ALU.add
                                                      ).then_inc(total_step, 1)


def output_stage(nc, w, d, out, eps):
    with ExitStack() as stack:
        s = Scope(nc, stack)
        w_raw = s.sb("o_wraw", [P, 2, DM])
        w_hi, w_lo = s.sb("o_whi", [P, KC, DM], F32R), s.sb("o_wlo", [P, KC, DM], F32R)
        m_raw = s.sb("o_mraw", [P, 2, KC, P])
        m_hi, m_lo = s.sb("o_mhi", [P, 2, KC, P], F32R), s.sb("o_mlo", [P, 2, KC, P], F32R)
        x_sb = s.sb("o_x", [P, 2, DM])
        w_post = s.sb("o_wpost", [P, DM])
        sq = s.sb("o_sq", [P, 2, DM])
        ss, std, rstd = (s.sb(n, [P, 2]) for n in ("o_ss", "o_std", "o_rstd"))
        y = s.sb("o_y", [P, 2, DM])
        acc = s.ps("o_acc", [P, 2, DM])
        w_loaded, post_loaded = s.sems("o_w_loaded", 2), s.sem("o_post_loaded")
        m_loaded, x_loaded = s.sems("o_m_loaded", 2), s.sems("o_x_loaded", 2)
        w_hi_made, w_made = s.sem("o_whi_r"), s.sem("o_w_made")
        m_hi_made, squared, std_made, rstd_made = (s.sem("o_" + n) for n in ("mhi_r", "sq_r", "std_r", "rstd_r"))
        m_made = s.sem("o_m_made")
        acc_made = s.sem("o_acc_made")
        acc_taken = s.sem("o_acc_taken")
        y_made = s.sem("o_y_made")
        y_free = s.sem("o_y_free")
        stored = s.sems("o_stored", 2)
        with nc.Block() as block:

            @block.sync
            def _(sp):
                sp.dma_start(w_post[:], w["norm_post"][0:1, :].to_broadcast([P, DM])).then_inc(post_loaded, 16)
                for c in range(KC):
                    sp.wait_ge(w_made, c + 1)
                    sp.dma_start(w_raw[:, c % 2], w["w_out"][0, c * P:(c + 1) * P, :]).then_inc(w_loaded[c % 2], 16)
                with sp.Fori(0, TILES // 2) as i:
                    for k in range(2):
                        c = 2 * i + k
                        sp.wait_ge(m_made, c + 1)
                        sp.dma_start(m_raw[:, k], d["merged"][:, :, bass.ds(c * P, P)].rearrange("b p t -> p b t")
                                     ).then_inc(m_loaded[k], 16)
                        sp.wait_ge(y_made, c + 1)
                        sp.dma_start(x_sb[:, k], w["x"][0, bass.ds(c * P, P), :]).then_inc(x_loaded[k], 16)

            @block.scalar
            def _(act):
                for c in range(KC):
                    act.wait_ge(w_loaded[c % 2], 16 * (c // 2) + 16)
                    act.activation(w_hi[:, c], w_raw[:, c % 2], ACT.Copy).then_inc(w_hi_made, 1)

                def finish(k, c, use):
                    act.wait_ge(acc_made, c + 3)
                    act.activation(sq[:, k], acc[:, k], ACT.Square, accum_out=ss[:, k:k + 1]).then_inc(squared, 1)
                    act.wait_ge(squared, c + 1)
                    act.activation(std[:, k:k + 1], ss[:, k:k + 1], ACT.Sqrt, bias=eps[:], scale=1.0 / DM
                                   ).then_inc(std_made, 1)

                with act.Fori(0, TILES // 2) as i:
                    for k in range(2):
                        c = 2 * i + k
                        act.wait_ge(m_loaded[k], 16 * i + 16)
                        act.wait_ge(acc_made, c + 1)
                        act.activation(m_hi[:, k], m_raw[:, k], ACT.Copy).then_inc(m_hi_made, 1)
                        finish(k, c, i)

            @block.gpsimd
            def _(pool):
                pool.sem_inc(y_free, 2)
                with pool.Fori(0, TILES // 2) as i:
                    for k in range(2):
                        c = 2 * i + k
                        pool.wait_ge(y_made, c + 3)
                        pool.dma_start(out[0, bass.ds(c * P, P), :], y[:, k]).then_inc(stored[k], 16)
                        pool.wait_ge(stored[k], 16 * i + 16)
                        pool.sem_inc(y_free, 1)

            @block.tensor
            def _(pe):
                pe.sem_inc(acc_made, 2)
                pe.wait_ge(w_made, KC + 2)
                with pe.Fori(0, TILES // 2) as i:
                    for k in range(2):
                        c = 2 * i + k
                        pe.wait_ge(m_made, c + 3)
                        pe.wait_ge(acc_taken, c + 1)
                        for t in range(2):
                            span = slice(t * BANK, (t + 1) * BANK)
                            for b in range(KC):
                                to = acc[:, k, span]
                                pe.matmul(to, m_hi[:, k, b], w_hi[:, b, span], start=b == 0, stop=False)
                                pe.matmul(to, m_hi[:, k, b], w_lo[:, b, span], start=False, stop=False)
                                last = pe.matmul(to, m_lo[:, k, b], w_hi[:, b, span], start=False, stop=b == KC - 1)
                        last.then_inc(acc_made, 1)

            @block.vector
            def _(dve):
                dve.sem_inc(w_made, 2)
                dve.sem_inc(m_made, 2)
                dve.sem_inc(acc_taken, 2)
                dve.sem_inc(y_made, 2)
                for c in range(KC):
                    dve.wait_ge(w_hi_made, c + 1)
                    dve.tensor_tensor(w_lo[:, c], w_raw[:, c % 2], w_hi[:, c], ALU.subtract).then_inc(w_made, 1)
                dve.wait_ge(post_loaded, 16)
                with dve.Fori(0, TILES // 2) as i:
                    for k in range(2):
                        c = 2 * i + k
                        dve.wait_ge(m_hi_made, c + 1)
                        dve.tensor_tensor(m_lo[:, k], m_raw[:, k], m_hi[:, k], ALU.subtract).then_inc(m_made, 1)
                        dve.wait_ge(std_made, c + 1)
                        dve.reciprocal(rstd[:, k:k + 1], std[:, k:k + 1]).then_inc(rstd_made, 1)
                        dve.wait_ge(rstd_made, c + 1)
                        dve.wait_ge(y_free, c + 1)
                        dve.scalar_tensor_tensor(y[:, k], acc[:, k], rstd[:, k:k + 1], w_post[:], ALU.mult, ALU.mult
                                                 ).then_inc(acc_taken, 1)
                        dve.wait_ge(acc_taken, c + 3)
                        dve.wait_ge(x_loaded[k], 16 * i + 16)
                        dve.tensor_tensor(y[:, k], y[:, k], x_sb[:, k], ALU.add).then_inc(y_made, 1)


def build(nc, w, out, stages=("norm", "proj", "ssd", "attn", "merge", "out"), given=()):
    def scratch(name, shape):
        kind = "ExternalInput" if name in given else "Internal"
        return nc.dram_tensor(name, shape, F32, kind=kind).ap()

    d = {"dt": scratch("s_dt", [P, SEQ]), "z": scratch("s_z", [SSM // P, P, SEQ]),
         "xbc": scratch("s_xbc", [16, P, SEQ]), "qkv": scratch("s_qkv", [20, P, SEQ]),
         "g": scratch("s_g", [4, P, SEQ]), "y_sc": scratch("s_ysc", [4, P, SEQ]),
         "gates": scratch("s_gates", [24, P, SEQ]), "y_ssm": scratch("s_yssm", [8, P, SEQ]),
         "att": scratch("s_att", [3, SEQ, SLOTS // 2, 2 * (HDIM + 2)]),
         "y_attn": scratch("s_yattn", [4, P, SEQ]), "merged": scratch("s_merged", [8, P, SEQ])}
    with ExitStack() as stack:
        s = Scope(nc, stack)
        ident = s.sb("ident", [P, P])
        eps = s.sb("eps", [P, 1])
        with ExitStack() as inner:
            h = Scope(nc, inner)
            h_hi = h.sb("h_hi", [P, KC, SEQ], F32R)
            h_lo = h.sb("h_lo", [P, KC, SEQ], F32R)
            if "norm" in stages:
                norm_stage(nc, w, h_hi, h_lo, ident, eps)
            if "proj" in stages:
                projection_stage(nc, w, d, h_hi, h_lo)
        if "ssd" in stages:
            ssd_stage(nc, w, d, ident, eps)
        if "attn" in stages:
            attention_stage(nc, w, d, ident)
            attention_merge_stage(nc, d, ident)
        if "merge" in stages:
            branch_stage(nc, w, d)
        if "out" in stages:
            output_stage(nc, w, d, out, eps)


INS = ("x", "norm_pre", "norm_post", "w_in", "ssm_conv_w", "ssm_conv_b", "dt_bias", "a_log", "d_skip", "ssm_norm",
       "sc_conv_w", "p_ssm", "p_attn", "p_sc", "w_out")


def kernel(**inputs):
    import numpy as np
    import concourse.bacc as bacc
    from concourse.bass_utils import run_bass_kernel_spmd

    nc = bacc.Bacc("TRN2", target_bir_lowering=False, num_devices=1)
    arrays = {name: np.ascontiguousarray(inputs[name]) for name in INS}
    w = {name: nc.dram_tensor(name, a.shape, F32, kind="ExternalInput").ap() for name, a in arrays.items()}
    out = nc.dram_tensor("out", (1, SEQ, DM), F32, kind="ExternalOutput").ap()
    build(nc, w, out)
    return run_bass_kernel_spmd(nc, [arrays], core_ids=[0]).results[0]["out"]
```

```python
from contextlib import ExitStack

import concourse.bass as bass
from concourse import mybir

F32 = mybir.dt.float32
F32R = mybir.dt.float32r
ALU = mybir.AluOpType
ACT = mybir.ActivationFunctionType

P = 128
SEQ, DM = 2048, 1024
KC = DM // P
TILES = SEQ // P
BANK = 512
SPANS = SEQ // BANK
HEADS, HDIM, GROUPS, STATE = 16, 64, 4, 128
SSM = HEADS * HDIM
GW = SSM // GROUPS
SLOTS, PATTERNS = 8, ((128, 1), (512, 4), (2048, 16))
KV = SLOTS * HDIM
SC = 512
EPS = 1e-6
NEG = -1e30

C_Z = 0
C_XBC = C_Z + SSM
C_DT = C_XBC + SSM + 2 * GROUPS * STATE
C_Q = C_DT + HEADS
C_G = C_Q + 3 * KV + 2 * KV
C_U = C_G + KV
C_B, C_C, C_GSC = C_U + SC, C_U + 2 * SC, C_U + 3 * SC
C_MERGE = C_U + 4 * SC
IN_W = C_MERGE + 3 * DM


class Scope:

    def __init__(self, nc, stack):
        self.nc, self.stack = nc, stack
        self.cleared = []

    def sb(self, name, shape, dt=F32):
        return self.stack.enter_context(self.nc.sbuf_tensor(name, shape, dt))

    def ps(self, name, shape, dt=F32):
        return self.stack.enter_context(self.nc.psum_tensor(name, shape, dt))

    def sem(self, name):
        return self.stack.enter_context(self.nc.semaphore(name))

    def cleared_sem(self, name):
        self.cleared.append(self.nc.alloc_semaphore(name=name))
        return self.cleared[-1]

    def clear(self):
        self.nc.clear_and_free_semaphores(self.cleared)
        self.nc.all_engine_barrier()

    def sems(self, name, n):
        return [self.sem(f"{name}{i}") for i in range(n)]


def wait_alone(eng, sem, value, carrier):
    eng.wait_ge(sem, value)
    eng.sem_inc(carrier, 1)


def projection_stage(nc, w, d, h_hi, h_lo, ident, eps):
    pairs = {"z": SSM // P // 2, "xbc": (C_DT - C_XBC) // P // 2, "q0": KV // P // 2, "q1": KV // P // 2,
             "q2": KV // P // 2, "kv": 2 * KV // P // 2, "g": KV // P // 2,
             "sc": 4 * SC // P // 2, "merge": 3 * DM // P // 2}
    base, n_pairs = {}, 0
    for kind, n in pairs.items():
        base[kind] = n_pairs
        n_pairs += n
    with ExitStack() as stack:
        s = Scope(nc, stack)
        cleared, cleared_sems = s.cleared_sem, lambda name, n: [s.cleared_sem(f"{name}{i}") for i in range(n)]
        raw = s.sb("p_raw", [P, 2, KC, P])
        w_hi = s.sb("p_whi", [P, 2, KC, P], F32R)
        w_lo = s.sb("p_wlo", [P, 2, KC, P], F32R)
        stage = s.sb("p_stage", [P, 2, SEQ])
        work = s.sb("p_work", [P, 2, SEQ])
        cw = s.sb("p_cw", [P, 16, 4])
        cb = s.sb("p_cb", [P, 16])
        scw = s.sb("p_scw", [P, 4, 3])
        w_pre, sq = s.sb("n_wpre", [P, DM]), s.sb("n_sq", [P, 2, DM])
        ssum, std, rstd = (s.sb(n, [P, 4]) for n in ("n_ssum", "n_std", "n_rstd"))
        acc = s.ps("p_acc", [P, 2, SEQ])
        x_sb = stage[:].rearrange("p a (b n) -> p (a b) n", n=DM)
        x_scaled, h_tok = (work[:, k].rearrange("p (b n) -> p b n", n=DM) for k in range(2))
        tr = acc[:, 1].rearrange("p (b n) -> p b n", n=DM)
        x_loaded, pre_loaded = cleared_sems("n_x_loaded", 4), cleared("n_pre_loaded")
        summed, std_made, rstd_made, hi_made, id_zero, id_ready, eps_ready = (
            cleared("n_" + n) for n in ("summed", "std_r", "rstd_r", "hi_r", "id_zero", "id_ready", "eps_ready"))
        scaled = cleared("n_scaled")
        h_made = cleared("n_h_made")
        tr_made = cleared("n_tr_made")
        lo_made = cleared("n_lo_made")
        raw_loaded = cleared_sems("p_raw_loaded", 2)
        consts_loaded = cleared("p_consts_loaded")
        hi_ready = cleared("p_hi_ready")
        carried_v = cleared("p_carried_v")
        carried = cleared("p_carried")
        w_made = cleared_sems("p_w_made", 2)
        acc_made = cleared_sems("p_acc_made", 2)
        acc_taken = cleared_sems("p_acc_taken", 2)
        stored = cleared_sems("p_stored", 2)
        conv_step = cleared("p_conv_step")
        q_hi_made = cleared("p_q_hi_r")
        hi_stored, lo_stored = cleared_sems("p_hi_stored", 2), cleared_sems("p_lo_stored", 2)
        conv_taken = cleared("p_conv_taken")
        sc_step = cleared("p_sc_step")
        sc_done = cleared("p_sc_done")
        with nc.Block() as block:

            @block.sync
            def _(sp):
                def load(slot, use, col):
                    sp.wait_ge(w_made[slot], use + 1)
                    sp.dma_start(raw[:, slot], w["w_in"][0, :, bass.ds(col, P)].rearrange("(c p) n -> p c n", p=P)
                                 ).then_inc(raw_loaded[slot], 16)

                sp.wait_ge(scaled, 4)
                for k in range(2):
                    sp.dma_start(x_sb[:, k], w["x"][0, k * P:(k + 1) * P, :]).then_inc(x_loaded[k], 16)
                load(0, 0, C_DT)
                sp.dma_start(w_pre[:], w["norm_pre"][0:1, :].to_broadcast([P, DM])).then_inc(pre_loaded, 16)
                for k in range(2, 4):
                    sp.dma_start(x_sb[:, k], w["x"][0, k * P:(k + 1) * P, :]).then_inc(x_loaded[k], 16)
                with sp.Fori(0, TILES // 4 - 1) as i:
                    for k in range(4):
                        n = 4 * i + 4 + k
                        sp.wait_ge(scaled, n + 1)
                        sp.dma_start(x_sb[:, k], w["x"][0, bass.ds(n * P, P), :]).then_inc(x_loaded[k], 16)
                with nc.allow_non_contiguous_dma(reason="per-channel taps, once"):
                    for t in range(4):
                        sp.dma_start(cw[:, :, t:t + 1], w["ssm_conv_w"][0, t, :].rearrange("(b p o) -> p b o", p=P, o=1)
                                     ).then_inc(consts_loaded, 16)
                    sp.dma_start(cb[:], w["ssm_conv_b"][0, :].rearrange("(b p) -> p b", p=P)
                                 ).then_inc(consts_loaded, 16)
                    for t in range(3):
                        sp.dma_start(scw[:, :, t:t + 1], w["sc_conv_w"][0, t, :].rearrange("(b p o) -> p b o", p=P, o=1)
                                     ).then_inc(consts_loaded, 16)

                def run(kind, col, step=P):
                    with sp.Fori(0, pairs[kind]) as i:
                        load(1, base[kind] + i, col + 2 * P * i)
                        load(0, base[kind] + i + 1, col + 2 * P * i + P)

                run("z", C_Z)
                run("xbc", C_XBC)
                for g in range(3):
                    run(f"q{g}", C_Q + g * KV)
                run("kv", C_Q + 3 * KV)
                run("g", C_G)
                with sp.Fori(0, SC // P) as f:
                    load(1, base["sc"] + 2 * f, C_U + P * f)
                    load(0, base["sc"] + 2 * f + 1, C_C + P * f)
                    load(1, base["sc"] + 2 * f + 1, C_B + P * f)
                    load(0, base["sc"] + 2 * f + 2, C_GSC + P * f)
                run("merge", C_MERGE)

            @block.gpsimd
            def _(pool):
                for k in range(2):
                    pool.sem_inc(w_made[k], 1)
                pool.sem_inc(h_made, 2)
                pool.memset(eps[:], EPS).then_inc(eps_ready, 1)
                pool.memset(ident[:], 0.0).then_inc(id_zero, 1)
                pool.wait_ge(id_zero, 1)
                pool.affine_select(out=ident[:], in_=ident[:], compare_op=ALU.not_equal, fill=1.0, base=0,
                                   pattern=[[-1, P]], channel_multiplier=1).then_inc(id_ready, 1)

                def split(slot, use, n):
                    pool.wait_ge(raw_loaded[slot], 16 * use + 16)
                    wait_alone(pool, acc_made[slot], use + 1, carried)
                    pool.tensor_copy(w_hi[:, slot], raw[:, slot]).then_inc(hi_ready, 1)
                    pool.wait_ge(hi_ready, n + 1)
                    pool.tensor_tensor(w_lo[:, slot], raw[:, slot], w_hi[:, slot], ALU.subtract
                                       ).then_inc(w_made[slot], 1)

                split(0, 0, 0)
                pool.wait_ge(pre_loaded, 16)
                with pool.Fori(0, TILES // 2) as i:
                    for k in range(2):
                        n = 2 * i + k
                        pool.wait_ge(scaled, n + 5)
                        pool.wait_ge(tr_made, n + 1)
                        pool.tensor_tensor(h_tok[:, k], x_scaled[:, k], w_pre[:], ALU.mult).then_inc(h_made, 1)
                with pool.Fori(0, n_pairs) as i:
                    split(1, i, 2 * i + 1)
                    split(0, i + 1, 2 * i + 2)

            @block.tensor
            def _(pe):
                for k in range(2):
                    pe.sem_inc(acc_made[k], 1)
                pe.sem_inc(tr_made, 2)
                pe.wait_ge(id_ready, 1)

                def transposes(n):
                    pe.wait_ge(h_made, n + 3)
                    pe.wait_ge(lo_made, n + 1)
                    for c in range(KC):
                        last = pe.transpose(tr[:, n % 2, c * P:(c + 1) * P], h_tok[:, n % 2, c * P:(c + 1) * P], ident[:])
                    last.then_inc(tr_made, 1)

                def product(slot, use, first=False):
                    if not first:
                        pe.wait_ge(w_made[slot], use + 2)
                        pe.wait_ge(acc_taken[slot], use + 1)
                    for t in range(SPANS):
                        span = slice(t * BANK, (t + 1) * BANK)
                        if first:
                            for n in range(4 * t + (1 if t else 0), min(4 * t + 5, TILES)):
                                transposes(n)
                            if t == 0:
                                pe.wait_ge(w_made[slot], 2)
                                pe.wait_ge(acc_taken[slot], 1)
                            pe.wait_ge(lo_made, 4 * t + 6)
                        for c in range(KC):
                            pe.matmul(acc[:, slot, span], w_hi[:, slot, c], h_hi[:, c, span], start=c == 0, stop=False)
                            pe.matmul(acc[:, slot, span], w_hi[:, slot, c], h_lo[:, c, span], start=False, stop=False)
                            last = pe.matmul(acc[:, slot, span], w_lo[:, slot, c], h_hi[:, c, span], start=False,
                                             stop=c == KC - 1)
                    last.then_inc(acc_made[slot], 1)

                product(0, 0, first=True)
                with pe.Fori(0, n_pairs) as i:
                    product(1, i)
                    product(0, i + 1)

            @block.scalar
            def _(act):
                act.sem_inc(stored[0], 16)
                act.sem_inc(stored[1], 16)
                act.sem_inc(acc_taken[0], 1)
                act.sem_inc(acc_taken[1], 1)
                act.sem_inc(conv_taken, 2)
                act.sem_inc(scaled, 4)
                act.wait_ge(eps_ready, 1)

                def scale(n, k):
                    at = slice(k, k + 1)
                    act.wait_ge(summed, n + 1)
                    act.activation(std[:, at], ssum[:, at], ACT.Sqrt, bias=eps[:], scale=1.0 / DM).then_inc(std_made, 1)
                    act.wait_ge(rstd_made, n + 1)
                    act.wait_ge(h_made, n + 1)
                    act.activation(x_scaled[:, k % 2], x_sb[:, k], ACT.Identity, scale=rstd[:, at]).then_inc(scaled, 1)

                def take_hi(n, k):
                    act.wait_ge(tr_made, n + 3)
                    act.activation(h_hi[:, :, bass.ds(n * P, P)], tr[:, k % 2].rearrange("p (c t) -> p c t", c=KC),
                                   ACT.Copy).then_inc(hi_made, 1)

                scale(0, 0)
                scale(1, 1)
                with act.Fori(0, TILES // 4 - 1) as i:
                    for k in range(4):
                        scale(4 * i + 2 + k, (k + 2) % 4)
                        take_hi(4 * i + k, k)
                for n in range(TILES - 2, TILES):
                    scale(n, n % 4)
                    take_hi(n - 2, n % 4)
                for n in range(TILES - 2, TILES):
                    take_hi(n, n % 4)
                for k in range(2):
                    act.sem_inc(hi_stored[k], 32)
                    act.sem_inc(lo_stored[k], 32)

                def put(slot, use, func, out):
                    act.wait_ge(acc_made[slot], use + 2)
                    act.wait_ge(stored[slot], 16 * use + 16)
                    act.activation(stage[:, slot], acc[:, slot], func).then_inc(acc_taken[slot], 1)
                    act.wait_ge(acc_taken[slot], use + 2)
                    act.dma_start(out, stage[:, slot]).then_inc(stored[slot], 16)

                def run(kind, func, dest):
                    with act.Fori(0, pairs[kind]) as i:
                        put(1, base[kind] + i, func, dest[bass.ds(2 * i, 1)].rearrange("o p t -> p (o t)"))
                        put(0, base[kind] + i + 1, func, dest[bass.ds(2 * i + 1, 1)].rearrange("o p t -> p (o t)"))

                put(0, 0, ACT.Copy, d["dt"])
                run("z", ACT.Silu, d["z"])
                with act.Fori(0, pairs["xbc"]) as i:
                    for k in range(2):
                        slot, use = 1 - k, base["xbc"] + i + k
                        act.wait_ge(acc_taken[slot], use + 2)
                        act.wait_ge(stored[slot], 16 * use + 16)
                        act.activation(stage[:, slot], work[:, k], ACT.Silu).then_inc(conv_taken, 1)
                        act.wait_ge(conv_taken, 2 * i + k + 3)
                        act.dma_start(d["xbc"][bass.ds(2 * i + k, 1)].rearrange("o p t -> p (o t)"), stage[:, slot]
                                      ).then_inc(stored[slot], 16)
                for g, (_, r) in enumerate(PATTERNS):
                    with act.Fori(0, pairs["q0"]) as i:
                        for k in range(2):
                            slot, use, n = 1 - k, base[f"q{g}"] + i + k, 2 * g + i
                            to = d["qs"][bass.ds(4 * g + 2 * i + k, 1)]
                            act.wait_ge(acc_made[slot], use + 2)
                            if g == 0:
                                act.wait_ge(stored[slot], 16 * (base["q0"] + k) + 16)
                            act.wait_ge(hi_stored[slot], 32 * n + 32)
                            act.activation(stage[:, slot].bitcast(F32R).rearrange("p (r m) -> p r m", r=r),
                                           acc[:, slot].rearrange("p (m r) -> p r m", r=r), ACT.Copy
                                           ).then_inc(q_hi_made, 1)
                            act.wait_ge(q_hi_made, 2 * n + k + 1)
                            for sl in range(2):
                                act.dma_start(to[0, sl, :HDIM], stage[sl * HDIM:(sl + 1) * HDIM, slot]
                                              ).then_inc(hi_stored[slot], 16)
                            act.wait_ge(acc_taken[slot], use + 2)
                            for sl in range(2):
                                act.dma_start(to[0, sl, HDIM:], work[sl * HDIM:(sl + 1) * HDIM, slot]
                                              ).then_inc(lo_stored[slot], 16)
                for k in range(2):
                    act.wait_ge(hi_stored[k], 32 * 7)
                    act.sem_inc(stored[k], 16 * 6)
                run("kv", ACT.Copy, d["kv"])
                run("g", ACT.Silu, d["g"])
                with act.Fori(0, SC // P) as f:
                    use = base["sc"] + 2 * f
                    act.wait_ge(acc_made[1], use + 2)
                    for k in range(2):
                        act.wait_ge(lo_stored[k], 32 * 7)
                    act.wait_ge(sc_done, f + 1)
                    act.activation(work[:, 0], acc[:, 1], ACT.Copy).then_inc(acc_taken[1], 1)
                    act.wait_ge(acc_made[0], use + 4)
                    act.wait_ge(stored[1], 16 * use + 16)
                    act.activation(stage[:, 1], acc[:, 0], ACT.Silu).then_inc(acc_taken[0], 1)
                    act.wait_ge(sc_done, f + 2)
                    act.sem_inc(stored[0], 32)
                    act.sem_inc(stored[1], 16)
                    act.dma_start(d["y_sc"][bass.ds(f, 1)].rearrange("o p t -> p (o t)"), stage[:, 1]
                                  ).then_inc(stored[1], 16)
                run("merge", ACT.Sigmoid, d["gates"])
                act.wait_ge(stored[0], 16 * (n_pairs + 2))
                act.wait_ge(stored[1], 16 * (n_pairs + 1))

            @block.vector
            def _(dve):
                dve.sem_inc(sc_done, 1)
                dve.sem_inc(lo_made, 2)

                def squares(n, k, use):
                    wait_alone(dve, x_loaded[k], 16 * use + 16, carried_v)
                    dve.tensor_tensor_reduce(out=sq[:, k % 2], in0=x_sb[:, k], in1=x_sb[:, k], scale=1.0, scalar=0.0,
                                             op0=ALU.mult, op1=ALU.add, accum_out=ssum[:, k:k + 1]).then_inc(summed, 1)

                def invert(n, k):
                    at = slice(k, k + 1)
                    dve.wait_ge(std_made, n + 1)
                    dve.reciprocal(rstd[:, at], std[:, at]).then_inc(rstd_made, 1)

                def take_lo(n, k):
                    at = bass.ds(n * P, P)
                    dve.wait_ge(hi_made, n + 1)
                    dve.tensor_tensor(h_lo[:, :, at], tr[:, k % 2].rearrange("p (c t) -> p c t", c=KC), h_hi[:, :, at],
                                      ALU.subtract).then_inc(lo_made, 1)

                squares(0, 0, 0)
                for n in range(2):
                    squares(n + 1, n + 1, 0)
                    invert(n, n)
                squares(3, 3, 0)
                invert(2, 2)
                take_lo(0, 0)
                with dve.Fori(0, TILES // 4 - 1) as i:
                    for k in range(4):
                        squares(4 * i + 4 + k, k, i + 1)
                        invert(4 * i + 3 + k, (3 + k) % 4)
                        take_lo(4 * i + 1 + k, (k + 1) % 4)
                invert(TILES - 1, 3)
                for n in range(TILES - 3, TILES):
                    take_lo(n, n % 4)
                dve.wait_ge(consts_loaded, 16 * 8)
                with dve.Fori(0, pairs["xbc"]) as i:
                    for k in range(2):
                        slot, use, b = 1 - k, base["xbc"] + i + k, 2 * i + k
                        n = 4 * b
                        dve.wait_ge(acc_made[slot], use + 2)
                        dve.wait_ge(conv_taken, b + 1)
                        dve.tensor_scalar(work[:, k], acc[:, slot], cw[:, bass.ds(b, 1), 3].rearrange("p o -> p o"),
                                          cb[:, bass.ds(b, 1)], ALU.mult, ALU.add).then_inc(conv_step, 1)
                        for tap in range(3):
                            back = 3 - tap
                            dve.wait_ge(conv_step, 3 * b + tap + 1)
                            ins = dve.scalar_tensor_tensor(work[:, k, back:], acc[:, slot, :SEQ - back],
                                                           cw[:, bass.ds(b, 1), tap], work[:, k, back:], ALU.mult,
                                                           ALU.add)
                            ins.then_inc(conv_step if tap < 2 else acc_taken[slot], 1)
                for g, (_, r) in enumerate(PATTERNS):
                    with dve.Fori(0, pairs["q0"]) as i:
                        for k in range(2):
                            slot, use, n = 1 - k, base[f"q{g}"] + i + k, 2 * g + i
                            if g == 0:
                                dve.wait_ge(conv_taken, 2 * 2 * pairs["xbc"] // 2 + 2)
                            dve.wait_ge(lo_stored[slot], 32 * n + 32)
                            dve.wait_ge(q_hi_made, 2 * n + k + 1)
                            dve.tensor_tensor(work[:, slot].bitcast(F32R).rearrange("p (r m) -> p r m", r=r),
                                              acc[:, slot].rearrange("p (m r) -> p r m", r=r),
                                              stage[:, slot].rearrange("p (r m) -> p r m", r=r), ALU.subtract
                                              ).then_inc(acc_taken[slot], 1)
                with dve.Fori(0, SC // P) as f:
                    use = base["sc"] + 2 * f
                    tap = lambda t: scw[:, bass.ds(f, 1), t]
                    dve.wait_ge(acc_made[0], use + 3)
                    dve.wait_ge(acc_taken[1], use + 2)
                    dve.tensor_tensor(work[:, 1], acc[:, 0], work[:, 0], ALU.mult).then_inc(acc_taken[0], 1)
                    dve.wait_ge(acc_taken[0], use + 3)
                    dve.tensor_scalar(work[:, 0], work[:, 1], tap(2), None, ALU.mult).then_inc(sc_step, 1)
                    for back in (1, 2):
                        dve.wait_ge(sc_step, 3 * f + back)
                        dve.scalar_tensor_tensor(work[:, 0, back:], work[:, 1, :SEQ - back], tap(2 - back),
                                                 work[:, 0, back:], ALU.mult, ALU.add).then_inc(sc_step, 1)
                    dve.wait_ge(sc_step, 3 * f + 3)
                    dve.wait_ge(acc_made[1], use + 3)
                    dve.tensor_tensor(work[:, 0], acc[:, 1], work[:, 0], ALU.mult).then_inc(acc_taken[1], 1)
                    dve.wait_ge(acc_taken[1], use + 3)
                    dve.wait_ge(acc_taken[0], use + 4)
                    dve.tensor_tensor(stage[:, 1], stage[:, 1], work[:, 0], ALU.mult).then_inc(sc_done, 1)
        s.clear()


def ssd_stage(nc, w, d, ident, eps):
    N = TILES * HEADS
    with ExitStack() as stack:
        s = Scope(nc, stack)
        dt_raw = s.sb("s_dtraw", [HEADS, SEQ])
        bias_b, alog_b, dskip_b = (s.sb(n, [P, HEADS]) for n in ("s_bias", "s_alog", "s_dskip"))
        norm_b = s.sb("s_norm", [P, SSM])
        tri = s.sb("s_tri", [P, P])
        ones = s.sb("s_ones", [P, P])
        t0, t1, t2, t3 = (s.sb(f"s_t{i}", [P, N]) for i in range(4))
        dt, a, cs, ecs, elast, wdec = (s.sb(n, [P, N]) for n in ("s_dtt", "s_a", "s_cs", "s_ecs", "s_elast", "s_wdec"))
        xbc_t = s.sb("s_xbct", [P, 2, 16, P])
        z_t = s.sb("s_zt", [P, 2, KC, P])
        x_tok = s.sb("s_xtok", [P, 2, SSM])
        b_tok = s.sb("s_btok", [P, 2, GROUPS * STATE])
        cs_now = s.sb("s_csnow", [P, 2, HEADS])
        xdt = s.sb("s_xdt", [P, 2, SSM + HDIM])
        xdec = s.sb("s_xdec", [P, 2, SSM])
        xd = s.sb("s_xd", [P, 2, SSM])
        cbm = s.sb("s_cbm", [P, GROUPS, P])
        fall = s.sb("s_fall", [P, 2, 4, P])
        decay = s.sb("s_decay", [P, 2, 4, P])
        mix = s.sb("s_mix", [P, 2, 4, P])
        state = s.sb("s_state", [P, SSM])
        sdec = s.sb("s_sdec", [P, SSM])
        y = s.sb("s_y", [P, SSM])
        yg = s.sb("s_yg", [P, TILES, SSM])
        sq = s.sb("s_sq", [P, 2, SSM])
        ss = s.sb("s_ss", [P, TILES * GROUPS])
        rstd = s.sb("s_rstd", [P, TILES * GROUPS])
        yn = s.sb("s_yn", [P, 2, SSM])
        y_out = s.sb("s_yout", [P, 2, KC, P])
        ps_x = s.ps("s_psx", [P, SSM])
        ps_m = s.ps("s_psm", [P, SSM])
        ps_bc = s.ps("s_psbc", [P, 2, BANK])
        ps_y = s.ps("s_psy", [P, 2, 2, GW])
        consts_loaded, turn = s.sem("s_consts_loaded"), s.sem("s_turn")
        loaded = s.sems("s_loaded", 2)
        x_transposed, b_transposed, cb_ready, z_transposed = (
            s.sem(n) for n in ("s_xT", "s_bT", "s_cb", "s_zT"))
        x_tok_ready, b_tok_ready, cbm_ready, yo_ready, skip_added, sdec_ready = (
            s.sem(n) for n in ("s_xtok_r", "s_btok_r", "s_cbm_r", "s_yo_r", "s_skip_r", "s_sdec_r"))
        a_ready, xdt_ready, xdec_ready, squared, bc_ready = (
            s.sem(n) for n in ("s_a_r", "s_xdt_r", "s_xdec_r", "s_sq_r", "s_bc_r"))
        y_made = s.sem("s_y_made")
        decay_made = s.sem("s_decay_made")
        fall_made = s.sem("s_fall_made")
        mix_made = s.sem("s_mix_made")
        y_taken = s.sem("s_y_taken")
        update_made = s.sem("s_update_made")
        gated = s.sem("s_gated")
        xd_made = s.sem("s_xd_made")
        state_made = s.sem("s_state_made")
        turn2, carried = s.sem("s_turn2"), s.sem("s_carried")
        yn_made = s.sem("s_yn_made")
        out_taken = s.sem("s_out_taken")
        out_made = s.sem("s_out_made")
        stored = s.sems("s_stored", 2)

        def heads(ap):
            return ap.rearrange("p (h q) -> p h q", q=HDIM)

        def spread(ap, n, width=HDIM):
            return ap.unsqueeze(2).to_broadcast([P, n, width])

        with nc.Block() as block:

            @block.sync
            def _(sp):
                sp.dma_start(dt_raw[:], d["dt"][0:HEADS, :]).then_inc(consts_loaded, 16)
                for to, of in ((bias_b, "dt_bias"), (alog_b, "a_log"), (dskip_b, "d_skip")):
                    sp.dma_start(to[:], w[of][0:1, :].to_broadcast([P, HEADS])).then_inc(consts_loaded, 16)
                sp.dma_start(norm_b[:], w["ssm_norm"][0:1, :].to_broadcast([P, SSM])).then_inc(consts_loaded, 16)
                with sp.Fori(0, TILES // 2) as i:
                    for k in range(2):
                        c = 2 * i + k
                        sp.wait_ge(y_made, 4 * c + 4)
                        at = bass.ds(c * P, P)
                        sp.dma_start(xbc_t[:, k], d["xbc"][:, :, at].rearrange("b p t -> p b t")).then_inc(loaded[k], 16)
                        sp.dma_start(z_t[:, k], d["z"][:, :, at].rearrange("b p t -> p b t")).then_inc(loaded[k], 16)

            @block.gpsimd
            def _(pool):
                pool.sem_inc(xd_made, 2)
                pool.memset(ones[:], 1.0).then_inc(turn, 1)
                pool.wait_ge(turn, 1)
                pool.affine_select(out=tri[:], in_=ones[:], compare_op=ALU.is_ge, fill=0.0, base=0,
                                   pattern=[[1, P]], channel_multiplier=-1).then_inc(turn, 1)
                pool.memset(xdt[:, :, SSM:], 0.0)
                pool.memset(state[:], 0.0).then_inc(state_made, 1)
                pool.wait_ge(turn, 21)
                with pool.Fori(0, TILES // 2) as i:
                    for k in range(2):
                        c = 2 * i + k
                        at = bass.ds(c * HEADS, HEADS)
                        wait_alone(pool, y_made, 4 * c + 4, carried)
                        pool.tensor_copy(cs_now[:, k], cs[:, at]).then_inc(a_ready, 1)
                        pool.wait_ge(x_tok_ready, c + 1)
                        pool.tensor_tensor(heads(xdt[:, k, :SSM]), heads(x_tok[:, k]), spread(dt[:, at], HEADS), ALU.mult
                                           ).then_inc(xdt_ready, 1)
                        pool.wait_ge(update_made, c + 1)
                        pool.tensor_tensor(heads(xdec[:, k]), heads(x_tok[:, k]), spread(wdec[:, at], HEADS), ALU.mult
                                           ).then_inc(xdec_ready, 1)
                        pool.wait_ge(gated, c + 1)
                        pool.tensor_tensor(heads(xd[:, k]), heads(x_tok[:, k]), spread(dskip_b[:], HEADS), ALU.mult
                                           ).then_inc(xd_made, 1)
                        pool.wait_ge(state_made, c + 1)
                        pool.tensor_tensor(heads(sdec[:]), heads(state[:]), spread(elast[:, at], HEADS), ALU.mult
                                           ).then_inc(sdec_ready, 1)

            @block.tensor
            def _(pe):
                pe.sem_inc(y_made, 8)
                pe.sem_inc(update_made, 2)
                pe.wait_ge(consts_loaded, 80)
                pe.wait_ge(turn, 2)
                for c in range(TILES):
                    last = pe.transpose(ps_x[:, c * HEADS:(c + 1) * HEADS], dt_raw[:, c * P:(c + 1) * P],
                                        ident[:HEADS, :HEADS])
                last.then_inc(turn, 1)
                pe.wait_ge(turn, 16)
                pe.matmul(ps_y[:, 0, 0], tri[:], a[:], start=True, stop=True)
                pe.matmul(ps_y[:, 1, 0], ones[:], a[:], start=True, stop=True).then_inc(turn, 1)
                pe.wait_ge(turn, 21)
                with pe.Fori(0, TILES // 2) as i:
                    for k in range(2):
                        c = 2 * i + k
                        b_t, c_t = xbc_t[:, k, 8:12], xbc_t[:, k, 12:16]
                        pe.wait_ge(loaded[k], 32 * i + 32)
                        pe.wait_ge(gated, c + 2)
                        for b in range(KC):
                            last = pe.transpose(ps_x[:, b * P:(b + 1) * P], xbc_t[:, k, b], ident[:])
                        last.then_inc(x_transposed, 1)
                        pe.wait_ge(state_made, c + 1)
                        for g in range(GROUPS):
                            last = pe.transpose(ps_m[:, g * P:(g + 1) * P], b_t[:, g], ident[:])
                        last.then_inc(b_transposed, 1)
                        for g in range(GROUPS):
                            last = pe.matmul(ps_m[:, BANK + g * P:BANK + (g + 1) * P], b_t[:, g], c_t[:, g],
                                             start=True, stop=True)
                        last.then_inc(cb_ready, 1)

                        flat_y = ps_y[:].rearrange("p b a q -> p b (a q)")

                        def running_sums(g):
                            pe.wait_ge(fall_made, 4 * c + g + 1)
                            for j in range(4):
                                h = 4 * g + j
                                last = pe.transpose(ps_bc[:, g % 2, j * P:(j + 1) * P],
                                                    cs_now[:, k, h:h + 1].to_broadcast([P, P]), ident[:])
                            last.then_inc(bc_ready, 1)

                        def group(g):
                            pe.wait_ge(mix_made, 4 * c + g + 3)
                            pe.wait_ge(y_taken, 4 * c + g + 1)
                            for j in range(4):
                                at = slice(j * HDIM, (j + 2) * HDIM)
                                pe.matmul(flat_y[:, g % 2, at], mix[:, g % 2, j], xdt[:, k, g * GW + j * HDIM:
                                          g * GW + (j + 2) * HDIM], start=True, stop=True)
                            pe.matmul(ps_y[:, g % 2, 1], c_t[:, g], state[:, g * GW:(g + 1) * GW], start=True,
                                      stop=True).then_inc(y_made, 1)

                        pe.wait_ge(a_ready, c + 1)
                        running_sums(0)
                        pe.wait_ge(x_tok_ready, c + 1)
                        for b in range(KC):
                            last = pe.transpose(ps_x[:, b * P:(b + 1) * P], z_t[:, k, b], ident[:])
                        last.then_inc(z_transposed, 1)
                        running_sums(1)
                        pe.wait_ge(xdt_ready, c + 1)
                        group(0)
                        running_sums(2)
                        group(1)
                        running_sums(3)
                        group(2)
                        group(3)
                        pe.wait_ge(b_tok_ready, c + 1)
                        pe.wait_ge(xdec_ready, c + 1)
                        pe.wait_ge(cbm_ready, c + 1)
                        for g in range(GROUPS):
                            last = pe.matmul(ps_m[:, g * GW:(g + 1) * GW], b_tok[:, k, g * P:(g + 1) * P],
                                             xdec[:, k, g * GW:(g + 1) * GW], start=True, stop=True)
                        last.then_inc(update_made, 1)
                with pe.Fori(0, TILES // 2) as i:
                    for k in range(2):
                        bank = (ps_x, ps_m)[k]
                        pe.wait_ge(yn_made, 2 * i + k + 3)
                        pe.wait_ge(out_taken, 2 * i + k + 1)
                        for b in range(KC):
                            last = pe.transpose(bank[:, b * P:(b + 1) * P], yn[:, k, b * P:(b + 1) * P], ident[:])
                        last.then_inc(out_made, 1)

            @block.scalar
            def _(act):
                act.sem_inc(decay_made, 2)
                act.sem_inc(squared, 1)
                act.sem_inc(fall_made, 2)
                act.sem_inc(out_taken, 2)
                act.wait_ge(turn, 5)
                act.activation(t1[:], t1[:], ACT.Exp, scale=-1.0).then_inc(turn, 1)
                act.wait_ge(turn, 7)
                act.activation(t3[:], t2[:], ACT.Ln).then_inc(turn, 1)
                act.activation(alog_b[:], alog_b[:], ACT.Exp).then_inc(turn, 1)
                act.wait_ge(turn, 17)
                act.activation(ecs[:], ps_y[:, 0, 0], ACT.Exp).then_inc(turn, 1)
                act.activation(elast[:], ps_y[:, 1, 0], ACT.Exp).then_inc(turn, 1)
                act.wait_ge(turn, 20)
                act.activation(t1[:], t0[:], ACT.Exp).then_inc(turn2, 1)
                with act.Fori(0, TILES // 2) as i:
                    for k in range(2):
                        c = 2 * i + k
                        act.wait_ge(x_transposed, c + 1)
                        act.wait_ge(xd_made, c + 1)
                        act.activation(x_tok[:, k], ps_x[:], ACT.Copy).then_inc(x_tok_ready, 1)
                        act.wait_ge(b_transposed, c + 1)
                        act.wait_ge(update_made, c + 1)
                        act.activation(b_tok[:, k], ps_m[:, :BANK], ACT.Copy).then_inc(b_tok_ready, 1)
                        for g in range(GROUPS):
                            act.wait_ge(bc_ready, 4 * c + g + 1)
                            act.wait_ge(mix_made, 4 * c + g + 1)
                            for j in range(4):
                                last = act.activation(fall[:, g % 2, j], ps_bc[:, g % 2, j * P:(j + 1) * P], ACT.Relu,
                                                      bias=cs[:, bass.ds(c * HEADS + 4 * g + j, 1)], scale=-1.0)
                            last.then_inc(fall_made, 1)
                            act.wait_ge(fall_made, 4 * c + g + 3)
                            act.activation(decay[:, g % 2], fall[:, g % 2], ACT.Exp, scale=-1.0).then_inc(decay_made, 1)
                        if k:
                            act.wait_ge(squared, i + 1)
                            for q in range(2):
                                act.wait_ge(gated, 2 * i + q + 3)
                                for g in range(GROUPS):
                                    last = act.activation(sq[:, q, g * GW:(g + 1) * GW], yg[:, bass.ds(2 * i + q, 1), g * GW:(g + 1) * GW
                                                                    ].rearrange("p o q -> p (o q)"), ACT.Square,
                                                          accum_out=ss[:, bass.ds((2 * i + q) * GROUPS + g, 1)])
                            last.then_inc(squared, 1)
                act.wait_ge(squared, TILES // 2 + 1)
                act.activation(rstd[:], ss[:], ACT.Sqrt, bias=eps[:], scale=1.0 / GW).then_inc(turn2, 1)
                with act.Fori(0, TILES // 2) as i:
                    for k in range(2):
                        c = 2 * i + k
                        act.wait_ge(out_made, c + 1)
                        act.wait_ge(stored[k], 16 * i + 16)
                        act.activation(y_out[:, k], (ps_x, ps_m)[k][:], ACT.Copy).then_inc(out_taken, 1)
                        act.wait_ge(out_taken, c + 3)
                        act.dma_start(d["y_ssm"][:, :, bass.ds(c * P, P)].rearrange("b p t -> p b t"), y_out[:, k]
                                      ).then_inc(stored[k], 16)
                for k in range(2):
                    act.wait_ge(stored[k], 16 * (TILES // 2) + 16)

            @block.vector
            def _(dve):
                dve.sem_inc(mix_made, 2)
                dve.sem_inc(y_taken, 2)
                dve.sem_inc(gated, 2)
                dve.sem_inc(yn_made, 2)
                for k in range(2):
                    dve.sem_inc(stored[k], 16)
                tt, ts, stt = dve.tensor_tensor, dve.tensor_scalar, dve.scalar_tensor_tensor
                chunked = lambda ap: ap.rearrange("p (c h) -> p c h", h=HEADS)
                every = lambda ap: ap.unsqueeze(1).to_broadcast([P, TILES, HEADS])
                dve.wait_ge(turn, 3)
                tt(chunked(t0[:]), chunked(ps_x[:, :N]), every(bias_b[:]), ALU.add).then_inc(turn, 1)
                dve.wait_ge(turn, 4)
                stt(t1[:], t0[:], -1.0, t0[:], ALU.mult, ALU.max).then_inc(turn, 1)
                dve.wait_ge(turn, 6)
                ts(t2[:], t1[:], 1.0, None, ALU.add).then_inc(turn, 1)
                dve.wait_ge(turn, 9)
                ts(t2[:], t2[:], -1.0, None, ALU.add).then_inc(turn, 1)
                dve.wait_ge(turn, 10)
                ts(dt[:], t2[:], 0.0, None, ALU.is_equal).then_inc(turn, 1)
                dve.wait_ge(turn, 11)
                tt(t3[:], t3[:], dt[:], ALU.add)
                tt(t2[:], t2[:], dt[:], ALU.add).then_inc(turn, 1)
                dve.wait_ge(turn, 12)
                dve.reciprocal(t2[:], t2[:])
                tt(t3[:], t3[:], t1[:], ALU.mult).then_inc(turn, 1)
                dve.wait_ge(turn, 13)
                tt(t3[:], t3[:], t2[:], ALU.mult).then_inc(turn, 1)
                dve.wait_ge(turn, 14)
                stt(dt[:], t0[:], 0.0, t3[:], ALU.max, ALU.add).then_inc(turn, 1)
                dve.wait_ge(turn, 15)
                stt(chunked(a[:]), chunked(dt[:]), -1.0, every(alog_b[:]), ALU.mult, ALU.mult).then_inc(turn, 1)
                dve.wait_ge(turn, 19)
                dve.tensor_copy(cs[:], ps_y[:, 0, 0]).then_inc(turn2, 1)
                dve.wait_ge(turn2, 1)
                tt(t0[:], ps_y[:, 1, 0], cs[:], ALU.subtract).then_inc(turn, 1)
                dve.wait_ge(turn2, 2)
                tt(wdec[:], dt[:], t1[:], ALU.mult).then_inc(turn, 1)
                with dve.Fori(0, TILES // 2) as i:
                    for k in range(2):
                        c = 2 * i + k
                        dve.wait_ge(cb_ready, c + 1)
                        tt(cbm[:], ps_m[:, BANK:].rearrange("p (g l) -> p g l", l=P),
                           tri[:].unsqueeze(1).to_broadcast([P, GROUPS, P]), ALU.mult).then_inc(cbm_ready, 1)
                        dve.wait_ge(cbm_ready, c + 1)

                        def combine(g):
                            dve.wait_ge(decay_made, 4 * c + g + 3)
                            dve.wait_ge(y_made, 4 * c + g + 7)
                            tt(mix[:, g % 2], decay[:, g % 2], cbm[:, g].unsqueeze(1).to_broadcast([P, 4, P]),
                               ALU.mult).then_inc(mix_made, 1)

                        def take(g):
                            at = slice(g * GW, (g + 1) * GW)
                            dve.wait_ge(y_made, 4 * c + g + 9)
                            tt(heads(y[:, at]), heads(ps_y[:, g % 2, 1]), spread(ecs[:, bass.ds(c * HEADS + 4 * g, 4)], 4),
                               ALU.mult).then_inc(yo_ready, 1)
                            dve.wait_ge(yo_ready, 4 * c + g + 1)
                            tt(y[:, at], ps_y[:, g % 2, 0], y[:, at], ALU.add).then_inc(y_taken, 1)

                        combine(0)
                        combine(1)
                        take(0)
                        combine(2)
                        take(1)
                        combine(3)
                        take(2)
                        take(3)
                        dve.wait_ge(y_taken, 4 * c + 6)
                        dve.wait_ge(xd_made, c + 3)
                        tt(y[:], y[:], xd[:, k], ALU.add).then_inc(skip_added, 1)
                        dve.wait_ge(skip_added, c + 1)
                        dve.wait_ge(z_transposed, c + 1)
                        tt(yg[:, bass.ds(c, 1)].rearrange("p o q -> p (o q)"), ps_x[:], y[:], ALU.mult).then_inc(gated, 1)
                        dve.wait_ge(sdec_ready, c + 1)
                        dve.wait_ge(update_made, c + 3)
                        tt(state[:], ps_m[:], sdec[:], ALU.add).then_inc(state_made, 1)
                dve.wait_ge(turn2, 3)
                dve.reciprocal(rstd[:], rstd[:]).then_inc(turn2, 1)
                dve.wait_ge(turn2, 4)
                with dve.Fori(0, TILES // 2) as i:
                    for k in range(2):
                        c = 2 * i + k
                        dve.wait_ge(out_taken, c + 1)
                        for g in range(GROUPS):
                            at = slice(g * GW, (g + 1) * GW)
                            last = stt(yn[:, k, at], yg[:, bass.ds(c, 1), at].rearrange("p o q -> p (o q)"),
                                       rstd[:, bass.ds(c * GROUPS + g, 1)], norm_b[:, at], ALU.mult, ALU.mult)
                        last.then_inc(yn_made, 1)


def attention_stage(nc, w, d, ident):
    NB, W, PAIRS = TILES, HDIM + 2, SLOTS // 2
    dil = [x[1] for x in PATTERNS]
    blocks = [[(r, n) for r in range(x) for n in range(SEQ // x // P)] for x in dil]
    steps = [(g, sl, b) for sl in range(2) for g in range(3) for b in range(0, NB, 2)]
    NS, NV = len(steps), 12
    SPAN = NB // 2
    HALF = (NS + NV) // 2
    stores = [1, dil[1], 1]
    with ExitStack() as stack:
        s = Scope(nc, stack)
        q_s = s.sb("a_q", [P, 3, SEQ], F32R)
        k_raw, v_t = s.sb("a_kraw", [P, SEQ]), s.sb("a_v", [P, SEQ])
        k_hi, k_lo = s.sb("a_khi", [P, 3, SEQ], F32R), s.sb("a_klo", [P, 3, SEQ], F32R)
        v_tok = s.sb("a_vt", [P, 3, NB, P])
        band = s.sb("a_band", [P, 2, P])
        zero = s.sb("a_zero", [P, 2, P])
        scores = s.sb("a_scores", [P, 4, 2, 2 * P])
        probs = s.sb("a_probs", [P, 4, 2, 2 * P])
        probs_t = s.sb("a_probst", [P, 4, 4, P])
        neg = s.sb("a_neg", [P, 4, 2])
        att = s.sb("a_att", [P, 3, NB, 2, W])
        ps_s = s.ps("a_pss", [P, 2, 2, 2 * P])
        ps_t = s.ps("a_pst", [P, 4, 4, P])
        ps_o = s.ps("a_pso", [P, 2, 4, P])
        q_loaded = s.sems("a_q_loaded", 3)
        k_loaded, v_loaded, band_turn = s.sem("a_k_loaded"), s.sem("a_v_loaded"), s.sem("a_band_turn")
        k_hi_made, v_turned, max_made, negated = (s.sem(n) for n in ("a_khi_r", "a_vT", "a_max", "a_neg_r"))
        k_made = s.sem("a_k_made")
        s_made = s.sem("a_s_made")
        masked = s.sem("a_masked")
        exped = s.sem("a_exped")
        p_turned = s.sem("a_pT")
        t_taken = s.sems("a_t_taken", 2)
        o_made = s.sem("a_o_made")
        o_taken = s.sem("a_o_taken")
        stored = s.sems("a_stored", 3)
        carried = s.sem("a_carried")

        def width(g, b):
            return (1 if blocks[g][b][1] == 0 else 2) * P

        def strided(ap, g):
            return ap.rearrange("p (m r) -> p r m", r=dil[g])

        def residues(ap, g):
            return ap.rearrange("p (r m) -> p r m", r=dil[g])

        def evacuate(eng, parity, copy, i, j):
            eng.wait_ge(p_turned, NS * i + j + 5)
            eng.wait_ge(o_made, NS * i + j + 1)
            n = NV + j
            g, sl, b = steps[j]
            if width(g, b) == width(g, b + 1) == 2 * P:
                copy(probs_t[:, j % 4], ps_t[:, n % 4]).then_inc(t_taken[parity], 1)
            elif width(g, b + 1) == P:
                copy(probs_t[:, j % 4, 1::2], ps_t[:, n % 4, 1::2]).then_inc(t_taken[parity], 1)
            else:
                copy(probs_t[:, j % 4, 1:], ps_t[:, n % 4, 1:]).then_inc(t_taken[parity], 1)

        def evacuate_v(eng, parity, copy, i):
            eng.wait_ge(o_made, NS * i + 4)
            for n in range(parity, NV, 2):
                eng.wait_ge(v_turned, NV * i + n + 1)
                copy(v_tok[:, n // 4, n % 4 * 4:n % 4 * 4 + 4], ps_t[:, n % 4]).then_inc(t_taken[parity], 1)

        def scored(unit, g):
            return NS // 2 * unit + SPAN * (g + 1) + NS // 2

        def split_hi(act, unit, g):
            act.wait_ge(k_loaded, 32 * unit + 32)
            act.wait_ge(s_made, scored(unit, g))
            act.activation(residues(k_hi[:, g], g), strided(k_raw[:], g), ACT.Copy).then_inc(k_hi_made, 1)

        def split_lo(pool, unit, g):
            pool.wait_ge(k_hi_made, 3 * unit + g + 1)
            pool.tensor_tensor(residues(k_lo[:, g], g), strided(k_raw[:], g), residues(k_hi[:, g].bitcast(F32), g),
                               ALU.subtract).then_inc(k_made, 1)

        with nc.Block() as block:

            @block.sync
            def _(sp):
                def load_k(pair, sl, unit):
                    sp.wait_ge(k_made, 3 * unit + 1)
                    for half in range(2):
                        sp.dma_start(k_raw[HDIM * half:HDIM * (half + 1)], d["kv"][
                            bass.ds(pair, 1), HDIM * sl:HDIM * (sl + 1)].rearrange("o p t -> p (o t)")
                            ).then_inc(k_loaded, 16)

                def load_q(pair, sl, unit, g):
                    sp.wait_ge(s_made, scored(unit, g))
                    sp.dma_start(q_s[:, g].bitcast(F32), d["qs"][bass.ds(4 * g + pair, 1), sl].rearrange(
                        "o p t -> p (o t)")).then_inc(q_loaded[g], 16)

                def store(i, g):
                    sp.wait_ge(o_taken, 24 * i + 12 + 4 * g + 6)
                    to = d["att"][g, :, bass.ds(i, 1)]
                    for r in range(stores[g]):
                        if g == 1:
                            n = NB // dil[1]
                            sp.dma_start(to.rearrange("(n p r) o q -> r p n (o q)", p=P, r=dil[1])[r],
                                         att[:, g, r * n:(r + 1) * n].rearrange("p n a b -> p n (a b)")
                                         ).then_inc(stored[g], 16)
                        else:
                            order = "(n p) o q -> p n (o q)" if g == 0 else "(p n) o q -> p n (o q)"
                            sp.dma_start(to.rearrange(order, p=P), att[:, g].rearrange("p n a b -> p n (a b)")
                                         ).then_inc(stored[g], 16)

                sp.wait_ge(s_made, NS)
                load_k(0, 0, 0)
                sp.dma_start(v_t[:], d["kv"][4]).then_inc(v_loaded, 16)
                for g in range(3):
                    load_q(0, 0, 0, g)
                with sp.Fori(0, PAIRS) as i:
                    following = (i + 1) % PAIRS
                    sp.wait_ge(v_turned, NV * i + NV)
                    sp.dma_start(v_t[:], d["kv"][bass.ds(4 + following, 1)].rearrange("o p t -> p (o t)")
                                 ).then_inc(v_loaded, 16)
                    load_k(i, 1, 2 * i + 1)
                    for g in range(3):
                        load_q(i, 1, 2 * i + 1, g)
                    load_k(following, 0, 2 * i + 2)
                    for g in range(3):
                        load_q(following, 0, 2 * i + 2, g)
                        store(i, g)
                for g in range(3):
                    sp.wait_ge(stored[g], 16 * stores[g] * (PAIRS + 1))
                    sp.wait_ge(q_loaded[g], 16 * (2 * PAIRS + 1))
                sp.wait_ge(v_loaded, 16 * (PAIRS + 1))
                sp.wait_ge(k_loaded, 32 * (2 * PAIRS + 1))

            @block.gpsimd
            def _(pool):
                pool.sem_inc(k_made, 1)
                pool.memset(zero[:], 0.0).then_inc(band_turn, 1)
                pool.wait_ge(band_turn, 1)
                pool.affine_select(out=band[:, 0], in_=zero[:, 0], compare_op=ALU.is_ge, fill=NEG, base=0,
                                   pattern=[[1, P]], channel_multiplier=-1).then_inc(band_turn, 1)
                pool.affine_select(out=band[:, 1], in_=zero[:, 1], compare_op=ALU.is_ge, fill=NEG, base=0,
                                   pattern=[[-1, P]], channel_multiplier=1).then_inc(band_turn, 1)
                with pool.Fori(0, 2 * PAIRS + 1) as unit:
                    for g in range(3):
                        split_lo(pool, unit, g)

            @block.tensor
            def _(pe):
                pe.sem_inc(s_made, NS)
                pe.sem_inc(p_turned, 4)
                pe.sem_inc(o_made, 4)
                with pe.Fori(0, PAIRS) as i:
                    pe.wait_ge(v_loaded, 16 * i + 16)
                    for n in range(NV):
                        g = n // 4
                        pe.wait_ge(t_taken[n % 2], HALF * i + n // 2 + 1)
                        for b in range(4):
                            r, m = blocks[g][n % 4 * 4 + b]
                            last = pe.transpose(ps_t[:, n % 4, b], strided(v_t[:], g)[:, r, m * P:(m + 1) * P], ident[:])
                        last.then_inc(v_turned, 1)

                    def score(j):
                        g, sl, b = steps[j]
                        if b == 0:
                            pe.wait_ge(q_loaded[g], 32 * i + 16 * sl + 16)
                            pe.wait_ge(k_made, 6 * i + 3 * sl + g + 2)
                        pe.wait_ge(masked, NS * i + j + 1)
                        bank = ps_s[:, j % 2].rearrange("p e k -> p (e k)")
                        for e in range(2):
                            at = (b + e) * P
                            to, keys = (e * 2 * P, at - P) if at else (P, 0)
                            for k, first in ((k_hi, True), (k_lo, False)):
                                last = pe.matmul(bank[:, to:to + 2 * P], q_s[:, g, at:at + P],
                                                 k[:, g, keys:keys + 2 * P], start=first, stop=not first)
                        last.then_inc(s_made, 1)

                    def turn(j):
                        g, sl, b = steps[j]
                        pe.wait_ge(exped, NS * i + j + 5)
                        pe.wait_ge(t_taken[j % 2], HALF * i + (NV + j) // 2 + 1)
                        for e in range(2):
                            for h in range(2 - width(g, b + e) // P, 2):
                                last = pe.transpose(ps_t[:, (NV + j) % 4, 2 * e + h], probs[:, j % 4, e, h * P:(h + 1) * P],
                                                    ident[:])
                        last.then_inc(p_turned, 1)

                    def output(j):
                        g, sl, b = steps[j]
                        if j == 0:
                            pe.wait_ge(t_taken[1], HALF * i + NV // 2 + 2)
                        pe.wait_ge(t_taken[j % 2], HALF * i + (NV + j) // 2 + 3)
                        if j % 2 == 0:
                            pe.wait_ge(o_taken, 24 * i + j // 2 + 1)
                        for e in range(2):
                            first = 2 - width(g, b + e) // P
                            for h in range(first, 2):
                                last = pe.matmul(ps_o[:, j // 2 % 2, (b + e) % 4], probs_t[:, j % 4, 2 * e + h],
                                                 v_tok[:, g, b + e - 1 + h], start=h == first, stop=h == 1)
                        last.then_inc(o_made, 1)

                    for j in range(NS + 4):
                        if j < NS:
                            score(j)
                        if 2 <= j < NS + 2:
                            turn(j - 2)
                        if j >= 4:
                            output(j - 4)

            @block.scalar
            def _(act):
                act.sem_inc(exped, 4)
                act.sem_inc(t_taken[1], 2)
                copy = lambda to, of: act.activation(to, of, ACT.Copy)
                for g in range(3):
                    split_hi(act, 0, g)
                with act.Fori(0, PAIRS) as i:
                    evacuate_v(act, 1, copy, i)
                    for j in range(NS + 2):
                        if j < NS:
                            g, sl, b = steps[j]
                            act.wait_ge(negated, NS * i + j + 1)
                            act.wait_ge(p_turned, NS * i + j + 1)
                            if j % SPAN == 0:
                                act.wait_ge(stored[g], 16 * stores[g] * (i + 1))
                            for e in range(2):
                                n = width(g, b + e)
                                last = act.activation(probs[:, j % 4, e, 2 * P - n:], scores[:, j % 4, e, 2 * P - n:],
                                                      ACT.Exp, bias=neg[:, j % 4, e:e + 1], scale=HDIM ** -0.5,
                                                      accum_out=att[:, g, b + e, sl, HDIM + 1:])
                            last.then_inc(exped, 1)
                            if j % SPAN == 2 and j > SPAN:
                                unit, of = divmod(j // SPAN - 1, 3)
                                split_hi(act, 2 * i + unit + 1, of)
                        if j >= 2 and j % 2:
                            evacuate(act, 1, copy, i, j - 2)
                    split_hi(act, 2 * i + 2, 2)

            @block.vector
            def _(dve):
                dve.sem_inc(masked, 2)
                dve.sem_inc(t_taken[0], 2)
                dve.sem_inc(o_taken, 2)
                for g in range(3):
                    dve.sem_inc(stored[g], 16 * stores[g])
                dve.wait_ge(band_turn, 3)
                keys = band[:].rearrange("p a k -> p (a k)")
                with dve.Fori(0, PAIRS) as i:
                    evacuate_v(dve, 0, dve.tensor_copy, i)
                    for j in range(NS + 5):
                        if j < NS:
                            g, sl, b = steps[j]
                            if j % SPAN == 0:
                                dve.wait_ge(stored[g], 16 * stores[g] * (i + 1))
                            dve.wait_ge(exped, NS * i + j + 1)
                            wait_alone(dve, s_made, NS * i + j + 1 + NS, carried)
                            for e in range(2):
                                n = width(g, b + e)
                                last = dve.tensor_tensor_reduce(
                                    out=scores[:, j % 4, e, 2 * P - n:], in0=ps_s[:, j % 2, e, 2 * P - n:],
                                    in1=keys[:, 2 * P - n:], scale=1.0, scalar=NEG, op0=ALU.add, op1=ALU.max,
                                    accum_out=att[:, g, b + e, sl, HDIM:HDIM + 1])
                            last.then_inc(masked, 1)
                            dve.wait_ge(masked, NS * i + j + 3)
                            dve.tensor_scalar(neg[:, j % 4], att[:, g, b:b + 2, sl, HDIM], -HDIM ** -0.5, None, ALU.mult
                                              ).then_inc(negated, 1)
                        if 2 <= j < NS + 2 and j % 2 == 0:
                            evacuate(dve, 0, dve.tensor_copy, i, j - 2)
                        if j >= 6 and j % 2 == 0:
                            grp = j // 2 - 3
                            g, sl, b = steps[2 * grp]
                            dve.wait_ge(o_made, NS * i + 2 * grp + 6)
                            dve.tensor_copy(att[:, g, b:b + 4, sl, :HDIM], ps_o[:, grp % 2, :, HDIM * sl:HDIM * (sl + 1)]
                                            ).then_inc(o_taken, 1)


BRANCHES = [("y_ssm", "p_ssm", 0, 8), ("y_sc", "p_sc", 12, 4), ("y_attn", "p_attn", 8, 4)]
HALF = SEQ // 2


def weights_of_branches(eng, w, raw, m, raw_loaded):
    for _, p, first, n in BRANCHES:
        eng.dma_start(raw[:, first:first + n], w[p][0, :, bass.ds(m * P, P)].rearrange("(c p) n -> p c n", p=P)
                      ).then_inc(raw_loaded, 16)


def attention_merge_stage(nc, w, d, ident, b):
    W = HDIM + 2
    with ExitStack() as stack:
        s = Scope(nc, stack)
        att = s.sb("m_att", [P, 2, 3, SLOTS, W])
        g_t = s.sb("m_gt", [P, 2, KV // P, P])
        top = s.sb("m_top", [P, 2, SLOTS])
        low = s.sb("m_low", [P, 2, 3, SLOTS])
        ex = s.sb("m_ex", [P, 2, 3, SLOTS])
        den = s.sb("m_den", [P, 2, SLOTS])
        part = s.sb("m_part", [P, 2, 3, SLOTS, HDIM])
        o = s.sb("m_o", [P, 2, KV])
        y = s.sb("m_y", [P, 2, KV // P, P])
        ps = s.ps("m_ps", [P, 2, KV])
        loaded, stored = s.sems("m_loaded", 2), s.sems("m_stored", 2)
        low_made, ex_made, step, part_made, o_half = (s.sem("m_" + n) for n in ("low", "exr", "step", "partr", "ohalf"))
        den_made, ex_scaled, part2_made = s.sem("m_denr"), s.sem("m_exs"), s.sem("m_part2")
        ssm_loaded, sc_loaded, raw_loaded = s.sem("m_ssm_loaded"), s.sem("m_sc_loaded"), s.sem("m_raw_loaded")
        y_hi_made, w_hi_made = s.sem("m_yhi"), s.sem("m_whi")
        o_made = s.sem("m_o_made")
        turned = s.sem("m_turned")
        y_made = s.sem("m_y_made")
        y_raw = b["y_lo"][:].bitcast(F32)
        flat = lambda ap: ap.rearrange("p s q -> p (s q)")
        one = lambda ap: ap.rearrange("p o t -> p (o t)")
        with nc.Block() as block:

            @block.sync
            def _(sp):
                with sp.Fori(0, TILES // 2) as i:
                    for k in range(2):
                        c = 2 * i + k
                        at = bass.ds(c * P, P)
                        sp.wait_ge(y_made, c + 1)
                        for g in range(3):
                            sp.dma_start(flat(att[:, k, g]), d["att"][g, at].rearrange("t a q -> t (a q)")
                                         ).then_inc(loaded[k], 16)
                        sp.dma_start(g_t[:, k], d["g"][:, :, at].rearrange("b p t -> p b t")).then_inc(loaded[k], 16)

            @block.vector
            def _(dve):
                tt = dve.tensor_tensor
                dve.sem_inc(y_made, 2)

                def weigh(c, k, use):
                    m = lambda g: att[:, k, g, :, HDIM]
                    dve.wait_ge(loaded[k], 64 * use + 64)
                    tt(top[:, k], m(0), m(1), ALU.max).then_inc(step, 1)
                    dve.wait_ge(step, 4 * c + 1)
                    tt(top[:, k], top[:, k], m(2), ALU.max).then_inc(step, 1)
                    dve.wait_ge(step, 4 * c + 2)
                    tt(low[:, k], att[:, k, :, :, HDIM], top[:, k].unsqueeze(1).to_broadcast([P, 3, SLOTS]),
                       ALU.subtract).then_inc(low_made, 1)
                    dve.wait_ge(ex_made, c + 1)
                    tt(low[:, k], ex[:, k], att[:, k, :, :, HDIM + 1], ALU.mult).then_inc(step, 1)
                    dve.wait_ge(step, 4 * c + 3)
                    dve.tensor_reduce(den[:, k], low[:, k].rearrange("p g s -> p s g"), mybir.AxisListType.X, ALU.add
                                      ).then_inc(step, 1)
                    dve.wait_ge(step, 4 * c + 4)
                    dve.reciprocal(den[:, k], den[:, k]).then_inc(den_made, 1)
                    dve.wait_ge(den_made, c + 1)
                    tt(ex[:, k], ex[:, k], den[:, k].unsqueeze(1).to_broadcast([P, 3, SLOTS]), ALU.mult
                       ).then_inc(ex_scaled, 1)
                    dve.wait_ge(ex_scaled, c + 1)
                    dve.wait_ge(o_made, c + 1)
                    for g in range(2):
                        last = tt(part[:, k, g], att[:, k, g, :, :HDIM], ex[:, k, g].unsqueeze(2).to_broadcast(
                            [P, SLOTS, HDIM]), ALU.mult)
                    last.then_inc(part_made, 1)

                def gate(c, k, use):
                    dve.wait_ge(turned, c + 3)
                    dve.wait_ge(stored[k], 16 * use + 16)
                    tt(y[:, k], ps[:, k].rearrange("p (b t) -> p b t", t=P), g_t[:, k], ALU.mult).then_inc(y_made, 1)

                weigh(0, 0, 0)
                with dve.Fori(0, TILES // 2 - 1) as i:
                    weigh(2 * i + 1, 1, i)
                    gate(2 * i, 0, i)
                    weigh(2 * i + 2, 0, i + 1)
                    gate(2 * i + 1, 1, i)
                weigh(TILES - 1, 1, TILES // 2 - 1)
                gate(TILES - 2, 0, TILES // 2 - 1)
                gate(TILES - 1, 1, TILES // 2 - 1)

            @block.gpsimd
            def _(pool):
                pool.sem_inc(o_made, 2)
                tt = pool.tensor_tensor
                with pool.Fori(0, TILES // 2) as i:
                    for k in range(2):
                        c = 2 * i + k
                        pool.wait_ge(ex_scaled, c + 1)
                        tt(part[:, k, 2], att[:, k, 2, :, :HDIM], ex[:, k, 2].unsqueeze(2).to_broadcast([P, SLOTS, HDIM]),
                           ALU.mult).then_inc(part2_made, 1)
                        pool.wait_ge(part_made, c + 1)
                        pool.wait_ge(turned, c + 1)
                        tt(o[:, k], flat(part[:, k, 0]), flat(part[:, k, 1]), ALU.add).then_inc(o_half, 1)
                        pool.wait_ge(o_half, c + 1)
                        pool.wait_ge(part2_made, c + 1)
                        tt(o[:, k], o[:, k], flat(part[:, k, 2]), ALU.add).then_inc(o_made, 1)
                    pool.wait_ge(y_hi_made, i + 1)
                    at = bass.ds(i, 1)
                    tt(one(b["y_lo"][:, at]), one(y_raw[:, at]), one(b["y_hi"][:, at].bitcast(F32)), ALU.subtract)
                for c in range(12, 16):
                    pool.wait_ge(y_hi_made, c - 3)
                    tt(b["y_lo"][:, c], y_raw[:, c], b["y_hi"][:, c].bitcast(F32), ALU.subtract)
                pool.wait_ge(w_hi_made, 1)
                tt(b["w_lo"][:, 0], b["raw"][:], b["w_hi"][:, 0].bitcast(F32), ALU.subtract)

            @block.tensor
            def _(pe):
                pe.sem_inc(turned, 2)
                with pe.Fori(0, TILES // 2) as i:
                    for k in range(2):
                        c = 2 * i + k
                        pe.wait_ge(o_made, c + 3)
                        pe.wait_ge(y_made, c + 1)
                        for q in range(KV // P):
                            last = pe.transpose(ps[:, k, q * P:(q + 1) * P], o[:, k, q * P:(q + 1) * P], ident[:])
                        last.then_inc(turned, 1)

            @block.scalar
            def _(act):
                act.sem_inc(stored[0], 16)
                act.sem_inc(stored[1], 16)
                act.wait_ge(loaded[0], 64)
                for c in range(8):
                    act.dma_start(y_raw[:, c], d["y_ssm"][c, :, :HALF]).then_inc(ssm_loaded, 16)
                for c in range(4):
                    act.dma_start(y_raw[:, 12 + c], d["y_sc"][c, :, :HALF]).then_inc(sc_loaded, 16)
                weights_of_branches(act, w, b["raw"], 0, raw_loaded)

                def weight(c, k):
                    act.wait_ge(low_made, c + 1)
                    act.activation(ex[:, k], low[:, k], ACT.Exp, scale=HDIM ** -0.5).then_inc(ex_made, 1)

                def store(c, k):
                    act.wait_ge(y_made, c + 3)
                    act.dma_start(d["y_attn"][:, :, bass.ds(c * P, P)].rearrange("b p t -> p b t"), y[:, k]
                                  ).then_inc(stored[k], 16)

                weight(0, 0)
                with act.Fori(0, TILES // 2 - 1) as i:
                    weight(2 * i + 1, 1)
                    weight(2 * i + 2, 0)
                    store(2 * i, 0)
                    act.wait_ge(ssm_loaded, 128)
                    at = bass.ds(i, 1)
                    act.activation(one(b["y_hi"][:, at]), one(y_raw[:, at]), ACT.Copy).then_inc(y_hi_made, 1)
                    store(2 * i + 1, 1)
                weight(TILES - 1, 1)
                act.activation(b["y_hi"][:, 7], y_raw[:, 7], ACT.Copy).then_inc(y_hi_made, 1)
                act.wait_ge(sc_loaded, 64)
                for c in range(12, 16):
                    act.activation(b["y_hi"][:, c], y_raw[:, c], ACT.Copy).then_inc(y_hi_made, 1)
                act.wait_ge(raw_loaded, 48)
                act.activation(b["w_hi"][:, 0], b["raw"][:], ACT.Copy).then_inc(w_hi_made, 1)
                store(TILES - 2, 0)
                store(TILES - 1, 1)
                for k in range(2):
                    act.wait_ge(stored[k], 16 * (TILES // 2) + 16)


def branch_stage(nc, w, d, b):
    NM = DM // P
    y_hi, y_lo, raw, w_hi, w_lo = (b[n] for n in ("y_hi", "y_lo", "raw", "w_hi", "w_lo"))
    y_raw = y_lo[:].bitcast(F32)
    order = [(br, c) for br, (_, _, first, n) in enumerate(BRANCHES) for c in range(first, first + n)]
    with ExitStack() as stack:
        s = Scope(nc, stack)
        gate = s.sb("b_gate", [P, 3, HALF])
        total = s.sb("b_total", [P, 2, HALF])
        part = s.sb("b_part", [P, 2, HALF])
        acc = s.ps("b_acc", [P, 3, HALF])
        y_loaded = s.sems("b_y_loaded", 4)
        gate_loaded, raw_loaded = s.sems("b_gate_loaded", 3), s.sem("b_raw_loaded")
        y_hi_made, w_hi_made, total_step, carried = (s.sem("b_" + n) for n in ("yhi_r", "whi_r", "total", "carried"))
        y_made = s.sem("b_y_made")
        w_made = s.sem("b_w_made")
        acc_made = s.sems("b_acc_made", 3)
        acc_taken = s.sems("b_acc_taken", 3)
        stored = s.sems("b_stored", 2)
        GATE = (0, 2, 1)
        with nc.Block() as block:

            @block.sync
            def _(sp):
                for h in range(2):
                    tokens = slice(h * HALF, (h + 1) * HALF)
                    with sp.Fori(0, NM // 2) as i:
                        for k in range(2):
                            m = 2 * i + k
                            for br in range(3):
                                sp.wait_ge(acc_taken[br], NM * h + m + 1)
                                sp.dma_start(gate[:, br], d["gates"][bass.ds(NM * GATE[br] + m, 1), :, tokens].rearrange(
                                    "o p t -> p (o t)")).then_inc(gate_loaded[br], 16)
                            sp.wait_ge(total_step, 2 * (NM * h + m) + 2)
                            sp.dma_start(d["merged"][bass.ds(m, 1), :, tokens].rearrange("o p t -> p (o t)"),
                                         total[:, k]).then_inc(stored[k], 16)
                for k in range(2):
                    sp.wait_ge(stored[k], 16 * NM + 16)

            @block.gpsimd
            def _(pool):
                pool.sem_inc(w_made, 2)

                def split(u, k):
                    pool.wait_ge(raw_loaded, 48 * u)
                    wait_alone(pool, acc_made[2], u + 1, carried)
                    pool.tensor_copy(w_hi[:, k], raw[:]).then_inc(w_hi_made, 1)
                    pool.wait_ge(w_hi_made, u)
                    pool.tensor_tensor(w_lo[:, k], raw[:], w_hi[:, k].bitcast(F32), ALU.subtract).then_inc(w_made, 1)

                split(1, 1)
                with pool.Fori(1, NM) as i:
                    for k in range(2):
                        split(2 * i + k, k)

            @block.scalar
            def _(act):
                act.sem_inc(stored[0], 16)
                act.sem_inc(stored[1], 16)

                def load_weights(u):
                    act.wait_ge(w_made, u + 1)
                    weights_of_branches(act, w, raw, u % NM, raw_loaded)

                load_weights(1)
                for h in range(2):
                    for br, (y, _, first, n) in enumerate(BRANCHES):
                        if h or br == 2:
                            act.wait_ge(acc_made[br], NM * h + 2)
                            for c in range(n):
                                act.dma_start(y_raw[:, first + c], d[y][c, :, h * HALF:(h + 1) * HALF]
                                              ).then_inc(y_loaded[br + 1 if br else c // 4], 16)
                    for at, (br, c) in enumerate(order):
                        if h or br == 2:
                            q = br + 1 if br else c // 4
                            act.wait_ge(y_loaded[q], 64 * (h + 1) if br == 2 else 64)
                            act.activation(y_hi[:, c], y_raw[:, c], ACT.Copy).then_inc(y_hi_made, 1)
                    with act.Fori(0, NM - (2 if h else 0)) as m:
                        load_weights(m + NM * h + 2)

            @block.tensor
            def _(pe):
                for br in range(3):
                    pe.sem_inc(acc_made[br], 2)
                for h in range(2):
                    with pe.Fori(0, NM // 2) as i:
                        for k in range(2):
                            u = NM * h + 2 * i + k
                            pe.wait_ge(w_made, u + 2)
                            for br, (_, _, first, n) in enumerate(BRANCHES):
                                pe.wait_ge(acc_taken[br], u + 1)
                                for t in range(2):
                                    span = slice(t * BANK, (t + 1) * BANK)
                                    for c in range(first, first + n):
                                        if t == 0:
                                            pe.wait_ge(y_made, 16 * h + order.index((br, c)) + 1)
                                        to = acc[:, br, span]
                                        pe.matmul(to, w_hi[:, k, c], y_hi[:, c, span], start=c == first, stop=False)
                                        pe.matmul(to, w_hi[:, k, c], y_lo[:, c, span], start=False, stop=False)
                                        last = pe.matmul(to, w_lo[:, k, c], y_hi[:, c, span], start=False,
                                                         stop=c == first + n - 1)
                                last.then_inc(acc_made[br], 1)

            @block.vector
            def _(dve):
                dve.sem_inc(y_made, 12)
                for br in range(3):
                    dve.sem_inc(acc_taken[br], 1)
                for h in range(2):
                    for at, (br, c) in enumerate(order):
                        if h or br == 2:
                            dve.wait_ge(y_hi_made, 16 * h + at - 11)
                            dve.tensor_tensor(y_lo[:, c], y_raw[:, c], y_hi[:, c].bitcast(F32), ALU.subtract
                                              ).then_inc(y_made, 1)
                    with dve.Fori(0, NM // 2) as i:
                        for k in range(2):
                            u = NM * h + 2 * i + k
                            dve.wait_ge(stored[k], 64 * h + 16 * i + 16)
                            for br in range(3):
                                dve.wait_ge(acc_made[br], u + 3)
                                dve.wait_ge(gate_loaded[br], 16 * u + 16)
                                to = total[:, k] if br == 0 else part[:, br - 1]
                                if br == 2:
                                    dve.wait_ge(total_step, 2 * u + 1)
                                dve.tensor_tensor(to, acc[:, br], gate[:, br], ALU.mult).then_inc(acc_taken[br], 1)
                                dve.wait_ge(acc_taken[br], u + 2)
                                if br:
                                    dve.tensor_tensor(total[:, k], total[:, k], part[:, br - 1], ALU.add
                                                      ).then_inc(total_step, 1)


def output_stage(nc, w, d, out, eps):
    with ExitStack() as stack:
        s = Scope(nc, stack)
        w_hi, w_lo = s.sb("o_whi", [P, KC, DM], F32R), s.sb("o_wlo", [P, KC, DM], F32R)
        w_raw = s.sb("o_wraw", [P, KC, DM])
        m_raw = s.sb("o_mraw", [P, 2, KC, P])
        m_hi, m_lo = s.sb("o_mhi", [P, 2, KC, P], F32R), s.sb("o_mlo", [P, 2, KC, P], F32R)
        x_sb = s.sb("o_x", [P, 2, DM])
        w_post = s.sb("o_wpost", [P, DM])
        sq = s.sb("o_sq", [P, 2, DM])
        ss, std, rstd = (s.sb(n, [P, 2]) for n in ("o_ss", "o_std", "o_rstd"))
        y = s.sb("o_y", [P, 2, DM])
        acc = s.ps("o_acc", [P, 2, DM])
        w_loaded, post_loaded = s.sems("o_w_loaded", KC), s.sem("o_post_loaded")
        m_loaded, x_loaded = s.sems("o_m_loaded", 2), s.sems("o_x_loaded", 2)
        w_hi_made, w_made = s.sem("o_whi_r"), s.sem("o_w_made")
        m_hi_made, squared, std_made, rstd_made = (s.sem("o_" + n) for n in ("mhi_r", "sq_r", "std_r", "rstd_r"))
        m_made = s.sem("o_m_made")
        acc_made = s.sem("o_acc_made")
        acc_taken = s.sem("o_acc_taken")
        y_made = s.sem("o_y_made")
        y_free = s.sem("o_y_free")
        stored = s.sems("o_stored", 2)
        with nc.Block() as block:

            @block.sync
            def _(sp):
                def load_m(c, k):
                    sp.wait_ge(m_made, c + 1)
                    sp.dma_start(m_raw[:, k], d["merged"][:, :, bass.ds(c * P, P)].rearrange("b p t -> p b t")
                                 ).then_inc(m_loaded[k], 16)

                def load_x(c, k):
                    sp.wait_ge(y_made, c + 1)
                    sp.dma_start(x_sb[:, k], w["x"][0, bass.ds(c * P, P), :]).then_inc(x_loaded[k], 16)

                load_m(0, 0)
                for c in range(KC):
                    sp.dma_start(w_raw[:, c], w["w_out"][0, c * P:(c + 1) * P, :]).then_inc(w_loaded[c], 16)
                sp.dma_start(w_post[:], w["norm_post"][0:1, :].to_broadcast([P, DM])).then_inc(post_loaded, 16)
                with sp.Fori(0, TILES // 2 - 1) as i:
                    for k in range(2):
                        load_m(2 * i + k + 1, 1 - k)
                        load_x(2 * i + k, k)
                load_m(TILES - 1, 1)
                load_x(TILES - 2, 0)
                load_x(TILES - 1, 1)

            @block.scalar
            def _(act):
                def hi(c, k, use):
                    act.wait_ge(m_loaded[k], 16 * use + 16)
                    act.wait_ge(acc_made, c + 1)
                    act.activation(m_hi[:, k], m_raw[:, k], ACT.Copy).then_inc(m_hi_made, 1)

                def finish(c, k):
                    act.wait_ge(acc_made, c + 3)
                    act.activation(sq[:, k], acc[:, k], ACT.Square, accum_out=ss[:, k:k + 1]).then_inc(squared, 1)
                    act.wait_ge(squared, c + 1)
                    act.activation(std[:, k:k + 1], ss[:, k:k + 1], ACT.Sqrt, bias=eps[:], scale=1.0 / DM
                                   ).then_inc(std_made, 1)

                hi(0, 0, 0)
                for c in range(KC):
                    act.wait_ge(w_loaded[c], 16)
                    act.activation(w_hi[:, c], w_raw[:, c], ACT.Copy).then_inc(w_hi_made, 1)
                with act.Fori(0, TILES // 2 - 1) as i:
                    for k in range(2):
                        hi(2 * i + k + 1, 1 - k, i + k)
                        finish(2 * i + k, k)
                hi(TILES - 1, 1, TILES // 2 - 1)
                finish(TILES - 2, 0)
                finish(TILES - 1, 1)

            @block.gpsimd
            def _(pool):
                pool.sem_inc(y_free, 2)
                with pool.Fori(0, TILES // 2) as i:
                    for k in range(2):
                        c = 2 * i + k
                        pool.wait_ge(y_made, c + 3)
                        pool.dma_start(out[0, bass.ds(c * P, P), :], y[:, k]).then_inc(stored[k], 16)
                        pool.wait_ge(stored[k], 16 * i + 16)
                        pool.sem_inc(y_free, 1)

            @block.tensor
            def _(pe):
                pe.sem_inc(acc_made, 2)

                def product(c, k):
                    pe.wait_ge(m_made, c + 3)
                    pe.wait_ge(acc_taken, c + 1)
                    for b in range(KC):
                        pe.wait_ge(w_made, b + 1)
                        for t in range(2):
                            span = slice(t * BANK, (t + 1) * BANK)
                            to = acc[:, k, span]
                            pe.matmul(to, m_hi[:, k, b], w_hi[:, b, span], start=b == 0, stop=False)
                            pe.matmul(to, m_hi[:, k, b], w_lo[:, b, span], start=False, stop=False)
                            last = pe.matmul(to, m_lo[:, k, b], w_hi[:, b, span], start=False, stop=b == KC - 1)
                    last.then_inc(acc_made, 1)

                with pe.Fori(0, TILES // 2) as i:
                    for k in range(2):
                        product(2 * i + k, k)

            @block.vector
            def _(dve):
                dve.sem_inc(m_made, 2)
                dve.sem_inc(acc_taken, 2)
                dve.sem_inc(y_made, 2)

                def lo(c, k):
                    dve.wait_ge(m_hi_made, c + 1)
                    dve.tensor_tensor(m_lo[:, k], m_raw[:, k], m_hi[:, k].bitcast(F32), ALU.subtract).then_inc(m_made, 1)

                def finish(c, k, use):
                    dve.wait_ge(std_made, c + 1)
                    dve.reciprocal(rstd[:, k:k + 1], std[:, k:k + 1]).then_inc(rstd_made, 1)
                    dve.wait_ge(rstd_made, c + 1)
                    dve.wait_ge(y_free, c + 1)
                    dve.scalar_tensor_tensor(y[:, k], acc[:, k], rstd[:, k:k + 1], w_post[:], ALU.mult, ALU.mult
                                             ).then_inc(acc_taken, 1)
                    dve.wait_ge(acc_taken, c + 3)
                    dve.wait_ge(x_loaded[k], 16 * use + 16)
                    dve.tensor_tensor(y[:, k], y[:, k], x_sb[:, k], ALU.add).then_inc(y_made, 1)

                lo(0, 0)
                for c in range(KC):
                    dve.wait_ge(w_hi_made, c + 1)
                    dve.tensor_tensor(w_lo[:, c], w_raw[:, c], w_hi[:, c].bitcast(F32), ALU.subtract).then_inc(w_made, 1)
                dve.wait_ge(post_loaded, 16)
                with dve.Fori(0, TILES // 2 - 1) as i:
                    for k in range(2):
                        lo(2 * i + k + 1, 1 - k)
                        finish(2 * i + k, k, i)
                lo(TILES - 1, 1)
                finish(TILES - 2, 0, TILES // 2 - 1)
                finish(TILES - 1, 1, TILES // 2 - 1)


def constants_stage(nc, ident, eps):
    with nc.semaphore("c_z") as z, nc.Block() as block:
        @block.gpsimd
        def _(pool):
            pool.memset(eps[:], EPS)
            pool.memset(ident[:], 0.0).then_inc(z, 1)
            pool.wait_ge(z, 1)
            pool.affine_select(out=ident[:], in_=ident[:], compare_op=ALU.not_equal, fill=1.0, base=0,
                               pattern=[[-1, P]], channel_multiplier=1)


def build(nc, w, out, stages=("proj", "ssd", "attn", "merge", "out"), given=()):
    def scratch(name, shape):
        kind = "ExternalInput" if name in given else "Internal"
        return nc.dram_tensor(name, shape, F32, kind=kind).ap()

    d = {"dt": scratch("s_dt", [P, SEQ]), "z": scratch("s_z", [SSM // P, P, SEQ]),
         "xbc": scratch("s_xbc", [16, P, SEQ]), "qs": scratch("s_qs", [12, 2, P, SEQ]),
         "kv": scratch("s_kv", [8, P, SEQ]),
         "g": scratch("s_g", [4, P, SEQ]), "y_sc": scratch("s_ysc", [4, P, SEQ]),
         "gates": scratch("s_gates", [24, P, SEQ]), "y_ssm": scratch("s_yssm", [8, P, SEQ]),
         "att": scratch("s_att", [3, SEQ, SLOTS // 2, 2 * (HDIM + 2)]),
         "y_attn": scratch("s_yattn", [4, P, SEQ]), "merged": scratch("s_merged", [8, P, SEQ])}
    with ExitStack() as stack:
        s = Scope(nc, stack)
        ident = s.sb("ident", [P, P])
        eps = s.sb("eps", [P, 1])
        if "proj" not in stages:
            constants_stage(nc, ident, eps)
        with ExitStack() as inner:
            if "proj" in stages:
                h = Scope(nc, inner)
                h_hi = h.sb("h_hi", [P, KC, SEQ], F32R)
                h_lo = h.sb("h_lo", [P, KC, SEQ], F32R)
                projection_stage(nc, w, d, h_hi, h_lo, ident, eps)
        if "ssd" in stages:
            ssd_stage(nc, w, d, ident, eps)
        if "attn" in stages:
            attention_stage(nc, w, d, ident)
        if "merge" in stages:
            with ExitStack() as inner:
                h = Scope(nc, inner)
                b = {n: h.sb("b_" + n, [P, 16, HALF], F32R) for n in ("y_hi", "y_lo")}
                b["raw"] = h.sb("b_raw", [P, 16, P])
                b.update({n: h.sb("b_" + n, [P, 2, 16, P], F32R) for n in ("w_hi", "w_lo")})
                attention_merge_stage(nc, w, d, ident, b)
                branch_stage(nc, w, d, b)
        if "out" in stages:
            output_stage(nc, w, d, out, eps)


INS = ("x", "norm_pre", "norm_post", "w_in", "ssm_conv_w", "ssm_conv_b", "dt_bias", "a_log", "d_skip", "ssm_norm",
       "sc_conv_w", "p_ssm", "p_attn", "p_sc", "w_out")


def kernel(**inputs):
    import numpy as np
    import concourse.bacc as bacc
    from concourse.bass_utils import run_bass_kernel_spmd

    nc = bacc.Bacc("TRN2", target_bir_lowering=False, num_devices=1)
    arrays = {name: np.ascontiguousarray(inputs[name]) for name in INS}
    w = {name: nc.dram_tensor(name, a.shape, F32, kind="ExternalInput").ap() for name, a in arrays.items()}
    out = nc.dram_tensor("out", (1, SEQ, DM), F32, kind="ExternalOutput").ap()
    build(nc, w, out)
    return run_bass_kernel_spmd(nc, [arrays], core_ids=[0]).results[0]["out"]
```

```python
from contextlib import ExitStack

import concourse.bass as bass
from concourse import mybir

F32 = mybir.dt.float32
F32R = mybir.dt.float32r
ALU = mybir.AluOpType
ACT = mybir.ActivationFunctionType

P = 128
SEQ, DM = 2048, 1024
KC = DM // P
TILES = SEQ // P
BANK = 512
SPANS = SEQ // BANK
HEADS, HDIM, GROUPS, STATE = 16, 64, 4, 128
SSM = HEADS * HDIM
HALF = SEQ // 2
GW = SSM // GROUPS
SLOTS, PATTERNS = 8, ((128, 1), (512, 4), (2048, 16))
KV = SLOTS * HDIM
PAIR = 2 * HDIM
SC = 512
EPS = 1e-6
NEG = -1e30

C_Z = 0
C_XBC = C_Z + SSM
C_DT = C_XBC + SSM + 2 * GROUPS * STATE
C_Q = C_DT + HEADS
C_G = C_Q + 3 * KV + 2 * KV
C_U = C_G + KV
C_B, C_C, C_GSC = C_U + SC, C_U + 2 * SC, C_U + 3 * SC
C_MERGE = C_U + 4 * SC
IN_W = C_MERGE + 3 * DM


class Scope:

    def __init__(self, nc, stack):
        self.nc, self.stack = nc, stack
        self.cleared = []

    def sb(self, name, shape, dt=F32):
        return self.stack.enter_context(self.nc.sbuf_tensor(name, shape, dt))

    def ps(self, name, shape, dt=F32):
        return self.stack.enter_context(self.nc.psum_tensor(name, shape, dt))

    def sem(self, name):
        return self.stack.enter_context(self.nc.semaphore(name))

    def cleared_sem(self, name):
        self.cleared.append(self.nc.alloc_semaphore(name=name))
        return self.cleared[-1]

    def clear(self):
        self.nc.clear_and_free_semaphores(self.cleared)
        self.nc.all_engine_barrier()

    def sems(self, name, n):
        return [self.sem(f"{name}{i}") for i in range(n)]


def wait_alone(eng, sem, value, carrier):
    eng.wait_ge(sem, value)
    eng.sem_inc(carrier, 1)


def projection_stage(nc, w, d, h, wt, v, ident, eps):
    pairs = {"z": SSM // P // 2, "xbc": (C_DT - C_XBC) // P // 2, "q0": KV // P // 2, "q1": KV // P // 2,
             "q2": KV // P // 2, "kv": 2 * KV // P // 2, "g": KV // P // 2,
             "sc": 4 * SC // P // 2, "gates": 3 * DM // P // 2}
    base, n_pairs = {}, 0
    for kind, n in pairs.items():
        base[kind] = n_pairs
        n_pairs += n
    with ExitStack() as stack:
        s = Scope(nc, stack)
        cleared, cleared_sems = s.cleared_sem, lambda name, n: [s.cleared_sem(f"{name}{i}") for i in range(n)]
        raw, w_hi, w_lo, work = wt["raw"], wt["w_hi"], wt["w_lo"], wt["work"]
        stage = s.sb("p_stage", [P, 2, SEQ])
        cw = s.sb("p_cw", [P, 16, 4])
        cb = s.sb("p_cb", [P, 16])
        scw = s.sb("p_scw", [P, 4, 3])
        bias_b, alog_b = s.sb("p_bias", [P, HEADS]), s.sb("p_alog", [P, HEADS])
        w_pre = s.sb("n_wpre", [P, DM])
        ssum, std, rstd = (s.sb(n, [P, 4]) for n in ("n_ssum", "n_std", "n_rstd"))
        acc = s.ps("p_acc", [P, 2, SEQ])
        x_sb = stage[:].rearrange("p a (b n) -> p (a b) n", n=DM)
        x_scaled, h_tok = (work[:, k].rearrange("p (b n) -> p b n", n=DM) for k in range(2))
        tr = acc[:, 1].rearrange("p (b n) -> p b n", n=DM)
        squared = raw[:, 1].rearrange("p c n -> p (c n)")
        dt_raw = work[:HEADS, 0]
        t0, t1, t2, t3 = (work[:, 1, j * TILES * HEADS:(j + 1) * TILES * HEADS] for j in range(4))
        ps_dt, ps_cs, ps_last = (acc[:, 1, at:at + TILES * HEADS] for at in (2 * BANK, 3 * BANK, 3 * BANK + TILES * HEADS))
        x_loaded, pre_loaded = cleared_sems("n_x_loaded", 4), cleared("n_pre_loaded")
        summed, std_made, rstd_made, hi_made, id_zero, id_ready, eps_ready = (
            cleared("n_" + n) for n in ("summed", "std_r", "rstd_r", "hi_r", "id_zero", "id_ready", "eps_ready"))
        scaled = cleared("n_scaled")
        h_made = cleared("n_h_made")
        tr_made = cleared("n_tr_made")
        lo_made = cleared("n_lo_made")
        raw_loaded = cleared_sems("p_raw_loaded", 2)
        consts_loaded = cleared("p_consts_loaded")
        hi_ready = cleared("p_hi_ready")
        carried_v = cleared("p_carried_v")
        carried = cleared("p_carried")
        w_made = cleared_sems("p_w_made", 2)
        acc_made = cleared_sems("p_acc_made", 2)
        acc_taken = cleared_sems("p_acc_taken", 2)
        stored = cleared_sems("p_stored", 2)
        conv_step = cleared("p_conv_step")
        q_hi_made = cleared("p_q_hi_r")
        hi_stored, lo_stored = cleared_sems("p_hi_stored", 2), cleared_sems("p_lo_stored", 2)
        conv_taken = cleared("p_conv_taken")
        sc_step = cleared("p_sc_step")
        sc_done = cleared("p_sc_done")
        dt_loaded, turn, turn2, first_made = (cleared("p_" + n) for n in ("dt_loaded", "turn", "turn2", "first_made"))
        chunk_loaded = cleared("p_chunk_loaded")

        def tiled(ap):
            return ap.rearrange("p (n t) -> p n t", t=P)

        def tile_of(n, part, half):
            return h[half][:, bass.ds(n - TILES // 2 * half, 1), part].rearrange("p o c t -> p (o c) t")

        with nc.Block() as block:

            @block.sync
            def _(sp):
                def load(slot, use, col):
                    sp.wait_ge(w_made[slot], use + 1)
                    sp.dma_start(raw[:, slot], w["w_in"][0, :, bass.ds(col, P)].rearrange("(c p) n -> p c n", p=P)
                                 ).then_inc(raw_loaded[slot], 16)

                sp.wait_ge(scaled, 4)
                for k in range(2):
                    sp.dma_start(x_sb[:, k], w["x"][0, k * P:(k + 1) * P, :]).then_inc(x_loaded[k], 16)
                sp.dma_start(w_pre[:], w["norm_pre"][0:1, :].to_broadcast([P, DM])).then_inc(pre_loaded, 16)
                for k in range(2, 4):
                    sp.dma_start(x_sb[:, k], w["x"][0, k * P:(k + 1) * P, :]).then_inc(x_loaded[k], 16)
                    if k == 2:
                        load(0, 0, C_DT)
                with sp.Fori(0, TILES // 4 - 1) as i:
                    for k in range(4):
                        n = 4 * i + 4 + k
                        sp.wait_ge(scaled, n + 1)
                        sp.dma_start(x_sb[:, k], w["x"][0, bass.ds(n * P, P), :]).then_inc(x_loaded[k], 16)
                sp.wait_ge(summed, TILES)
                with nc.allow_non_contiguous_dma(reason="per-channel taps, once"):
                    for t in range(4):
                        sp.dma_start(cw[:, :, t:t + 1], w["ssm_conv_w"][0, t, :].rearrange("(b p o) -> p b o", p=P, o=1)
                                     ).then_inc(consts_loaded, 16)
                    sp.dma_start(cb[:], w["ssm_conv_b"][0, :].rearrange("(b p) -> p b", p=P)
                                 ).then_inc(consts_loaded, 16)
                    for t in range(3):
                        sp.dma_start(scw[:, :, t:t + 1], w["sc_conv_w"][0, t, :].rearrange("(b p o) -> p b o", p=P, o=1)
                                     ).then_inc(consts_loaded, 16)

                def run(kind, col, first=0, end=None):
                    with sp.Fori(first, end or pairs[kind]) as i:
                        load(1, base[kind] + i, col + 2 * P * i)
                        load(0, base[kind] + i + 1, col + 2 * P * i + P)

                run("z", C_Z)
                run("xbc", C_XBC)
                for g in range(3):
                    run(f"q{g}", C_Q + g * KV)
                run("kv", C_Q + 3 * KV)
                run("g", C_G)
                with sp.Fori(0, SC // P) as f:
                    load(1, base["sc"] + 2 * f, C_U + P * f)
                    load(0, base["sc"] + 2 * f + 1, C_C + P * f)
                    load(1, base["sc"] + 2 * f + 1, C_B + P * f)
                    load(0, base["sc"] + 2 * f + 2, C_GSC + P * f)
                gates_done = pairs["gates"] // 3
                run("gates", C_MERGE, 0, gates_done)
                sp.wait_ge(sc_done, SC // P + 1)
                sp.dma_start(dt_raw, d["dt"][0:HEADS, :]).then_inc(dt_loaded, 16)
                for to, of in ((bias_b, "dt_bias"), (alog_b, "a_log"), (v["dskip"], "d_skip")):
                    sp.dma_start(to[:], w[of][0:1, :].to_broadcast([P, HEADS])).then_inc(dt_loaded, 16)
                run("gates", C_MERGE, gates_done)
                load(1, n_pairs, C_MERGE)
                load(0, n_pairs + 1, C_MERGE + P)
                sp.wait_ge(turn, 3)
                sp.dma_start(work[:, 0].rearrange("p (b t) -> p b t", t=P), d["xbc"][:, :, :P].rearrange("b p t -> p b t")
                             ).then_inc(chunk_loaded, 16)
                sp.wait_ge(chunk_loaded, 16)
                sp.wait_ge(raw_loaded[0], 16 * (n_pairs + 2))

            @block.gpsimd
            def _(pool):
                for k in range(2):
                    pool.sem_inc(w_made[k], 1)
                pool.sem_inc(h_made, 2)
                pool.memset(eps[:], EPS).then_inc(eps_ready, 1)
                pool.memset(ident[:], 0.0).then_inc(id_zero, 1)
                pool.wait_ge(id_zero, 1)
                pool.affine_select(out=ident[:], in_=ident[:], compare_op=ALU.not_equal, fill=1.0, base=0,
                                   pattern=[[-1, P]], channel_multiplier=1).then_inc(id_ready, 1)

                pool.memset(v["ones"][:], 1.0).then_inc(turn, 1)
                pool.wait_ge(turn, 1)
                pool.affine_select(out=v["tri"][:], in_=v["ones"][:], compare_op=ALU.is_ge, fill=0.0, base=0,
                                   pattern=[[1, P]], channel_multiplier=-1).then_inc(turn, 1)

                def split(slot, use, n):
                    pool.wait_ge(raw_loaded[slot], 16 * use + 16)
                    wait_alone(pool, acc_made[slot], use + 1, carried)
                    pool.tensor_copy(w_hi[:, slot], raw[:, slot]).then_inc(hi_ready, 1)
                    pool.wait_ge(hi_ready, n + 1)
                    pool.tensor_tensor(w_lo[:, slot], raw[:, slot], w_hi[:, slot], ALU.subtract
                                       ).then_inc(w_made[slot], 1)

                pool.wait_ge(pre_loaded, 16)
                with pool.Fori(0, TILES // 2) as i:
                    for k in range(2):
                        n = 2 * i + k
                        pool.wait_ge(scaled, n + 5)
                        pool.wait_ge(tr_made, n + 1)
                        pool.tensor_tensor(h_tok[:, k], x_scaled[:, k], w_pre[:], ALU.mult).then_inc(h_made, 1)
                with pool.Fori(0, n_pairs) as i:
                    split(1, i, 2 * i + 1)
                    split(0, i + 1, 2 * i + 2)
                pool.wait_ge(raw_loaded[1], 16 * n_pairs + 16)
                pool.tensor_copy(w_hi[:, 2], raw[:, 1]).then_inc(first_made, 1)
                pool.wait_ge(first_made, 1)
                pool.tensor_tensor(w_lo[:, 2], raw[:, 1], w_hi[:, 2], ALU.subtract)

            @block.tensor
            def _(pe):
                for k in range(2):
                    pe.sem_inc(acc_made[k], 1)
                pe.sem_inc(tr_made, 2)
                pe.wait_ge(id_ready, 1)

                def transposes(n):
                    pe.wait_ge(h_made, n + 3)
                    pe.wait_ge(lo_made, n + 1)
                    for c in range(KC):
                        last = pe.transpose(tr[:, n % 2, c * P:(c + 1) * P], h_tok[:, n % 2, c * P:(c + 1) * P], ident[:])
                    last.then_inc(tr_made, 1)

                def span_of(slot, t, chunks=range(KC)):
                    to = tiled(acc[:, slot, t * BANK:(t + 1) * BANK])
                    for c in chunks:
                        h_hi, h_lo = (h[t // 2][:, t % 2 * 4:t % 2 * 4 + 4, part, c] for part in range(2))
                        pe.matmul(to, w_hi[:, slot, c], h_hi, start=c == 0, stop=False)
                        pe.matmul(to, w_hi[:, slot, c], h_lo, start=False, stop=False)
                        last = pe.matmul(to, w_lo[:, slot, c], h_hi, start=False, stop=c == KC - 1)
                    return last

                def product(slot, use, spans=SPANS):
                    pe.wait_ge(w_made[slot], use + 2)
                    pe.wait_ge(acc_taken[slot], use + 1)
                    for t in range(spans):
                        last = span_of(slot, t)
                    last.then_inc(acc_made[slot], 1)

                for n in range(4):
                    transposes(n)
                pe.wait_ge(w_made[0], 2)
                pe.wait_ge(acc_taken[0], 1)
                for t in range(SPANS):
                    for q in range(4):
                        if 4 * t + 4 + q < TILES:
                            transposes(4 * t + 4 + q)
                        if q == 0:
                            pe.wait_ge(lo_made, 4 * t + 6)
                        last = span_of(0, t, range(2 * q, 2 * q + 2))
                last.then_inc(acc_made[0], 1)
                with pe.Fori(0, base["gates"]) as i:
                    product(1, i)
                    product(0, i + 1)
                for third in range(3):
                    at = base["gates"] + third * pairs["gates"] // 3
                    with pe.Fori(0, pairs["gates"] // 3) as i:
                        product(1, at + i, spans=SPANS // 2)
                        product(0, at + i + 1, spans=SPANS // 2)
                    if third == 0:
                        pe.wait_ge(dt_loaded, 64)
                        pe.wait_ge(turn, 2)
                        for c in range(TILES):
                            last = pe.transpose(ps_dt[:, c * HEADS:(c + 1) * HEADS], dt_raw[:, c * P:(c + 1) * P],
                                                ident[:HEADS, :HEADS])
                        last.then_inc(turn, 1)
                    if third == 1:
                        pe.wait_ge(turn, 16)
                        pe.matmul(ps_cs, v["tri"][:], v["a"][:], start=True, stop=True)
                        pe.matmul(ps_last, v["ones"][:], v["a"][:], start=True, stop=True).then_inc(turn, 1)

            @block.scalar
            def _(act):
                act.sem_inc(stored[0], 16)
                act.sem_inc(stored[1], 16)
                act.sem_inc(acc_taken[0], 1)
                act.sem_inc(acc_taken[1], 1)
                act.sem_inc(conv_taken, 2)
                act.sem_inc(scaled, 4)
                act.wait_ge(eps_ready, 1)

                def root(n, k):
                    at = slice(k, k + 1)
                    act.wait_ge(summed, n + 1)
                    act.activation(std[:, at], ssum[:, at], ACT.Sqrt, bias=eps[:], scale=1.0 / DM).then_inc(std_made, 1)

                def scale(n, k):
                    at = slice(k, k + 1)
                    act.wait_ge(rstd_made, n + 1)
                    act.wait_ge(h_made, n + 1)
                    act.activation(x_scaled[:, k % 2], x_sb[:, k], ACT.Identity, scale=rstd[:, at]).then_inc(scaled, 1)

                def take_hi(n, k, half):
                    act.wait_ge(tr_made, n + 3)
                    act.activation(tile_of(n, 0, half), tr[:, k % 2].rearrange("p (c t) -> p c t", c=KC),
                                   ACT.Copy).then_inc(hi_made, 1)

                root(0, 0)
                root(1, 1)
                scale(0, 0)
                act.wait_ge(raw_loaded[0], 16)
                act.activation(w_hi[:, 0], raw[:, 0], ACT.Copy).then_inc(hi_ready, 1)
                root(2, 2)
                scale(1, 1)
                for half, passes in enumerate(((0, TILES // 8), (TILES // 8, TILES // 4 - 1))):
                    with act.Fori(*passes) as i:
                        for k in range(4):
                            root(4 * i + 3 + k, (k + 3) % 4)
                            scale(4 * i + 2 + k, (k + 2) % 4)
                            take_hi(4 * i + k, k, half)
                root(TILES - 1, 3)
                for n in range(TILES - 2, TILES):
                    scale(n, n % 4)
                    take_hi(n - 2, n % 4, 1)
                for n in range(TILES - 2, TILES):
                    take_hi(n, n % 4, 1)
                for k in range(2):
                    act.sem_inc(hi_stored[k], 32)
                    act.sem_inc(lo_stored[k], 32)

                def put(slot, use, func, out, n=SEQ):
                    act.wait_ge(acc_made[slot], use + 2)
                    act.wait_ge(stored[slot], 16 * use + 16)
                    act.activation(stage[:, slot, :n], acc[:, slot, :n], func).then_inc(acc_taken[slot], 1)
                    act.wait_ge(acc_taken[slot], use + 2)
                    act.dma_start(out, stage[:, slot, :n]).then_inc(stored[slot], 16)

                def run(kind, func, dest):
                    with act.Fori(0, pairs[kind]) as i:
                        put(1, base[kind] + i, func, dest[bass.ds(2 * i, 1)].rearrange("o p t -> p (o t)"))
                        put(0, base[kind] + i + 1, func, dest[bass.ds(2 * i + 1, 1)].rearrange("o p t -> p (o t)"))

                put(0, 0, ACT.Copy, d["dt"])
                run("z", ACT.Silu, d["z"])
                with act.Fori(0, pairs["xbc"]) as i:
                    for k in range(2):
                        slot, use = 1 - k, base["xbc"] + i + k
                        act.wait_ge(acc_taken[slot], use + 2)
                        act.wait_ge(stored[slot], 16 * use + 16)
                        act.activation(stage[:, slot], work[:, k], ACT.Silu).then_inc(conv_taken, 1)
                        act.wait_ge(conv_taken, 2 * i + k + 3)
                        act.dma_start(d["xbc"][bass.ds(2 * i + k, 1)].rearrange("o p t -> p (o t)"), stage[:, slot]
                                      ).then_inc(stored[slot], 16)
                for g, (_, r) in enumerate(PATTERNS):
                    with act.Fori(0, pairs["q0"]) as i:
                        for k in range(2):
                            slot, use, n = 1 - k, base[f"q{g}"] + i + k, 2 * g + i
                            to = d["qs"][bass.ds(4 * g + 2 * i + k, 1)]
                            act.wait_ge(acc_made[slot], use + 2)
                            if g == 0:
                                act.wait_ge(stored[slot], 16 * (base["q0"] + k) + 16)
                            act.wait_ge(hi_stored[slot], 32 * n + 32)
                            act.activation(stage[:, slot].bitcast(F32R).rearrange("p (r m) -> p r m", r=r),
                                           acc[:, slot].rearrange("p (m r) -> p r m", r=r), ACT.Copy
                                           ).then_inc(q_hi_made, 1)
                            act.wait_ge(q_hi_made, 2 * n + k + 1)
                            for sl in range(2):
                                act.dma_start(to[0, sl, :HDIM], stage[sl * HDIM:(sl + 1) * HDIM, slot]
                                              ).then_inc(hi_stored[slot], 16)
                            act.wait_ge(acc_taken[slot], use + 2)
                            for sl in range(2):
                                act.dma_start(to[0, sl, HDIM:], work[sl * HDIM:(sl + 1) * HDIM, slot]
                                              ).then_inc(lo_stored[slot], 16)
                for k in range(2):
                    act.wait_ge(hi_stored[k], 32 * 7)
                    act.sem_inc(stored[k], 16 * 6)
                run("kv", ACT.Copy, d["kv"])
                run("g", ACT.Silu, d["g"])
                with act.Fori(0, SC // P) as f:
                    use = base["sc"] + 2 * f
                    act.wait_ge(acc_made[1], use + 2)
                    for k in range(2):
                        act.wait_ge(lo_stored[k], 32 * 7)
                    act.wait_ge(sc_done, f + 1)
                    act.activation(work[:, 0], acc[:, 1], ACT.Copy).then_inc(acc_taken[1], 1)
                    act.wait_ge(acc_made[0], use + 4)
                    act.wait_ge(stored[1], 16 * use + 16)
                    act.activation(stage[:, 1], acc[:, 0], ACT.Silu).then_inc(acc_taken[0], 1)
                    act.wait_ge(sc_done, f + 2)
                    act.sem_inc(stored[0], 32)
                    act.sem_inc(stored[1], 16)
                    act.dma_start(d["y_sc"][bass.ds(f, 1)].rearrange("o p t -> p (o t)"), stage[:, 1]
                                  ).then_inc(stored[1], 16)
                for third in range(3):
                    n = pairs["gates"] // 3
                    at = base["gates"] + third * n
                    with act.Fori(0, n) as i:
                        for k in range(2):
                            put(1 - k, at + i + k, ACT.Copy, d["gates"][bass.ds(2 * (third * n + i) + k, 1), :, :HALF
                                                                        ].rearrange("o p t -> p (o t)"), HALF)
                    if third == 0:
                        act.wait_ge(turn, 5)
                        act.activation(t1, t1, ACT.Exp, scale=-1.0).then_inc(turn, 1)
                        act.wait_ge(turn, 7)
                        act.activation(t3, t2, ACT.Ln).then_inc(turn, 1)
                        act.activation(alog_b[:], alog_b[:], ACT.Exp).then_inc(turn, 1)
                    if third == 1:
                        act.wait_ge(turn, 17)
                        act.activation(v["ecs"][:], ps_cs, ACT.Exp).then_inc(turn, 1)
                        act.activation(v["elast"][:], ps_last, ACT.Exp).then_inc(turn, 1)
                        act.wait_ge(turn, 20)
                        act.activation(t1, t0, ACT.Exp).then_inc(turn2, 1)
                act.wait_ge(stored[0], 16 * (n_pairs + 2))
                act.wait_ge(stored[1], 16 * (n_pairs + 1))

            @block.vector
            def _(dve):
                dve.sem_inc(sc_done, 1)
                dve.sem_inc(lo_made, 2)

                def squares(n, k, use):
                    if not (isinstance(n, int) and n == 0):
                        dve.wait_ge(summed, n)
                    wait_alone(dve, x_loaded[k], 16 * use + 16, carried_v)
                    dve.tensor_tensor_reduce(out=squared, in0=x_sb[:, k], in1=x_sb[:, k], scale=1.0, scalar=0.0,
                                             op0=ALU.mult, op1=ALU.add, accum_out=ssum[:, k:k + 1]).then_inc(summed, 1)

                def invert(n, k):
                    at = slice(k, k + 1)
                    dve.wait_ge(std_made, n + 1)
                    dve.reciprocal(rstd[:, at], std[:, at]).then_inc(rstd_made, 1)

                def take_lo(n, k, half):
                    dve.wait_ge(hi_made, n + 1)
                    dve.tensor_tensor(tile_of(n, 1, half), tr[:, k % 2].rearrange("p (c t) -> p c t", c=KC),
                                      tile_of(n, 0, half), ALU.subtract).then_inc(lo_made, 1)

                squares(0, 0, 0)
                for n in range(2):
                    squares(n + 1, n + 1, 0)
                    invert(n, n)
                dve.wait_ge(hi_ready, 1)
                dve.tensor_tensor(w_lo[:, 0], raw[:, 0], w_hi[:, 0].bitcast(F32), ALU.subtract).then_inc(w_made[0], 1)
                squares(3, 3, 0)
                invert(2, 2)
                for half, passes in enumerate(((0, TILES // 8), (TILES // 8, TILES // 4 - 1))):
                    with dve.Fori(*passes) as i:
                        for k in range(4):
                            squares(4 * i + 4 + k, k, i + 1)
                            invert(4 * i + 3 + k, (3 + k) % 4)
                            take_lo(4 * i + k, k, half)
                invert(TILES - 1, 3)
                for n in range(TILES - 4, TILES):
                    take_lo(n, n % 4, 1)
                dve.wait_ge(consts_loaded, 16 * 8)
                with dve.Fori(0, pairs["xbc"]) as i:
                    for k in range(2):
                        slot, use, b = 1 - k, base["xbc"] + i + k, 2 * i + k
                        n = 4 * b
                        dve.wait_ge(acc_made[slot], use + 2)
                        dve.wait_ge(conv_taken, b + 1)
                        dve.tensor_scalar(work[:, k], acc[:, slot], cw[:, bass.ds(b, 1), 3].rearrange("p o -> p o"),
                                          cb[:, bass.ds(b, 1)], ALU.mult, ALU.add).then_inc(conv_step, 1)
                        for tap in range(3):
                            back = 3 - tap
                            dve.wait_ge(conv_step, 3 * b + tap + 1)
                            ins = dve.scalar_tensor_tensor(work[:, k, back:], acc[:, slot, :SEQ - back],
                                                           cw[:, bass.ds(b, 1), tap], work[:, k, back:], ALU.mult,
                                                           ALU.add)
                            ins.then_inc(conv_step if tap < 2 else acc_taken[slot], 1)
                for g, (_, r) in enumerate(PATTERNS):
                    with dve.Fori(0, pairs["q0"]) as i:
                        for k in range(2):
                            slot, use, n = 1 - k, base[f"q{g}"] + i + k, 2 * g + i
                            if g == 0:
                                dve.wait_ge(conv_taken, 2 * 2 * pairs["xbc"] // 2 + 2)
                            dve.wait_ge(lo_stored[slot], 32 * n + 32)
                            dve.wait_ge(q_hi_made, 2 * n + k + 1)
                            dve.tensor_tensor(work[:, slot].bitcast(F32R).rearrange("p (r m) -> p r m", r=r),
                                              acc[:, slot].rearrange("p (m r) -> p r m", r=r),
                                              stage[:, slot].rearrange("p (r m) -> p r m", r=r), ALU.subtract
                                              ).then_inc(acc_taken[slot], 1)
                with dve.Fori(0, SC // P) as f:
                    use = base["sc"] + 2 * f
                    tap = lambda t: scw[:, bass.ds(f, 1), t]
                    dve.wait_ge(acc_made[0], use + 3)
                    dve.wait_ge(acc_taken[1], use + 2)
                    dve.tensor_tensor(work[:, 1], acc[:, 0], work[:, 0], ALU.mult).then_inc(acc_taken[0], 1)
                    dve.wait_ge(acc_taken[0], use + 3)
                    dve.tensor_scalar(work[:, 0], work[:, 1], tap(2), None, ALU.mult).then_inc(sc_step, 1)
                    for back in (1, 2):
                        dve.wait_ge(sc_step, 3 * f + back)
                        dve.scalar_tensor_tensor(work[:, 0, back:], work[:, 1, :SEQ - back], tap(2 - back),
                                                 work[:, 0, back:], ALU.mult, ALU.add).then_inc(sc_step, 1)
                    dve.wait_ge(sc_step, 3 * f + 3)
                    dve.wait_ge(acc_made[1], use + 3)
                    dve.tensor_tensor(work[:, 0], acc[:, 1], work[:, 0], ALU.mult).then_inc(acc_taken[1], 1)
                    dve.wait_ge(acc_taken[1], use + 3)
                    dve.wait_ge(acc_taken[0], use + 4)
                    dve.tensor_tensor(stage[:, 1], stage[:, 1], work[:, 0], ALU.mult).then_inc(sc_done, 1)
                tt, ts, stt = dve.tensor_tensor, dve.tensor_scalar, dve.scalar_tensor_tensor
                chunked = lambda ap: ap.rearrange("p (c h) -> p c h", h=HEADS)
                every = lambda ap: ap.unsqueeze(1).to_broadcast([P, TILES, HEADS])
                dve.wait_ge(turn, 3)
                tt(chunked(t0), chunked(ps_dt), every(bias_b[:]), ALU.add).then_inc(turn, 1)
                dve.wait_ge(turn, 4)
                stt(t1, t0, -1.0, t0, ALU.mult, ALU.max).then_inc(turn, 1)
                dve.wait_ge(turn, 6)
                ts(t2, t1, 1.0, None, ALU.add).then_inc(turn, 1)
                dve.wait_ge(turn, 9)
                ts(t2, t2, -1.0, None, ALU.add).then_inc(turn, 1)
                dve.wait_ge(turn, 10)
                ts(v["dt"][:], t2, 0.0, None, ALU.is_equal).then_inc(turn, 1)
                dve.wait_ge(turn, 11)
                tt(t3, t3, v["dt"][:], ALU.add)
                tt(t2, t2, v["dt"][:], ALU.add).then_inc(turn, 1)
                dve.wait_ge(turn, 12)
                dve.reciprocal(t2, t2)
                tt(t3, t3, t1, ALU.mult).then_inc(turn, 1)
                dve.wait_ge(turn, 13)
                tt(t3, t3, t2, ALU.mult).then_inc(turn, 1)
                dve.wait_ge(turn, 14)
                stt(v["dt"][:], t0, 0.0, t3, ALU.max, ALU.add).then_inc(turn, 1)
                dve.wait_ge(turn, 15)
                stt(chunked(v["a"][:]), chunked(v["dt"][:]), -1.0, every(alog_b[:]), ALU.mult, ALU.mult).then_inc(turn, 1)
                dve.wait_ge(turn, 19)
                dve.tensor_copy(v["cs"][:], ps_cs).then_inc(turn2, 1)
                dve.wait_ge(turn2, 1)
                tt(t0, ps_last, v["cs"][:], ALU.subtract).then_inc(turn, 1)
                dve.wait_ge(turn2, 2)
                tt(v["wdec"][:], v["dt"][:], t1, ALU.mult).then_inc(turn, 1)
        s.clear()


def ssd_gates_stage(nc, w, d, h, wt, v, ident, eps):
    PAIRS, UNITS, ITEMS = TILES // 2, 3 * DM // P, 6
    raw, w_hi, w_lo = wt["raw"], wt["w_hi"], wt["w_lo"]
    dt, cs, ecs, elast, wdec, tri, dskip = (v[n] for n in ("dt", "cs", "ecs", "elast", "wdec", "tri", "dskip"))
    with ExitStack() as stack:
        s = Scope(nc, stack)
        xbc_t = wt["work"][:].rearrange("p k (b t) -> p k b t", t=P)
        z_t = s.sb("s_zt", [P, 2, KC, P])
        x_tok, xdec, xd, sdec, state, yg, y, sq, yn = (
            s.sb("s_" + n, [P, SSM]) for n in ("xtok", "xdec", "xd", "sdec", "state", "yg", "y", "sq", "yn"))
        norm_b = s.sb("s_norm", [P, SSM])
        b_tok = s.sb("s_btok", [P, GROUPS * STATE])
        cs_now = s.sb("s_csnow", [P, 2, HEADS])
        xdt = s.sb("s_xdt", [P, SSM + HDIM])
        cbm = s.sb("s_cbm", [P, GROUPS, P])
        fall = s.sb("s_fall", [P, 2, 4, P])
        decay = s.sb("s_decay", [P, 2, 4, P])
        mix = s.sb("s_mix", [P, 2, 4, P])
        ss, std, rstd = (s.sb(n, [P, GROUPS]) for n in ("s_ss", "s_std", "s_rstd"))
        y_out = s.sb("s_yout", [P, KC, P])
        g_out = s.sb("s_gout", [P, 2, BANK])
        ps_x = s.ps("s_psx", [P, SSM])
        ps_m = s.ps("s_psm", [P, SSM])
        ps_bc = s.ps("s_psbc", [P, BANK])
        ps_y = s.ps("s_psy", [P, 2, 2, GW])
        acc = s.ps("s_acc", [P, BANK])
        loaded, z_loaded, norm_loaded = s.sems("s_loaded", 2), s.sems("s_z_loaded", 2), s.sem("s_norm_loaded")
        x_transposed, b_transposed, cb_ready, z_transposed = (
            s.sem(n) for n in ("s_xT", "s_bT", "s_cb", "s_zT"))
        x_tok_ready, b_tok_ready, cbm_ready, yo_ready, skip_added, sdec_ready = (
            s.sem(n) for n in ("s_xtok_r", "s_btok_r", "s_cbm_r", "s_yo_r", "s_skip_r", "s_sdec_r"))
        cs_ready, xdt_ready, xdec_ready, squared, bc_ready, std_made, rstd_made, yn_made, out_made = (
            s.sem(n) for n in ("s_cs_r", "s_xdt_r", "s_xdec_r", "s_sq_r", "s_bc_r", "s_std_r", "s_rstd_r", "s_yn_r",
                               "s_out_r"))
        stored, carried = s.sem("s_stored"), s.sem("s_carried")
        raw_loaded, w_hi_made, g_stored = s.sem("s_raw_loaded"), s.sem("s_whi_r"), s.sems("s_g_stored", 2)
        y_made = s.sem("s_y_made")
        decay_made = s.sem("s_decay_made")
        fall_made = s.sem("s_fall_made")
        mix_made = s.sem("s_mix_made")
        y_taken = s.sem("s_y_taken")
        update_made = s.sem("s_update_made")
        gated = s.sem("s_gated")
        xd_made = s.sem("s_xd_made")
        out_taken = s.sem("s_out_taken")
        state_made = s.sem("s_state_made")
        w_made = s.sem("s_w_made")
        item_made = s.sem("s_item_made")
        item_taken = s.sem("s_item_taken")

        def heads(ap):
            return ap.rearrange("p (h q) -> p h q", q=HDIM)

        def spread(ap, n, width=HDIM):
            return ap.unsqueeze(2).to_broadcast([P, n, width])

        with nc.Block() as block:

            @block.sync
            def _(sp):
                def load_chunk(c, k, first=False):
                    at = bass.ds(c * P, P)
                    if not first:
                        sp.dma_start(xbc_t[:, k], d["xbc"][:, :, at].rearrange("b p t -> p b t")).then_inc(loaded[k], 16)
                    sp.dma_start(z_t[:, k], d["z"][:, :, at].rearrange("b p t -> p b t")).then_inc(z_loaded[k], 16)

                def load_unit(u):
                    sp.wait_ge(w_made, u)
                    sp.dma_start(raw[:, 0], w["w_in"][0, :, bass.ds(C_MERGE + P * u, P)].rearrange(
                        "(c p) n -> p c n", p=P)).then_inc(raw_loaded, 16)

                def store_item(i, j):
                    sp.wait_ge(item_taken, ITEMS * i + j + 2)
                    sp.dma_start(d["gates"][bass.ds(3 * i + j // 2, 1), :, HALF + j % 2 * BANK:HALF + (j % 2 + 1) * BANK
                                            ].rearrange("o p t -> p (o t)"), g_out[:, j % 2]
                                 ).then_inc(g_stored[j % 2], 16)

                def chunks(i, last):
                    for k in range(2):
                        c = 2 * i + k
                        if not (last and k):
                            sp.wait_ge(y_made, 4 * c + 8)
                            load_chunk(c + 1, 1 - k)
                            load_unit(3 * i + 2 + k)
                        store_item(i, 3 * k)
                        store_item(i, 3 * k + 1)
                        if k and not last:
                            load_unit(3 * i + 4)
                        store_item(i, 3 * k + 2)
                        sp.wait_ge(out_taken, c + 2)
                        sp.dma_start(d["y_ssm"][:, :, bass.ds(c * P, P)].rearrange("b p t -> p b t"), y_out[:]
                                     ).then_inc(stored, 16)

                load_chunk(0, 0, first=True)
                sp.dma_start(norm_b[:], w["ssm_norm"][0:1, :].to_broadcast([P, SSM])).then_inc(norm_loaded, 16)
                with sp.Fori(0, PAIRS - 1) as i:
                    chunks(i, False)
                chunks(PAIRS - 1, True)
                sp.wait_ge(stored, 16 * TILES + 16)
                for j in range(2):
                    sp.wait_ge(g_stored[j], 16 * UNITS + 16)

            @block.gpsimd
            def _(pool):
                def take_cs(c, k):
                    wait_alone(pool, y_made, 4 * c + 4, carried)
                    pool.tensor_copy(cs_now[:, k], cs[:, bass.ds(c * HEADS, HEADS)]).then_inc(cs_ready, 1)

                def split(u, slot):
                    pool.wait_ge(raw_loaded, 16 * u - 16)
                    wait_alone(pool, item_made, 2 * u, carried)
                    pool.tensor_copy(w_hi[:, slot], raw[:, 0]).then_inc(w_hi_made, 1)
                    pool.wait_ge(w_hi_made, u)
                    pool.tensor_tensor(w_lo[:, slot], raw[:, 0], w_hi[:, slot], ALU.subtract).then_inc(w_made, 1)

                def chunks(i, last):
                    for k in range(2):
                        c = 2 * i + k
                        at = bass.ds(c * HEADS, HEADS)
                        wait_alone(pool, x_tok_ready, c + 1, carried)
                        pool.tensor_tensor(heads(xdt[:, :SSM]), heads(x_tok[:]), spread(dt[:, at], HEADS), ALU.mult
                                           ).then_inc(xdt_ready, 1)
                        if not (last and k):
                            take_cs(c + 1, 1 - k)
                        wait_alone(pool, state_made, c + 1, carried)
                        pool.tensor_tensor(heads(sdec[:]), heads(state[:]), spread(elast[:, at], HEADS), ALU.mult
                                           ).then_inc(sdec_ready, 1)
                        wait_alone(pool, update_made, c + 1, carried)
                        pool.tensor_tensor(heads(xdec[:]), heads(x_tok[:]), spread(wdec[:, at], HEADS), ALU.mult
                                           ).then_inc(xdec_ready, 1)
                        pool.wait_ge(gated, c + 1)
                        pool.tensor_tensor(heads(xd[:]), heads(x_tok[:]), spread(dskip[:], HEADS), ALU.mult
                                           ).then_inc(xd_made, 1)
                        if k == 0:
                            split(3 * i + 2, 1)
                        elif not last:
                            split(3 * i + 3, 2)
                            split(3 * i + 4, 0)

                pool.sem_inc(xd_made, 1)
                pool.memset(xdt[:, SSM:], 0.0)
                pool.memset(state[:], 0.0).then_inc(state_made, 1)
                pool.tensor_copy(cs_now[:, 0], cs[:, :HEADS]).then_inc(cs_ready, 1)
                with pool.Fori(0, PAIRS - 1) as i:
                    chunks(i, False)
                chunks(PAIRS - 1, True)

            @block.tensor
            def _(pe):
                pe.sem_inc(y_made, 8)
                pe.sem_inc(update_made, 1)
                pe.sem_inc(item_made, 4)
                flat_y = ps_y[:].rearrange("p b a q -> p b (a q)")
                acc_tiled = acc[:].rearrange("p (n t) -> p n t", t=P)
                with pe.Fori(0, PAIRS) as i:
                    for k in range(2):
                        c = 2 * i + k
                        b_t, c_t = xbc_t[:, k, 8:12], xbc_t[:, k, 12:16]

                        def gates(half):
                            j, part = 3 * k + half // 2, half % 2
                            slot, first = (j // 2 + 2) % 3, 4 * (j % 2)
                            if part == 0:
                                if j % 2 == 0:
                                    pe.wait_ge(w_made, 3 * i + j // 2 + 1)
                                pe.wait_ge(item_taken, ITEMS * i + j + 1)
                            for b in range(4 * part, 4 * part + 4):
                                hi, lo = (h[:, first:first + 4, q, b] for q in range(2))
                                pe.matmul(acc_tiled, w_hi[:, slot, b], hi, start=b == 0, stop=False)
                                pe.matmul(acc_tiled, w_hi[:, slot, b], lo, start=False, stop=False)
                                last = pe.matmul(acc_tiled, w_lo[:, slot, b], hi, start=False, stop=b == KC - 1)
                            if part == 1:
                                last.then_inc(item_made, 1)

                        def running_sums(g):
                            pe.wait_ge(fall_made, 4 * c + g + 2)
                            for j in range(4):
                                at = 4 * g + j
                                last = pe.transpose(ps_bc[:, j * P:(j + 1) * P],
                                                    cs_now[:, k, at:at + 1].to_broadcast([P, P]), ident[:])
                            last.then_inc(bc_ready, 1)

                        def group(g):
                            pe.wait_ge(mix_made, 4 * c + g + 3)
                            pe.wait_ge(y_taken, 4 * c + g + 1)
                            for j in range(4):
                                at = slice(j * HDIM, (j + 2) * HDIM)
                                pe.matmul(flat_y[:, g % 2, at], mix[:, g % 2, j], xdt[:, g * GW + j * HDIM:
                                          g * GW + (j + 2) * HDIM], start=True, stop=True)
                            pe.matmul(ps_y[:, g % 2, 1], c_t[:, g], state[:, g * GW:(g + 1) * GW], start=True,
                                      stop=True).then_inc(y_made, 1)

                        pe.wait_ge(loaded[k], 16 * i + 16)
                        pe.wait_ge(gated, c + 1)
                        for b in range(KC):
                            last = pe.transpose(ps_x[:, b * P:(b + 1) * P], xbc_t[:, k, b], ident[:])
                        last.then_inc(x_transposed, 1)
                        pe.wait_ge(out_taken, c + 1)
                        for g in range(GROUPS):
                            last = pe.transpose(ps_m[:, g * P:(g + 1) * P], b_t[:, g], ident[:])
                        last.then_inc(b_transposed, 1)
                        pe.wait_ge(cs_ready, c + 1)
                        running_sums(0)
                        for g in range(GROUPS):
                            last = pe.matmul(ps_m[:, BANK + g * P:BANK + (g + 1) * P], b_t[:, g], c_t[:, g],
                                             start=True, stop=True)
                        last.then_inc(cb_ready, 1)
                        gates(0)
                        pe.wait_ge(z_loaded[k], 16 * i + 16)
                        pe.wait_ge(x_tok_ready, c + 1)
                        for b in range(KC):
                            last = pe.transpose(ps_x[:, b * P:(b + 1) * P], z_t[:, k, b], ident[:])
                        last.then_inc(z_transposed, 1)
                        running_sums(1)
                        pe.wait_ge(xdt_ready, c + 1)
                        pe.wait_ge(state_made, c + 1)
                        group(0)
                        gates(1)
                        running_sums(2)
                        group(1)
                        running_sums(3)
                        gates(2)
                        group(2)
                        group(3)
                        gates(3)
                        pe.wait_ge(b_tok_ready, c + 1)
                        pe.wait_ge(xdec_ready, c + 1)
                        pe.wait_ge(cbm_ready, c + 1)
                        for g in range(GROUPS):
                            last = pe.matmul(ps_m[:, g * GW:(g + 1) * GW], b_tok[:, g * P:(g + 1) * P],
                                             xdec[:, g * GW:(g + 1) * GW], start=True, stop=True)
                        last.then_inc(update_made, 1)
                        gates(4)
                        gates(5)
                        pe.wait_ge(yn_made, c + 1)
                        pe.wait_ge(state_made, c + 2)
                        for b in range(KC):
                            last = pe.transpose(ps_m[:, b * P:(b + 1) * P], yn[:, b * P:(b + 1) * P], ident[:])
                        last.then_inc(out_made, 1)

            @block.scalar
            def _(act):
                act.sem_inc(decay_made, 2)
                act.sem_inc(fall_made, 2)
                act.sem_inc(out_taken, 1)
                act.sem_inc(stored, 16)
                act.sem_inc(item_taken, 1)
                act.sem_inc(loaded[0], 16)
                act.activation(w_hi[:, 0], raw[:, 0], ACT.Copy).then_inc(w_hi_made, 1)
                for j in range(2):
                    act.sem_inc(g_stored[j], 16)

                with act.Fori(0, PAIRS) as i:
                    for k in range(2):
                        c = 2 * i + k

                        def take_item(j):
                            act.wait_ge(item_made, ITEMS * i + j + 5)
                            act.wait_ge(g_stored[j % 2], 48 * i + 16 * (j // 2) + 16)
                            act.activation(g_out[:, j % 2], acc[:], ACT.Copy).then_inc(item_taken, 1)

                        def decays(g):
                            act.wait_ge(bc_ready, 4 * c + g + 1)
                            act.wait_ge(mix_made, 4 * c + g + 1)
                            for j in range(4):
                                last = act.activation(fall[:, g % 2, j], ps_bc[:, j * P:(j + 1) * P], ACT.Relu,
                                                      bias=cs[:, bass.ds(c * HEADS + 4 * g + j, 1)], scale=-1.0)
                            last.then_inc(fall_made, 1)
                            act.wait_ge(fall_made, 4 * c + g + 3)
                            act.activation(decay[:, g % 2], fall[:, g % 2], ACT.Exp, scale=-1.0).then_inc(decay_made, 1)

                        act.wait_ge(x_transposed, c + 1)
                        act.wait_ge(xd_made, c + 1)
                        act.activation(x_tok[:], ps_x[:], ACT.Copy).then_inc(x_tok_ready, 1)
                        act.wait_ge(b_transposed, c + 1)
                        act.wait_ge(update_made, c + 1)
                        act.activation(b_tok[:], ps_m[:, :BANK], ACT.Copy).then_inc(b_tok_ready, 1)
                        decays(0)
                        decays(1)
                        take_item(3 * k)
                        decays(2)
                        decays(3)
                        take_item(3 * k + 1)
                        act.wait_ge(gated, c + 2)
                        for g in range(GROUPS):
                            at = slice(g * GW, (g + 1) * GW)
                            last = act.activation(sq[:, at], yg[:, at], ACT.Square, accum_out=ss[:, g:g + 1])
                        last.then_inc(squared, 1)
                        act.wait_ge(squared, c + 1)
                        act.activation(std[:], ss[:], ACT.Sqrt, bias=eps[:], scale=1.0 / GW).then_inc(std_made, 1)
                        take_item(3 * k + 2)
                        act.wait_ge(out_made, c + 1)
                        act.wait_ge(stored, 16 * c + 16)
                        act.activation(y_out[:], ps_m[:].rearrange("p (b t) -> p b t", t=P), ACT.Copy
                                       ).then_inc(out_taken, 1)

            @block.vector
            def _(dve):
                dve.sem_inc(mix_made, 2)
                dve.sem_inc(y_taken, 2)
                dve.sem_inc(gated, 1)
                dve.sem_inc(w_made, 1)
                dve.wait_ge(w_hi_made, 1)
                dve.tensor_tensor(w_lo[:, 0], raw[:, 0], w_hi[:, 0].bitcast(F32), ALU.subtract).then_inc(w_made, 1)
                dve.wait_ge(norm_loaded, 16)
                tt, stt = dve.tensor_tensor, dve.scalar_tensor_tensor
                with dve.Fori(0, PAIRS) as i:
                    for k in range(2):
                        c = 2 * i + k
                        dve.wait_ge(cb_ready, c + 1)
                        tt(cbm[:], ps_m[:, BANK:].rearrange("p (g l) -> p g l", l=P),
                           tri[:].unsqueeze(1).to_broadcast([P, GROUPS, P]), ALU.mult).then_inc(cbm_ready, 1)
                        dve.wait_ge(cbm_ready, c + 1)

                        def combine(g):
                            dve.wait_ge(decay_made, 4 * c + g + 3)
                            dve.wait_ge(y_made, 4 * c + g + 7)
                            tt(mix[:, g % 2], decay[:, g % 2], cbm[:, g].unsqueeze(1).to_broadcast([P, 4, P]),
                               ALU.mult).then_inc(mix_made, 1)

                        def take(g):
                            at = slice(g * GW, (g + 1) * GW)
                            dve.wait_ge(y_made, 4 * c + g + 9)
                            tt(heads(y[:, at]), heads(ps_y[:, g % 2, 1]), spread(ecs[:, bass.ds(c * HEADS + 4 * g, 4)], 4),
                               ALU.mult).then_inc(yo_ready, 1)
                            dve.wait_ge(yo_ready, 4 * c + g + 1)
                            tt(y[:, at], ps_y[:, g % 2, 0], y[:, at], ALU.add).then_inc(y_taken, 1)

                        combine(0)
                        combine(1)
                        take(0)
                        combine(2)
                        take(1)
                        combine(3)
                        take(2)
                        take(3)
                        dve.wait_ge(y_taken, 4 * c + 6)
                        dve.wait_ge(xd_made, c + 2)
                        tt(y[:], y[:], xd[:], ALU.add).then_inc(skip_added, 1)
                        dve.wait_ge(skip_added, c + 1)
                        dve.wait_ge(z_transposed, c + 1)
                        tt(yg[:], ps_x[:], y[:], ALU.mult).then_inc(gated, 1)
                        dve.wait_ge(sdec_ready, c + 1)
                        dve.wait_ge(update_made, c + 2)
                        tt(state[:], ps_m[:], sdec[:], ALU.add).then_inc(state_made, 1)
                        dve.wait_ge(std_made, c + 1)
                        dve.reciprocal(rstd[:], std[:]).then_inc(rstd_made, 1)
                        dve.wait_ge(rstd_made, c + 1)
                        for g in range(GROUPS):
                            at = slice(g * GW, (g + 1) * GW)
                            last = stt(yn[:, at], yg[:, at], rstd[:, g:g + 1], norm_b[:, at], ALU.mult, ALU.mult)
                        last.then_inc(yn_made, 1)


def load_first_block(sp, w, d, raw, y_lo, loaded):
    for c in range(8):
        sp.dma_start(y_lo[c].bitcast(F32), d["y_ssm"][c, :, :HALF]).then_inc(loaded, 16)
    for p, at, n in (("p_ssm", 0, 8), ("p_sc", 8, 4)):
        sp.dma_start(raw[:, at:at + n], w[p][0, :, :P].rearrange("(c p) n -> p c n", p=P)).then_inc(loaded, 16)


def attention_stage(nc, w, d, ident, raw, y_lo):
    NB, PAIRS = TILES, SLOTS // 2
    dil = [x[1] for x in PATTERNS]
    blocks = [[(r, n) for r in range(x) for n in range(SEQ // x // P)] for x in dil]
    steps = [(g, sl, b) for sl in range(2) for g in range(3) for b in range(0, NB, 2)]
    NS, NV = len(steps), 12
    SPAN = NB // 2
    TURNS = (NS + NV) // 2
    stores = [1, dil[1], 1]
    with ExitStack() as stack:
        s = Scope(nc, stack)
        q_s = s.sb("a_q", [P, 3, SEQ], F32R)
        k_raw, v_t = s.sb("a_kraw", [P, SEQ]), s.sb("a_v", [P, SEQ])
        k_hi, k_lo = s.sb("a_khi", [P, 3, SEQ], F32R), s.sb("a_klo", [P, 3, SEQ], F32R)
        v_tok = s.sb("a_vt", [P, 3, NB, P])
        band = s.sb("a_band", [P, 2, P])
        zero = s.sb("a_zero", [P, 2, P])
        scores = s.sb("a_scores", [P, 4, 2, 2 * P])
        probs = s.sb("a_probs", [P, 4, 2, 2 * P])
        probs_t = s.sb("a_probst", [P, 4, 4, P])
        neg = s.sb("a_neg", [P, 4, 2])
        att = s.sb("a_att", [P, 3, NB, PAIR + 4])
        ps_s = s.ps("a_pss", [P, 2, 2, 2 * P])
        ps_t = s.ps("a_pst", [P, 4, 4, P])
        ps_o = s.ps("a_pso", [P, 2, 4, P])
        q_loaded = s.sems("a_q_loaded", 3)
        next_loaded = s.sem("a_next_loaded")
        k_loaded, v_loaded, band_turn = s.sem("a_k_loaded"), s.sem("a_v_loaded"), s.sem("a_band_turn")
        k_hi_made, v_turned, negated = (s.sem(n) for n in ("a_khi_r", "a_vT", "a_neg_r"))
        k_made = s.sem("a_k_made")
        s_made = s.sem("a_s_made")
        masked = s.sem("a_masked")
        exped = s.sem("a_exped")
        p_turned = s.sem("a_pT")
        t_taken = s.sems("a_t_taken", 2)
        o_made = s.sem("a_o_made")
        o_taken = s.sem("a_o_taken")
        stored = s.sems("a_stored", 3)
        carried = s.sem("a_carried")

        def width(g, b):
            return (1 if blocks[g][b][1] == 0 else 2) * P

        def strided(ap, g):
            return ap.rearrange("p (m r) -> p r m", r=dil[g])

        def residues(ap, g):
            return ap.rearrange("p (r m) -> p r m", r=dil[g])

        def evacuate(eng, parity, copy, i, j):
            eng.wait_ge(p_turned, NS * i + j + 5)
            eng.wait_ge(o_made, NS * i + j + 1)
            n = NV + j
            g, sl, b = steps[j]
            if width(g, b) == width(g, b + 1) == 2 * P:
                copy(probs_t[:, j % 4], ps_t[:, n % 4]).then_inc(t_taken[parity], 1)
            elif width(g, b + 1) == P:
                copy(probs_t[:, j % 4, 1::2], ps_t[:, n % 4, 1::2]).then_inc(t_taken[parity], 1)
            else:
                copy(probs_t[:, j % 4, 1:], ps_t[:, n % 4, 1:]).then_inc(t_taken[parity], 1)

        def evacuate_v(eng, parity, copy, i):
            eng.wait_ge(o_made, NS * i + 4)
            for n in range(parity, NV, 2):
                eng.wait_ge(v_turned, NV * i + n + 1)
                copy(v_tok[:, n // 4, n % 4 * 4:n % 4 * 4 + 4], ps_t[:, n % 4]).then_inc(t_taken[parity], 1)

        def scored(unit, g):
            return NS // 2 * unit + SPAN * (g + 1) + NS // 2

        def split_hi(act, unit, g):
            act.wait_ge(k_loaded, 32 * unit + 32)
            act.wait_ge(s_made, scored(unit, g))
            act.activation(residues(k_hi[:, g], g), strided(k_raw[:], g), ACT.Copy).then_inc(k_hi_made, 1)

        def split_lo(pool, unit, g):
            pool.wait_ge(k_hi_made, 3 * unit + g + 1)
            pool.tensor_tensor(residues(k_lo[:, g], g), strided(k_raw[:], g), residues(k_hi[:, g].bitcast(F32), g),
                               ALU.subtract).then_inc(k_made, 1)

        with nc.Block() as block:

            @block.sync
            def _(sp):
                def load_k(pair, sl, unit):
                    sp.wait_ge(k_made, 3 * unit + 1)
                    for half in range(2):
                        sp.dma_start(k_raw[HDIM * half:HDIM * (half + 1)], d["kv"][
                            bass.ds(pair, 1), HDIM * sl:HDIM * (sl + 1)].rearrange("o p t -> p (o t)")
                            ).then_inc(k_loaded, 16)

                def load_q(pair, sl, unit, g):
                    sp.wait_ge(s_made, scored(unit, g))
                    sp.dma_start(q_s[:, g].bitcast(F32), d["qs"][bass.ds(4 * g + pair, 1), sl].rearrange(
                        "o p t -> p (o t)")).then_inc(q_loaded[g], 16)

                def store(i, g):
                    sp.wait_ge(o_taken, 24 * i + 12 + 4 * g + 6)
                    to = d["att"][g, :, bass.ds(i, 1)]
                    for r in range(stores[g]):
                        if g == 1:
                            n = NB // dil[1]
                            sp.dma_start(to.rearrange("(n p r) o q -> r p n (o q)", p=P, r=dil[1])[r],
                                         att[:, g, r * n:(r + 1) * n]
                                         ).then_inc(stored[g], 16)
                        else:
                            order = "(n p) o q -> p n (o q)" if g == 0 else "(p n) o q -> p n (o q)"
                            sp.dma_start(to.rearrange(order, p=P), att[:, g]
                                         ).then_inc(stored[g], 16)

                sp.wait_ge(s_made, NS)
                load_k(0, 0, 0)
                sp.dma_start(v_t[:], d["kv"][4]).then_inc(v_loaded, 16)
                for g in range(3):
                    load_q(0, 0, 0, g)
                load_first_block(sp, w, d, raw, y_lo, next_loaded)
                with sp.Fori(0, PAIRS) as i:
                    following = (i + 1) % PAIRS
                    sp.wait_ge(v_turned, NV * i + NV)
                    sp.dma_start(v_t[:], d["kv"][bass.ds(4 + following, 1)].rearrange("o p t -> p (o t)")
                                 ).then_inc(v_loaded, 16)
                    load_k(i, 1, 2 * i + 1)
                    for g in range(3):
                        load_q(i, 1, 2 * i + 1, g)
                    load_k(following, 0, 2 * i + 2)
                    for g in range(3):
                        load_q(following, 0, 2 * i + 2, g)
                        store(i, g)
                for g in range(3):
                    sp.wait_ge(stored[g], 16 * stores[g] * (PAIRS + 1))
                    sp.wait_ge(q_loaded[g], 16 * (2 * PAIRS + 1))
                sp.wait_ge(v_loaded, 16 * (PAIRS + 1))
                sp.wait_ge(next_loaded, 160)
                sp.wait_ge(k_loaded, 32 * (2 * PAIRS + 1))

            @block.gpsimd
            def _(pool):
                pool.sem_inc(k_made, 1)
                pool.memset(zero[:], 0.0).then_inc(band_turn, 1)
                pool.wait_ge(band_turn, 1)
                pool.affine_select(out=band[:, 0], in_=zero[:, 0], compare_op=ALU.is_ge, fill=NEG, base=0,
                                   pattern=[[1, P]], channel_multiplier=-1).then_inc(band_turn, 1)
                pool.affine_select(out=band[:, 1], in_=zero[:, 1], compare_op=ALU.is_ge, fill=NEG, base=0,
                                   pattern=[[-1, P]], channel_multiplier=1).then_inc(band_turn, 1)
                with pool.Fori(0, 2 * PAIRS + 1) as unit:
                    for g in range(3):
                        split_lo(pool, unit, g)

            @block.tensor
            def _(pe):
                pe.sem_inc(s_made, NS)
                pe.sem_inc(p_turned, 4)
                pe.sem_inc(o_made, 4)
                with pe.Fori(0, PAIRS) as i:
                    pe.wait_ge(v_loaded, 16 * i + 16)
                    for n in range(NV):
                        g = n // 4
                        pe.wait_ge(t_taken[n % 2], TURNS * i + n // 2 + 1)
                        for b in range(4):
                            r, m = blocks[g][n % 4 * 4 + b]
                            last = pe.transpose(ps_t[:, n % 4, b], strided(v_t[:], g)[:, r, m * P:(m + 1) * P], ident[:])
                        last.then_inc(v_turned, 1)

                    def score(j):
                        g, sl, b = steps[j]
                        if b == 0:
                            pe.wait_ge(q_loaded[g], 32 * i + 16 * sl + 16)
                            pe.wait_ge(k_made, 6 * i + 3 * sl + g + 2)
                        pe.wait_ge(masked, NS * i + j + 1)
                        bank = ps_s[:, j % 2].rearrange("p e k -> p (e k)")
                        for e in range(2):
                            at = (b + e) * P
                            to, keys = (e * 2 * P, at - P) if at else (P, 0)
                            for k, first in ((k_hi, True), (k_lo, False)):
                                last = pe.matmul(bank[:, to:to + 2 * P], q_s[:, g, at:at + P],
                                                 k[:, g, keys:keys + 2 * P], start=first, stop=not first)
                        last.then_inc(s_made, 1)

                    def turn(j):
                        g, sl, b = steps[j]
                        pe.wait_ge(exped, NS * i + j + 5)
                        pe.wait_ge(t_taken[j % 2], TURNS * i + (NV + j) // 2 + 1)
                        for e in range(2):
                            for h in range(2 - width(g, b + e) // P, 2):
                                last = pe.transpose(ps_t[:, (NV + j) % 4, 2 * e + h], probs[:, j % 4, e, h * P:(h + 1) * P],
                                                    ident[:])
                        last.then_inc(p_turned, 1)

                    def output(j):
                        g, sl, b = steps[j]
                        if j == 0:
                            pe.wait_ge(t_taken[1], TURNS * i + NV // 2 + 2)
                        pe.wait_ge(t_taken[j % 2], TURNS * i + (NV + j) // 2 + 3)
                        if j % 2 == 0:
                            pe.wait_ge(o_taken, 24 * i + j // 2 + 1)
                        for e in range(2):
                            first = 2 - width(g, b + e) // P
                            for h in range(first, 2):
                                last = pe.matmul(ps_o[:, j // 2 % 2, (b + e) % 4], probs_t[:, j % 4, 2 * e + h],
                                                 v_tok[:, g, b + e - 1 + h], start=h == first, stop=h == 1)
                        last.then_inc(o_made, 1)

                    for j in range(NS + 4):
                        if j < NS:
                            score(j)
                        if 2 <= j < NS + 2:
                            turn(j - 2)
                        if j >= 4:
                            output(j - 4)

            @block.scalar
            def _(act):
                act.sem_inc(exped, 4)
                act.sem_inc(t_taken[1], 2)
                copy = lambda to, of: act.activation(to, of, ACT.Copy)
                for g in range(3):
                    split_hi(act, 0, g)
                with act.Fori(0, PAIRS) as i:
                    evacuate_v(act, 1, copy, i)
                    for j in range(NS + 2):
                        if j < NS:
                            g, sl, b = steps[j]
                            act.wait_ge(negated, NS * i + j + 1)
                            act.wait_ge(p_turned, NS * i + j + 1)
                            if j % SPAN == 0:
                                act.wait_ge(stored[g], 16 * stores[g] * (i + 1))
                            for e in range(2):
                                n = width(g, b + e)
                                last = act.activation(probs[:, j % 4, e, 2 * P - n:], scores[:, j % 4, e, 2 * P - n:],
                                                      ACT.Exp, bias=neg[:, j % 4, e:e + 1], scale=HDIM ** -0.5,
                                                      accum_out=att[:, g, b + e, PAIR + 2 + sl:PAIR + 3 + sl])
                            last.then_inc(exped, 1)
                            if j % SPAN == 2 and j > SPAN:
                                unit, of = divmod(j // SPAN - 1, 3)
                                split_hi(act, 2 * i + unit + 1, of)
                        if j >= 2 and j % 2:
                            evacuate(act, 1, copy, i, j - 2)
                    split_hi(act, 2 * i + 2, 2)

            @block.vector
            def _(dve):
                dve.sem_inc(masked, 2)
                dve.sem_inc(t_taken[0], 2)
                dve.sem_inc(o_taken, 2)
                for g in range(3):
                    dve.sem_inc(stored[g], 16 * stores[g])
                dve.wait_ge(band_turn, 3)
                keys = band[:].rearrange("p a k -> p (a k)")
                with dve.Fori(0, PAIRS) as i:
                    evacuate_v(dve, 0, dve.tensor_copy, i)
                    for j in range(NS + 5):
                        if j < NS:
                            g, sl, b = steps[j]
                            if j % SPAN == 0:
                                dve.wait_ge(stored[g], 16 * stores[g] * (i + 1))
                            dve.wait_ge(exped, NS * i + j + 1)
                            wait_alone(dve, s_made, NS * i + j + 1 + NS, carried)
                            for e in range(2):
                                n = width(g, b + e)
                                last = dve.tensor_tensor_reduce(
                                    out=scores[:, j % 4, e, 2 * P - n:], in0=ps_s[:, j % 2, e, 2 * P - n:],
                                    in1=keys[:, 2 * P - n:], scale=1.0, scalar=NEG, op0=ALU.add, op1=ALU.max,
                                    accum_out=att[:, g, b + e, PAIR + sl:PAIR + 1 + sl])
                            last.then_inc(masked, 1)
                            dve.wait_ge(masked, NS * i + j + 3)
                            dve.tensor_scalar(neg[:, j % 4], att[:, g, b:b + 2, PAIR + sl], -HDIM ** -0.5, None, ALU.mult
                                              ).then_inc(negated, 1)
                        if 2 <= j < NS + 2 and j % 2 == 0:
                            evacuate(dve, 0, dve.tensor_copy, i, j - 2)
                        if j >= 6 and j % 2 == 0:
                            grp = j // 2 - 3
                            g, sl, b = steps[2 * grp]
                            dve.wait_ge(o_made, NS * i + 2 * grp + 6)
                            dve.tensor_copy(att[:, g, b:b + 4, sl * HDIM:(sl + 1) * HDIM], ps_o[:, grp % 2, :, HDIM * sl:HDIM * (sl + 1)]
                                            ).then_inc(o_taken, 1)


BRANCHES = [("y_ssm", "p_ssm", 0, 8), ("y_sc", "p_sc", 8, 4), ("y_attn", "p_attn", 12, 4)]


def merge_branches_stage(nc, w, d, ident, raw, y_lo_of_ssd):
    NM, UNITS, LATE, FULL, SECOND = DM // P, 20, 4, 8, 12
    with ExitStack() as stack:
        s = Scope(nc, stack)
        y_hi, y_lo_of_rest = s.sb("b_yhi", [P, 16, HALF], F32R), s.sb("b_ylo", [P, 8, HALF], F32R)
        w_hi, w_lo = s.sb("b_whi", [P, 2, 16, P], F32R), s.sb("b_wlo", [P, 2, 16, P], F32R)
        gate = s.sb("b_gate", [P, 3, HALF])
        total = s.sb("b_total", [P, 2, HALF])
        att = s.sb("b_att", [P, 2, 3, SLOTS // 2, PAIR + 4])
        top = s.sb("b_top", [P, 2, SLOTS])
        low = s.sb("b_low", [P, 2, 3, SLOTS])
        ex = s.sb("b_ex", [P, 2, 3, SLOTS])
        den = s.sb("b_den", [P, 2, SLOTS])
        g_t = s.sb("b_gt", [P, KV // P, 2 * P])
        acc = s.ps("b_acc", [P, 3, HALF])
        ps = s.ps("b_ps", [P, KV // P, 2 * P])
        y_lo = y_lo_of_ssd + [y_lo_of_rest[:, c] for c in range(8)]
        y_raw = [lo.bitcast(F32) for lo in y_lo]
        att_loaded, g_loaded, low_made, ex_made, step, ex_scaled, part_made, part2_made, o_half, o_made, ya_hi_made = (
            s.sem("b_" + n) for n in ("att_loaded", "g_loaded", "low_r", "ex_r", "step", "exs_r", "part_r", "part2_r",
                                      "ohalf_r", "o_r", "yahi_r"))
        y_loaded = s.sems("b_y_loaded", 4)
        gate_loaded, gate_made, acc_made = (s.sems("b_" + n, 3) for n in ("gate_loaded", "gate_r", "acc_r"))
        partial_loaded, raw_loaded, w_hi_made, w_made = (
            s.sems("b_partial_loaded", 2), s.sem("b_raw_loaded"), s.sem("b_whi_r"), s.sem("b_w_r"))
        y_hi_made, y0_made, y1_made = (s.sem("b_" + n) for n in ("yhi_r", "y0_r", "y1_r"))
        turned = s.sem("b_turned")
        gated = s.sem("b_gated")
        ya_made = s.sem("b_ya_r")
        y_stored = s.sem("b_y_stored")
        summed = s.sem("b_summed")
        acc_taken = s.sems("b_acc_taken", 3)
        stored = s.sems("b_stored", 2)

        late_loaded = s.sems("b_late_loaded", 4)
        o1_half, o1_made = s.sem("b_o1half_r"), s.sem("b_o1_r")

        def halves(t, g):
            return att[:, t, g, :, :PAIR].rearrange("p a (s q) -> p a s q", q=HDIM)

        def share(t, g):
            return ex[:, t, g].rearrange("p (a s) -> p a s", s=2).unsqueeze(3).to_broadcast([P, SLOTS // 2, 2, HDIM])

        def chunks_of(u):
            return slice(0, 12) if u < LATE else slice(12, 16) if u < FULL else slice(0, 16)

        def raw_of(u, at):
            turn = 4 * (u - LATE + 1) % 16 if LATE <= u < FULL else 0
            return raw[:, turn - 4:turn] if turn else raw[:, at]

        def lanes(u, k):
            return [(0, 0), (1, 1)] if u < LATE else [(k, 2)] if u < FULL else [(0, 0), (1, 1), (2, 2)]

        def raw_count(u):
            return 32 * u if u < LATE else 48 * u - 240

        with nc.Block() as block:

            @block.sync
            def _(sp):
                def load_weights(first, u):
                    sp.wait_ge(w_made, LATE if first == LATE else u)
                    m = u - (0 if first == 0 else LATE if first < SECOND else SECOND)
                    for _, p, at, n in BRANCHES:
                        if chunks_of(first).start <= at < chunks_of(first).stop:
                            to = raw_of(u if first == LATE else 0, slice(at, at + n))
                            sp.dma_start(to, w[p][0, :, bass.ds(m * P, P)].rearrange("(c p) n -> p c n", p=P)
                                         ).then_inc(late_loaded[u - LATE] if first == LATE else raw_loaded, 16)

                def load_gate(lane, br, m, half):
                    block_of = (0, 2, 1)[br]
                    sp.dma_start(gate[:, lane], d["gates"][bass.ds(NM * block_of + m, 1), :, half * HALF:(half + 1) * HALF
                                                           ].rearrange("o p t -> p (o t)")).then_inc(gate_loaded[lane], 16)

                def total_of(m, half):
                    return d["merged"][bass.ds(m, 1), :, half * HALF:(half + 1) * HALF].rearrange("o p t -> p (o t)")

                def load_att(pair):
                    sp.wait_ge(turned, pair + 1)
                    for g in range(3):
                        sp.dma_start(att[:, :, g].rearrange("p t a q -> p t (a q)"),
                                     d["att"][g, pair * 2 * P:(pair + 1) * 2 * P].rearrange("(t p) a q -> p t (a q)", p=P)
                                     ).then_inc(att_loaded, 16)

                def load_late(u):
                    k = u % 2
                    sp.wait_ge(summed, max(u, LATE + 1))
                    load_gate(k, 2, u - LATE, 0)
                    sp.wait_ge(stored[k], 16 * (u // 2) + 16)
                    sp.dma_start(total[:, k], total_of(u - LATE, 0)).then_inc(partial_loaded[k], 16)

                load_att(0)
                for u in range(SECOND):
                    k = u % 2
                    merging = u < LATE or u >= FULL
                    pair = u if u < LATE else u - LATE
                    m = u if u < LATE else u - LATE
                    if u == 0:
                        load_weights(0, 1)
                    if u == LATE:
                        load_late(u)
                    if LATE <= u < FULL - 1:
                        load_late(u + 1)
                    for lane, br in lanes(u, k) if merging else ():
                        sp.wait_ge(summed, u + 1 if u < LATE else max(9, 2 * u - (7 if lane == 2 else 8)))
                        load_gate(lane, br, m, 0)
                    if merging:
                        if u < LATE:
                            sp.wait_ge(ya_made, pair + 1)
                        else:
                            sp.wait_ge(ya_made, LATE + 1)
                            sp.wait_ge(y_stored, 16 * (u - FULL) + 16)
                        sp.dma_start(g_t[:], d["g"][:, :, pair * 2 * P:(pair + 1) * 2 * P].rearrange("b p t -> p b t")
                                     ).then_inc(g_loaded, 16)
                    ahead = {LATE - 2: range(LATE, FULL), LATE - 1: (), LATE: (), LATE + 1: (FULL,), LATE + 2: ()}
                    for v in ahead.get(u, (u + 2,)):
                        load_weights(next(x for x in (SECOND, FULL, LATE, 0) if v >= x), v)
                    if u >= FULL:
                        sp.wait_ge(gated, pair + 2)
                        sp.dma_start(d["y_attn"][:, :, pair * 2 * P:(pair + 1) * 2 * P].rearrange("b p t -> p b t"), g_t[:]
                                     ).then_inc(y_stored, 16)
                    if u < LATE:
                        load_att(u + 1)
                    elif FULL <= u < SECOND - 1:
                        load_att(pair + 1)
                    sp.wait_ge(summed, u + 2 if u < FULL else 2 * u - 5)
                    sp.dma_start(total_of(m, 0), total[:, k]).then_inc(stored[k], 16)

                def second_half(i, last):
                    for k in range(2):
                        u = SECOND + 2 * i + k
                        for lane, br in lanes(SECOND, k):
                            sp.wait_ge(summed, 2 * u - (7 if lane == 2 else 8))
                            load_gate(lane, br, 2 * i + k, 1)
                        if not last:
                            load_weights(SECOND, u + 2)
                        sp.wait_ge(summed, 2 * u - 5)
                        sp.dma_start(total_of(2 * i + k, 1), total[:, k]).then_inc(stored[k], 16)

                with sp.Fori(0, NM // 2 - 1) as i:
                    second_half(i, False)
                second_half(NM // 2 - 1, True)
                for k in range(2):
                    sp.wait_ge(stored[k], 16 * (UNITS // 2) + 16)

            @block.gpsimd
            def _(pool):
                pool.sem_inc(ya_made, 1)
                tt = pool.tensor_tensor

                def split(u, k, at):
                    pool.wait_ge(w_hi_made, u + 1)
                    tt(w_lo[:, k, at], raw_of(u if at.start else 0, at), w_hi[:, k, at].bitcast(F32), ALU.subtract
                       ).then_inc(w_made, 1)

                def weigh(pair):
                    window = lambda g: att[:, 0, g, :, :PAIR]
                    pool.wait_ge(ex_scaled, pair + 1)
                    tt(halves(0, 2), halves(0, 2), share(0, 2), ALU.mult).then_inc(part2_made, 1)
                    pool.wait_ge(part_made, 2 * pair + 1)
                    tt(window(0), window(0), window(1), ALU.add).then_inc(o_half, 1)
                    pool.wait_ge(o_half, pair + 1)
                    pool.wait_ge(part2_made, pair + 1)
                    tt(window(0), window(0), window(2), ALU.add).then_inc(o_made, 1)

                split(0, 0, chunks_of(0))
                for u in range(SECOND):
                    split(u + 1, (u + 1) % 2, chunks_of(u + 1))
                    if u < LATE or u >= FULL:
                        weigh(u if u < LATE else u - LATE)
                    if u < LATE:
                        at = slice(u * 2 * P, (u + 1) * 2 * P)
                        pool.wait_ge(ya_hi_made, u + 1)
                        tt(y_lo_of_rest[:, 4:, at], g_t[:], y_hi[:, 12:, at].bitcast(F32), ALU.subtract
                           ).then_inc(ya_made, 1)
                split(SECOND + 1, 1, chunks_of(SECOND))
                with pool.Fori(SECOND // 2 + 1, UNITS // 2) as i:
                    for k in range(2):
                        split(2 * i + k, k, chunks_of(SECOND))

            @block.scalar
            def _(act):
                for k in range(2):
                    act.sem_inc(stored[k], 16)
                act.sem_inc(y_stored, 16)
                copy = lambda to, of: act.activation(to, of, ACT.Copy)

                def load_y(br, half):
                    y, _, first, n = BRANCHES[br]
                    for c in range(n):
                        act.dma_start(y_raw[first + c], d[y][c, :, half * HALF:(half + 1) * HALF]
                                      ).then_inc(y_loaded[(first + c) // 4], 16)

                def hi_of_y(br, half, part=None):
                    _, _, first, n = BRANCHES[br]
                    for c in range(first, first + n) if part is None else range(4 * part, 4 * part + 4):
                        if br or half:
                            act.wait_ge(y_loaded[c // 4], 64 * (half + 1) if br == 1 else 64)
                        copy(y_hi[:, c], y_raw[c]).then_inc(y_hi_made, 1)

                def split(u, k, at, raw_at):
                    if isinstance(u, int) and LATE <= u < FULL:
                        act.wait_ge(late_loaded[u - LATE], 16)
                    elif raw_at is not None:
                        act.wait_ge(raw_loaded, raw_at)
                    v = u - 2
                    if not isinstance(u, int) or v >= FULL:
                        act.wait_ge(acc_made[2], v - FULL + 1)
                    elif v >= LATE:
                        act.wait_ge(acc_made[v % 2], v // 2 + 3)
                    elif v >= 0:
                        act.wait_ge(acc_made[1], v + 1)
                    copy(w_hi[:, k, at], raw_of(u if at.start else 0, at)).then_inc(w_hi_made, 1)

                def weights_of_windows(pair):
                    act.wait_ge(low_made, pair + 1)
                    act.activation(ex[:], low[:], ACT.Exp, scale=HDIM ** -0.5).then_inc(ex_made, 1)

                def gates(u, use):
                    for lane, _ in use:
                        n = use_of(lane, u)
                        act.wait_ge(gate_loaded[lane], 16 * n + 16)
                        act.activation(gate[:, lane], gate[:, lane], ACT.Sigmoid).then_inc(gate_made[lane], 1)

                load_y(1, 0)
                split(0, 0, chunks_of(0), None)
                for part in range(2):
                    hi_of_y(0, 0, part)
                    if part == 0:
                        weights_of_windows(0)
                hi_of_y(1, 0)
                for u in range(SECOND):
                    split(u + 1, (u + 1) % 2, chunks_of(u + 1), raw_count(u + 1))
                    if 0 < u < LATE or u >= FULL:
                        weights_of_windows(u if u < LATE else u - LATE)
                    gates(u, lanes(u, u % 2))
                act.wait_ge(acc_made[0], SECOND - 2)
                load_y(0, 1)
                act.wait_ge(acc_made[1], SECOND - 2)
                load_y(1, 1)
                hi_of_y(0, 1)
                act.wait_ge(acc_made[2], SECOND - FULL)
                act.wait_ge(y_stored, 16 * 4 + 16)
                load_y(2, 1)
                hi_of_y(1, 1)
                hi_of_y(2, 1)
                with act.Fori(0, NM // 2 - 1) as i:
                    for k in range(2):
                        u = SECOND + 2 * i + k
                        split(u + 1, 1 - k, chunks_of(SECOND), 48 * u - 192)
                        gates(u, lanes(SECOND, k))
                split(UNITS - 1, 1, chunks_of(SECOND), raw_count(UNITS - 1))
                for u in range(UNITS - 2, UNITS):
                    gates(u, lanes(SECOND, 0))

            @block.tensor
            def _(pe):
                pe.sem_inc(turned, 1)

                def products(u, k, first):
                    pe.wait_ge(w_made, u + 1)
                    for lane, br in lanes(first, k):
                        _, _, at, n = BRANCHES[br]
                        pe.wait_ge(acc_taken[lane], use_of(lane, u, first) + 1)
                        steps = [(c, t) for c in range(at, at + n) for t in range(2)]
                        for c, t in sorted(steps, key=lambda x: x[1]) if first == LATE else steps:
                            if first == LATE and c == at:
                                pe.wait_ge(ya_made, 2 * t + 3)
                            if first in (0, SECOND) and t == 0:
                                pe.wait_ge(y1_made if first else y0_made, c + 1)
                            span = slice(t * BANK, (t + 1) * BANK)
                            to = acc[:, lane, span]
                            pe.matmul(to, w_hi[:, k, c], y_hi[:, c, span], start=c == at, stop=False)
                            pe.matmul(to, w_hi[:, k, c], y_lo[c][:, span], start=False, stop=False)
                            last = pe.matmul(to, w_lo[:, k, c], y_hi[:, c, span], start=False, stop=c == at + n - 1)
                        last.then_inc(acc_made[lane], 1)
                        if first in (0, FULL) and lane == 1:
                            pair = u if first == 0 else u - LATE
                            pe.wait_ge(o_made, pair + 1)
                            pe.wait_ge(o1_made, pair + 1)
                            pe.wait_ge(gated, pair + 1)
                            for q in range(KV // P):
                                for x in range(2):
                                    last = pe.transpose(ps[:, q, x * P:(x + 1) * P], att[:, x, 0, q, :PAIR], ident[:])
                            last.then_inc(turned, 1)

                for first, end in ((0, LATE), (LATE, FULL), (FULL, SECOND), (SECOND, UNITS)):
                    with pe.Fori(0, (end - first) // 2) as i:
                        for k in range(2):
                            products(first + 2 * i + k, k, first)

            @block.vector
            def _(dve):
                dve.sem_inc(gated, 1)
                dve.sem_inc(summed, 1)
                for lane in range(3):
                    dve.sem_inc(acc_taken[lane], 1)
                tt = dve.tensor_tensor

                def weigh(pair):
                    of = lambda g, at: att[:, :, g, :, PAIR + at:PAIR + at + 2]
                    slots = lambda ap: ap.rearrange("p t (a s) -> p t a s", s=2)
                    windows = lambda ap: ap.rearrange("p g (a s) -> p g a s", s=2)
                    dve.wait_ge(att_loaded, 48 * (pair + 1))
                    tt(slots(top[:]), of(0, 0), of(1, 0), ALU.max).then_inc(step, 1)
                    dve.wait_ge(step, 5 * pair + 1)
                    tt(slots(top[:]), slots(top[:]), of(2, 0), ALU.max).then_inc(step, 1)
                    dve.wait_ge(step, 5 * pair + 2)
                    for t in range(2):
                        last = tt(windows(low[:, t]), att[:, t, :, :, PAIR:PAIR + 2], windows(
                            top[:, t].unsqueeze(1).to_broadcast([P, 3, SLOTS])), ALU.subtract)
                    last.then_inc(low_made, 1)
                    dve.wait_ge(ex_made, pair + 1)
                    for t in range(2):
                        last = tt(windows(low[:, t]), windows(ex[:, t]), att[:, t, :, :, PAIR + 2:], ALU.mult)
                    last.then_inc(step, 1)
                    dve.wait_ge(step, 5 * pair + 3)
                    dve.tensor_reduce(den[:], low[:].rearrange("p t g s -> p t s g"), mybir.AxisListType.X, ALU.add
                                      ).then_inc(step, 1)
                    dve.wait_ge(step, 5 * pair + 4)
                    dve.reciprocal(den[:], den[:]).then_inc(step, 1)
                    dve.wait_ge(step, 5 * pair + 5)
                    tt(ex[:], ex[:], den[:].unsqueeze(2).to_broadcast([P, 2, 3, SLOTS]), ALU.mult).then_inc(ex_scaled, 1)
                    dve.wait_ge(ex_scaled, pair + 1)
                    for t in range(2):
                        for g in range(2 + t):
                            last = tt(halves(t, g), halves(t, g), share(t, g), ALU.mult)
                        last.then_inc(part_made, 1)
                    window = lambda g: att[:, 1, g, :, :PAIR]
                    dve.wait_ge(part_made, 2 * pair + 2)
                    tt(window(0), window(0), window(1), ALU.add).then_inc(o1_half, 1)
                    dve.wait_ge(o1_half, pair + 1)
                    tt(window(0), window(0), window(2), ALU.add).then_inc(o1_made, 1)

                def gate_attention(pair):
                    dve.wait_ge(turned, pair + 2)
                    dve.wait_ge(g_loaded, 16 * (pair + 1))
                    tt(g_t[:], ps[:], g_t[:], ALU.mult).then_inc(gated, 1)
                    if pair < 4:
                        dve.wait_ge(gated, pair + 2)
                        dve.tensor_copy(y_hi[:, 12:, pair * 2 * P:(pair + 1) * 2 * P], g_t[:]).then_inc(ya_hi_made, 1)

                def gate_lane(lane, n):
                    dve.wait_ge(acc_made[lane], n + 1)
                    dve.wait_ge(gate_made[lane], n + 1)
                    tt(gate[:, lane], acc[:, lane], gate[:, lane], ALU.mult).then_inc(acc_taken[lane], 1)

                def add_first(n, k, use):
                    dve.wait_ge(stored[k], 16 * use + 16)
                    dve.wait_ge(acc_taken[0], n + 2)
                    dve.wait_ge(acc_taken[1], n + 2)
                    tt(total[:, k], gate[:, 0], gate[:, 1], ALU.add).then_inc(summed, 1)

                def add_attention(k, lane, n):
                    dve.wait_ge(acc_taken[lane], n + 2)
                    tt(total[:, k], total[:, k], gate[:, lane], ALU.add).then_inc(summed, 1)

                def lo_of_y(chunks, base, made):
                    for c in chunks:
                        dve.wait_ge(y_hi_made, base + c + 1)
                        tt(y_lo[c], y_raw[c], y_hi[:, c].bitcast(F32), ALU.subtract).then_inc(made, 1)

                for u in range(SECOND):
                    k = u % 2
                    merging, pair = u < LATE or u >= FULL, u if u < LATE else u - LATE
                    if u == 0:
                        lo_of_y(range(4), 0, y0_made)
                    if merging:
                        weigh(pair)
                    if u == 0:
                        lo_of_y(range(4, 12), 0, y0_made)
                    if not merging:
                        n = use_of(k, u)
                        gate_lane(k, n)
                        dve.wait_ge(partial_loaded[k], 16 * ((u - LATE) // 2 + 1))
                        add_attention(k, k, n)
                        continue
                    gate_lane(0, use_of(0, u))
                    gate_attention(pair)
                    gate_lane(1, use_of(1, u))
                    add_first(use_of(1, u), k, u // 2)
                    if u == SECOND - 1:
                        lo_of_y(range(2), 12, y1_made)
                    if u >= FULL:
                        gate_lane(2, use_of(2, u))
                        dve.wait_ge(summed, 2 * u - 6)
                        add_attention(k, 2, use_of(2, u))
                lo_of_y(range(2, 16), 12, y1_made)
                with dve.Fori(0, NM // 2) as i:
                    for k in range(2):
                        u = SECOND + 2 * i + k
                        for lane in range(2):
                            gate_lane(lane, use_of(lane, u))
                        add_first(use_of(1, u), k, SECOND // 2 + i)
                        gate_lane(2, use_of(2, u))
                        dve.wait_ge(summed, 2 * u - 6)
                        add_attention(k, 2, use_of(2, u))


def use_of(lane, u, first=None):
    first = first if first is not None else u if isinstance(u, int) else 12
    return u if first < 4 else 4 + (u - 4) // 2 if first < 8 else u - 8 if lane == 2 else u - 2


def output_stage(nc, w, d, out, eps):
    with ExitStack() as stack:
        s = Scope(nc, stack)
        w_hi, w_lo = s.sb("o_whi", [P, KC, DM], F32R), s.sb("o_wlo", [P, KC, DM], F32R)
        w_raw = s.sb("o_wraw", [P, KC, DM])
        m_raw = s.sb("o_mraw", [P, 2, KC, P])
        m_hi, m_lo = s.sb("o_mhi", [P, 2, KC, P], F32R), s.sb("o_mlo", [P, 2, KC, P], F32R)
        x_sb = s.sb("o_x", [P, 2, DM])
        w_post = s.sb("o_wpost", [P, DM])
        sq = s.sb("o_sq", [P, 2, DM])
        ss, std, rstd = (s.sb(n, [P, 2]) for n in ("o_ss", "o_std", "o_rstd"))
        y = s.sb("o_y", [P, 2, DM])
        acc = s.ps("o_acc", [P, 2, DM])
        w_loaded, post_loaded = s.sems("o_w_loaded", KC), s.sem("o_post_loaded")
        m_loaded, x_loaded = s.sems("o_m_loaded", 2), s.sems("o_x_loaded", 2)
        w_hi_made, w_made = s.sem("o_whi_r"), s.sem("o_w_made")
        m_hi_made, squared, std_made, rstd_made = (s.sem("o_" + n) for n in ("mhi_r", "sq_r", "std_r", "rstd_r"))
        m_made = s.sem("o_m_made")
        acc_made = s.sem("o_acc_made")
        acc_taken = s.sem("o_acc_taken")
        y_made = s.sem("o_y_made")
        y_free = s.sem("o_y_free")
        stored = s.sems("o_stored", 2)
        with nc.Block() as block:

            @block.sync
            def _(sp):
                def load_m(c, k):
                    sp.wait_ge(m_made, c + 1)
                    sp.dma_start(m_raw[:, k], d["merged"][:, :, bass.ds(c * P, P)].rearrange("b p t -> p b t")
                                 ).then_inc(m_loaded[k], 16)

                def load_x(c, k):
                    sp.wait_ge(y_made, c + 1)
                    sp.dma_start(x_sb[:, k], w["x"][0, bass.ds(c * P, P), :]).then_inc(x_loaded[k], 16)

                load_m(0, 0)
                for c in range(KC):
                    sp.dma_start(w_raw[:, c], w["w_out"][0, c * P:(c + 1) * P, :]).then_inc(w_loaded[c], 16)
                sp.dma_start(w_post[:], w["norm_post"][0:1, :].to_broadcast([P, DM])).then_inc(post_loaded, 16)
                with sp.Fori(0, TILES // 2 - 1) as i:
                    for k in range(2):
                        load_m(2 * i + k + 1, 1 - k)
                        load_x(2 * i + k, k)
                load_m(TILES - 1, 1)
                load_x(TILES - 2, 0)
                load_x(TILES - 1, 1)

            @block.scalar
            def _(act):
                def hi(c, k, use):
                    act.wait_ge(m_loaded[k], 16 * use + 16)
                    act.wait_ge(acc_made, c + 1)
                    act.activation(m_hi[:, k], m_raw[:, k], ACT.Copy).then_inc(m_hi_made, 1)

                def finish(c, k):
                    act.wait_ge(acc_made, c + 3)
                    act.activation(sq[:, k], acc[:, k], ACT.Square, accum_out=ss[:, k:k + 1]).then_inc(squared, 1)
                    act.wait_ge(squared, c + 1)
                    act.activation(std[:, k:k + 1], ss[:, k:k + 1], ACT.Sqrt, bias=eps[:], scale=1.0 / DM
                                   ).then_inc(std_made, 1)

                hi(0, 0, 0)
                for c in range(KC):
                    act.wait_ge(w_loaded[c], 16)
                    act.activation(w_hi[:, c], w_raw[:, c], ACT.Copy).then_inc(w_hi_made, 1)
                with act.Fori(0, TILES // 2 - 1) as i:
                    for k in range(2):
                        hi(2 * i + k + 1, 1 - k, i + k)
                        finish(2 * i + k, k)
                hi(TILES - 1, 1, TILES // 2 - 1)
                finish(TILES - 2, 0)
                finish(TILES - 1, 1)

            @block.gpsimd
            def _(pool):
                pool.sem_inc(y_free, 2)
                with pool.Fori(0, TILES // 2) as i:
                    for k in range(2):
                        c = 2 * i + k
                        pool.wait_ge(y_made, c + 3)
                        pool.dma_start(out[0, bass.ds(c * P, P), :], y[:, k]).then_inc(stored[k], 16)
                        pool.wait_ge(stored[k], 16 * i + 16)
                        pool.sem_inc(y_free, 1)

            @block.tensor
            def _(pe):
                pe.sem_inc(acc_made, 2)

                def product(c, k):
                    pe.wait_ge(m_made, c + 3)
                    pe.wait_ge(acc_taken, c + 1)
                    for b in range(KC):
                        pe.wait_ge(w_made, b + 1)
                        for t in range(2):
                            span = slice(t * BANK, (t + 1) * BANK)
                            to = acc[:, k, span]
                            pe.matmul(to, m_hi[:, k, b], w_hi[:, b, span], start=b == 0, stop=False)
                            pe.matmul(to, m_hi[:, k, b], w_lo[:, b, span], start=False, stop=False)
                            last = pe.matmul(to, m_lo[:, k, b], w_hi[:, b, span], start=False, stop=b == KC - 1)
                    last.then_inc(acc_made, 1)

                with pe.Fori(0, TILES // 2) as i:
                    for k in range(2):
                        product(2 * i + k, k)

            @block.vector
            def _(dve):
                dve.sem_inc(m_made, 2)
                dve.sem_inc(acc_taken, 2)
                dve.sem_inc(y_made, 2)

                def lo(c, k):
                    dve.wait_ge(m_hi_made, c + 1)
                    dve.tensor_tensor(m_lo[:, k], m_raw[:, k], m_hi[:, k].bitcast(F32), ALU.subtract).then_inc(m_made, 1)

                def finish(c, k, use):
                    dve.wait_ge(std_made, c + 1)
                    dve.reciprocal(rstd[:, k:k + 1], std[:, k:k + 1]).then_inc(rstd_made, 1)
                    dve.wait_ge(rstd_made, c + 1)
                    dve.wait_ge(y_free, c + 1)
                    dve.scalar_tensor_tensor(y[:, k], acc[:, k], rstd[:, k:k + 1], w_post[:], ALU.mult, ALU.mult
                                             ).then_inc(acc_taken, 1)
                    dve.wait_ge(acc_taken, c + 3)
                    dve.wait_ge(x_loaded[k], 16 * use + 16)
                    dve.tensor_tensor(y[:, k], y[:, k], x_sb[:, k], ALU.add).then_inc(y_made, 1)

                lo(0, 0)
                for c in range(KC):
                    dve.wait_ge(w_hi_made, c + 1)
                    dve.tensor_tensor(w_lo[:, c], w_raw[:, c], w_hi[:, c].bitcast(F32), ALU.subtract).then_inc(w_made, 1)
                dve.wait_ge(post_loaded, 16)
                with dve.Fori(0, TILES // 2 - 1) as i:
                    for k in range(2):
                        lo(2 * i + k + 1, 1 - k)
                        finish(2 * i + k, k, i)
                lo(TILES - 1, 1)
                finish(TILES - 2, 0, TILES // 2 - 1)
                finish(TILES - 1, 1, TILES // 2 - 1)


def build(nc, w, out):
    def scratch(name, shape):
        return nc.dram_tensor(name, shape, F32, kind="Internal").ap()

    d = {"dt": scratch("s_dt", [P, SEQ]), "z": scratch("s_z", [SSM // P, P, SEQ]),
         "xbc": scratch("s_xbc", [16, P, SEQ]), "qs": scratch("s_qs", [12, 2, P, SEQ]),
         "kv": scratch("s_kv", [8, P, SEQ]),
         "g": scratch("s_g", [4, P, SEQ]), "y_sc": scratch("s_ysc", [4, P, SEQ]),
         "gates": scratch("s_gates", [24, P, SEQ]), "y_ssm": scratch("s_yssm", [8, P, SEQ]),
         "att": scratch("s_att", [3, SEQ, SLOTS // 2, PAIR + 4]),
         "y_attn": scratch("s_yattn", [4, P, SEQ]), "merged": scratch("s_merged", [8, P, SEQ])}
    with ExitStack() as stack:
        s = Scope(nc, stack)
        ident = s.sb("ident", [P, P])
        eps = s.sb("eps", [P, 1])
        with ExitStack() as inner:
            k = Scope(nc, inner)
            h1 = k.sb("h1", [P, TILES // 2, 2, KC, P], F32R)
            wt = {"raw": k.sb("raw", [P, 2, KC, P]), "w_hi": k.sb("w_hi", [P, 3, KC, P], F32R),
                  "w_lo": k.sb("w_lo", [P, 3, KC, P], F32R), "work": k.sb("work", [P, 2, SEQ])}
            v = {n: k.sb("v_" + n, [P, TILES * HEADS]) for n in ("dt", "a", "cs", "ecs", "elast", "wdec")}
            v.update({"tri": k.sb("v_tri", [P, P]),
                      "ones": k.sb("v_ones", [P, P]), "dskip": k.sb("v_dskip", [P, HEADS])})
            with nc.sbuf_tensor("h0", [P, TILES // 2, 2, KC, P], F32R) as h0:
                projection_stage(nc, w, d, (h0, h1), wt, v, ident, eps)
            ssd_gates_stage(nc, w, d, h1, wt, v, ident, eps)
        with ExitStack() as inner:
            k = Scope(nc, inner)
            raw = k.sb("b_raw", [P, 16, P])
            y_lo = k.sb("b_ylo_ssd", [P, 8, HALF], F32R)
            y_lo = [y_lo[:, c] for c in range(8)]
            attention_stage(nc, w, d, ident, raw, y_lo)
            merge_branches_stage(nc, w, d, ident, raw, y_lo)
        output_stage(nc, w, d, out, eps)


INS = ("x", "norm_pre", "norm_post", "w_in", "ssm_conv_w", "ssm_conv_b", "dt_bias", "a_log", "d_skip", "ssm_norm",
       "sc_conv_w", "p_ssm", "p_attn", "p_sc", "w_out")


def kernel(**inputs):
    import numpy as np
    import concourse.bacc as bacc
    from concourse.bass_utils import run_bass_kernel_spmd

    nc = bacc.Bacc("TRN2", target_bir_lowering=False, num_devices=1)
    arrays = {name: np.ascontiguousarray(inputs[name]) for name in INS}
    w = {name: nc.dram_tensor(name, a.shape, F32, kind="ExternalInput").ap() for name, a in arrays.items()}
    out = nc.dram_tensor("out", (1, SEQ, DM), F32, kind="ExternalOutput").ap()
    build(nc, w, out)
    return run_bass_kernel_spmd(nc, [arrays], core_ids=[0]).results[0]["out"]
```
